# Optimizing a Trainium2 kernel written in Bass

```python
import math
import jax, jax.numpy as jnp
from jax import lax
import numpy as np

D_MODEL = 1024
BATCH = 1
SEQ = 256
DEPTH = 2

D_FF = 2816
NORM_EPS = 1e-6
N_BRANCH = 4

GDN_HEADS = 4
GDN_DK = 64
GDN_DV = 64
GDN_CONV = 4
GDN_CHUNK = 64

S5_GROUPS = 16
S5_GROUP_WIDTH = 16
S5_STATE = 64
S5_WIDTH = S5_GROUPS * S5_GROUP_WIDTH

LRU_WIDTH = 256
LRU_BLOCKS = 4
LRU_BLOCK_WIDTH = LRU_WIDTH // LRU_BLOCKS
LRU_CONV = 4
LRU_C = 8.0

RET_HEADS = 4
RET_DK = 64
RET_DV = 64
RET_CHUNK = 128
ROPE_BASE = 10000.0

BRANCH_WIDTH = 256

IN_SPLITS = (
    GDN_HEADS * (2 * GDN_DK + GDN_DV),
    GDN_HEADS * GDN_DV,
    GDN_HEADS,
    GDN_HEADS,
    S5_WIDTH,
    LRU_WIDTH,
    LRU_WIDTH,
    RET_HEADS * RET_DK,
    RET_HEADS * RET_DK,
    RET_HEADS * RET_DV,
    RET_HEADS * RET_DV,
    N_BRANCH * D_MODEL,
)
N_IN = sum(IN_SPLITS)

kernel_name = "hybrid_gdn_s5_rglru_retnet_macaron"

F32 = jnp.float32

def rms_norm(x, w, eps=NORM_EPS):
    x32 = x.astype(F32)
    y = x32 * lax.rsqrt(jnp.mean(x32 * x32, axis=-1, keepdims=True) + eps)
    return (y * w.astype(F32)).astype(x.dtype)

def swiglu(x, w_gate, w_up, w_down):
    return (jax.nn.silu(x @ w_gate) * (x @ w_up)) @ w_down

def causal_dwconv(x, w):
    k = w.shape[0]
    return lax.conv_general_dilated(
        x, w[:, None, :].astype(x.dtype), window_strides=(1,), padding=[(k - 1, 0)],
        dimension_numbers=("NWC", "WIO", "NWC"), feature_group_count=x.shape[-1])

def l2norm(x, eps=1e-6):
    return x * lax.rsqrt(jnp.sum(x * x, axis=-1, keepdims=True) + eps)

def to_chunks(t, c):
    b, s, h, d = t.shape
    return t.reshape(b, s // c, c, h, d).transpose(0, 3, 1, 2, 4)

def from_chunks(t):
    b, h, n, c, d = t.shape
    return t.transpose(0, 2, 3, 1, 4).reshape(b, n * c, h, d)

def apply_rope(x, positions):
    half = x.shape[-1] // 2
    freqs = jnp.power(ROPE_BASE, -jnp.arange(half, dtype=F32) / half)
    ang = positions.astype(F32)[..., None] * freqs
    cos = jnp.cos(ang)[:, :, None, :]
    sin = jnp.sin(ang)[:, :, None, :]
    x1, x2 = x[..., :half], x[..., half:]
    return jnp.concatenate([x1 * cos - x2 * sin, x1 * sin + x2 * cos], axis=-1)

def gated_deltanet(qkv, z, beta_logit, a_logit, conv_w, a_log, dt_bias, norm_w):
    b, s, _ = qkv.shape
    dtype = qkv.dtype
    h, dk, dv, c = GDN_HEADS, GDN_DK, GDN_DV, GDN_CHUNK
    qkv = jax.nn.silu(causal_dwconv(qkv, conv_w)).astype(F32)
    q, k, v = jnp.split(qkv, [h * dk, 2 * h * dk], axis=-1)
    q = l2norm(q.reshape(b, s, h, dk)) * (dk ** -0.5)
    k = l2norm(k.reshape(b, s, h, dk))
    v = v.reshape(b, s, h, dv)
    beta = jax.nn.sigmoid(beta_logit.astype(F32))
    g = -jnp.exp(a_log.astype(F32)) * jax.nn.softplus(a_logit.astype(F32) + dt_bias.astype(F32))
    q, k, v = to_chunks(q, c), to_chunks(k, c), to_chunks(v, c)
    beta = to_chunks(beta[..., None], c)[..., 0]
    gc = jnp.cumsum(to_chunks(g[..., None], c)[..., 0], axis=-1)
    incl = jnp.tril(jnp.ones((c, c), dtype=bool))
    strict = jnp.tril(jnp.ones((c, c), dtype=bool), -1)
    diff = gc[..., :, None] - gc[..., None, :]
    decay = jnp.where(incl, jnp.exp(jnp.where(incl, diff, 0.0)), 0.0)
    kk = jnp.einsum("bhncd,bhnmd->bhncm", k, k)
    lower = jnp.where(strict, beta[..., None] * kk * decay, 0.0)
    rhs = jnp.concatenate([v * beta[..., None], k * (beta * jnp.exp(gc))[..., None]], axis=-1)
    sol = lax.linalg.triangular_solve(lower, rhs, left_side=True, lower=True, unit_diagonal=True)
    u, w = sol[..., :dv], sol[..., dv:]
    attn = jnp.einsum("bhncd,bhnmd->bhncm", q, k) * decay
    q_dec = q * jnp.exp(gc)[..., None]
    k_dec = k * jnp.exp(gc[..., -1:] - gc)[..., None]
    chunk_decay = jnp.exp(gc[..., -1])

    def step(state, xs):
        u_n, w_n, attn_n, q_n, k_n, dec_n = xs
        v_new = u_n - jnp.einsum("bhcd,bhde->bhce", w_n, state)
        o = jnp.einsum("bhcd,bhde->bhce", q_n, state) + jnp.einsum("bhcm,bhme->bhce", attn_n, v_new)
        state = state * dec_n[..., None, None] + jnp.einsum("bhcd,bhce->bhde", k_n, v_new)
        return state, o

    xs = tuple(jnp.moveaxis(t, 2, 0) for t in (u, w, attn, q_dec, k_dec, chunk_decay))
    _, o = lax.scan(step, jnp.zeros((b, h, dk, dv), F32), xs)
    o = from_chunks(jnp.moveaxis(o, 0, 2))
    o = rms_norm(o, norm_w) * jax.nn.silu(z.astype(F32).reshape(b, s, h, dv))
    return o.reshape(b, s, h * dv).astype(dtype)

def s5_layer(u, lam_re, lam_im, b_re, b_im, c_re, c_im, d, log_dt, w_glu, b_glu):
    bsz, s, _ = u.shape
    dtype = u.dtype
    gsz, gw, p = S5_GROUPS, S5_GROUP_WIDTH, S5_STATE
    u32 = u.astype(F32).reshape(bsz, s, gsz, gw)
    dt = jnp.exp(log_dt.astype(F32))[:, None]
    lr, li = lam_re.astype(F32), lam_im.astype(F32)
    mag = jnp.exp(lr * dt)
    abar_re, abar_im = mag * jnp.cos(li * dt), mag * jnp.sin(li * dt)
    den = lr * lr + li * li
    nr = abar_re - 1.0
    coef_re = (nr * lr + abar_im * li) / den
    coef_im = (abar_im * lr - nr * li) / den
    br, bi = b_re.astype(F32), b_im.astype(F32)
    bbar_re = coef_re[..., None] * br - coef_im[..., None] * bi
    bbar_im = coef_re[..., None] * bi + coef_im[..., None] * br
    bu_re = jnp.einsum("gpc,bsgc->bsgp", bbar_re, u32)
    bu_im = jnp.einsum("gpc,bsgc->bsgp", bbar_im, u32)
    a_re = jnp.broadcast_to(abar_re, (1, s, gsz, p))
    a_im = jnp.broadcast_to(abar_im, (1, s, gsz, p))

    def combine(e1, e2):
        a1r, a1i, b1r, b1i = e1
        a2r, a2i, b2r, b2i = e2
        return (a2r * a1r - a2i * a1i, a2r * a1i + a2i * a1r,
                a2r * b1r - a2i * b1i + b2r, a2r * b1i + a2i * b1r + b2i)

    _, _, x_re, x_im = lax.associative_scan(combine, (a_re, a_im, bu_re, bu_im), axis=1)
    y = (jnp.einsum("gcp,bsgp->bsgc", c_re.astype(F32), x_re)
         - jnp.einsum("gcp,bsgp->bsgc", c_im.astype(F32), x_im)
         + d.astype(F32) * u32)
    y = jax.nn.gelu(y.reshape(bsz, s, S5_WIDTH))
    y = y * jax.nn.sigmoid(y @ w_glu.astype(F32) + b_glu.astype(F32))
    return y.astype(dtype)

def rg_lru_block(xb, yb, conv_w, conv_b, w_a, b_a, w_i, b_i, lam):
    bsz, s, _ = xb.shape
    dtype = xb.dtype
    xc = (causal_dwconv(xb, conv_w) + conv_b).astype(F32)
    xblk = xc.reshape(bsz, s, LRU_BLOCKS, LRU_BLOCK_WIDTH)
    r = jax.nn.sigmoid(jnp.einsum("bsnc,ncd->bsnd", xblk, w_a.astype(F32)).reshape(bsz, s, LRU_WIDTH) + b_a.astype(F32))
    i = jax.nn.sigmoid(jnp.einsum("bsnc,ncd->bsnd", xblk, w_i.astype(F32)).reshape(bsz, s, LRU_WIDTH) + b_i.astype(F32))
    log_a = -LRU_C * r * jax.nn.softplus(-lam.astype(F32))
    a = jnp.exp(log_a)
    mult = jnp.sqrt(-jnp.expm1(2.0 * log_a))
    gated_x = xc * i * mult

    def step(h, inp):
        a_t, x_t = inp
        h = a_t * h + x_t
        return h, h

    _, hs = lax.scan(step, jnp.zeros((bsz, LRU_WIDTH), F32), (jnp.swapaxes(a, 0, 1), jnp.swapaxes(gated_x, 0, 1)))
    h = jnp.swapaxes(hs, 0, 1)
    return (h * jax.nn.gelu(yb.astype(F32))).astype(dtype)

def retention(q, k, v, g, positions, norm_w):
    bsz, s, _ = q.shape
    dtype = q.dtype
    h, dk, dv, c = RET_HEADS, RET_DK, RET_DV, RET_CHUNK
    q = apply_rope(q.astype(F32).reshape(bsz, s, h, dk), positions)
    k = apply_rope(k.astype(F32).reshape(bsz, s, h, dk), positions) * (dk ** -0.5)
    v = v.astype(F32).reshape(bsz, s, h, dv)
    log_gamma = jnp.log1p(-jnp.exp2(-5.0 - jnp.arange(h, dtype=F32)))
    idx = jnp.arange(c, dtype=F32)
    rel = idx[:, None] - idx[None, :]
    causal = rel >= 0
    intra = jnp.where(causal, jnp.exp(jnp.where(causal, rel, 0.0)[None] * log_gamma[:, None, None]), 0.0)
    qc, kc, vc = to_chunks(q, c), to_chunks(k, c), to_chunks(v, c)
    scores = jnp.einsum("bhncd,bhnmd->bhncm", qc, kc) * intra[None, :, None]
    o = jnp.einsum("bhncm,bhnme->bhnce", scores, vc)
    zeta = jnp.exp((c - 1.0 - idx)[None] * log_gamma[:, None])
    xi = jnp.exp((idx + 1.0)[None] * log_gamma[:, None])
    chunk_decay = jnp.exp(c * log_gamma)
    kv = jnp.einsum("bhncd,bhnce->bhnde", kc * zeta[None, :, None, :, None], vc)

    def step(state, kv_n):
        return state * chunk_decay[None, :, None, None] + kv_n, state

    _, prev = lax.scan(step, jnp.zeros((bsz, h, dk, dv), F32), jnp.moveaxis(kv, 2, 0))
    prev = jnp.moveaxis(prev, 0, 2)
    o = o + jnp.einsum("bhncd,bhnde->bhnce", qc, prev) * xi[None, :, None, :, None]
    o = from_chunks(o)
    mu = jnp.mean(o, axis=-1, keepdims=True)
    var = jnp.mean(jnp.square(o - mu), axis=-1, keepdims=True)
    on = ((o - mu) * lax.rsqrt(var + NORM_EPS)).reshape(bsz, s, h * dv) * norm_w.astype(F32)
    return (jax.nn.silu(g.astype(F32)) * on).astype(dtype)

def split_in(proj):
    offs, acc = [], 0
    for n in IN_SPLITS[:-1]:
        acc += n
        offs.append(acc)
    return jnp.split(proj, offs, axis=-1)

def hybrid_mixer(hn, positions, w_in, gdn_conv_w, gdn_a_log, gdn_dt_bias, gdn_norm_w,
                 s5_lambda_re, s5_lambda_im, s5_b_re, s5_b_im, s5_c_re, s5_c_im, s5_d, s5_log_dt,
                 s5_w_glu, s5_b_glu, lru_conv_w, lru_conv_b, lru_w_a, lru_b_a, lru_w_i, lru_b_i,
                 lru_lambda, ret_norm_w, w_branch, w_out):
    bsz, s, _ = hn.shape
    proj = hn @ w_in
    (gdn_qkv, gdn_z, gdn_b, gdn_a, s5_u, lru_x, lru_y,
     ret_q, ret_k, ret_v, ret_g, gate_logits) = split_in(proj)
    out_a = gated_deltanet(gdn_qkv, gdn_z, gdn_b, gdn_a, gdn_conv_w, gdn_a_log, gdn_dt_bias, gdn_norm_w)
    out_b = s5_layer(s5_u, s5_lambda_re, s5_lambda_im, s5_b_re, s5_b_im, s5_c_re, s5_c_im,
                     s5_d, s5_log_dt, s5_w_glu, s5_b_glu)
    out_c = rg_lru_block(lru_x, lru_y, lru_conv_w, lru_conv_b, lru_w_a, lru_b_a, lru_w_i, lru_b_i, lru_lambda)
    out_d = retention(ret_q, ret_k, ret_v, ret_g, positions, ret_norm_w)
    branches = jnp.stack([out_a, out_b, out_c, out_d], axis=2)
    gates = jax.nn.sigmoid(gate_logits.reshape(bsz, s, N_BRANCH, D_MODEL))
    merged = jnp.sum(gates * jnp.einsum("bsnc,ncd->bsnd", branches, w_branch), axis=2)
    return merged @ w_out

def setup_inputs(seed: int = 0) -> dict:
    key = jax.random.key(seed)
    ks = iter(jax.random.split(key, 48))
    L = DEPTH

    def nrm(shape, scale):
        return jax.random.normal(next(ks), shape, F32) * scale

    def unif(shape, lo, hi):
        return jax.random.uniform(next(ks), shape, F32, lo, hi)

    x = jax.random.normal(next(ks), (BATCH, SEQ, D_MODEL), F32)
    positions = jnp.broadcast_to(jnp.arange(SEQ, dtype=jnp.int32), (BATCH, SEQ))
    gdn_dt = jnp.exp(unif((L, GDN_HEADS), math.log(1e-3), math.log(1e-1)))
    lru_a0 = unif((L, LRU_WIDTH), 0.9, 0.999) ** (1.0 / LRU_C)
    return {
        "x": x,
        "positions": positions,
        "ffn1_norm": 1.0 + nrm((L, D_MODEL), 0.02),
        "ffn1_w_gate": nrm((L, D_MODEL, D_FF), D_MODEL ** -0.5),
        "ffn1_w_up": nrm((L, D_MODEL, D_FF), D_MODEL ** -0.5),
        "ffn1_w_down": nrm((L, D_FF, D_MODEL), D_FF ** -0.5),
        "mix_norm": 1.0 + nrm((L, D_MODEL), 0.02),
        "w_in": nrm((L, D_MODEL, N_IN), D_MODEL ** -0.5),
        "gdn_conv_w": nrm((L, GDN_CONV, GDN_HEADS * (2 * GDN_DK + GDN_DV)), GDN_CONV ** -0.5),
        "gdn_a_log": jnp.log(unif((L, GDN_HEADS), 1.0, 16.0)),
        "gdn_dt_bias": gdn_dt + jnp.log(-jnp.expm1(-gdn_dt)),
        "gdn_norm_w": 1.0 + nrm((L, GDN_DV), 0.02),
        "s5_lambda_re": -0.5 + nrm((L, S5_GROUPS, S5_STATE), 0.01),
        "s5_lambda_im": jnp.pi * jnp.arange(S5_STATE, dtype=F32) + nrm((L, S5_GROUPS, S5_STATE), 0.01),
        "s5_b_re": nrm((L, S5_GROUPS, S5_STATE, S5_GROUP_WIDTH), (2.0 * S5_GROUP_WIDTH) ** -0.5),
        "s5_b_im": nrm((L, S5_GROUPS, S5_STATE, S5_GROUP_WIDTH), (2.0 * S5_GROUP_WIDTH) ** -0.5),
        "s5_c_re": nrm((L, S5_GROUPS, S5_GROUP_WIDTH, S5_STATE), S5_STATE ** -0.5),
        "s5_c_im": nrm((L, S5_GROUPS, S5_GROUP_WIDTH, S5_STATE), S5_STATE ** -0.5),
        "s5_d": nrm((L, S5_GROUPS, S5_GROUP_WIDTH), 1.0),
        "s5_log_dt": unif((L, S5_GROUPS), math.log(1e-3), math.log(1e-1)),
        "s5_w_glu": nrm((L, S5_WIDTH, S5_WIDTH), S5_WIDTH ** -0.5),
        "s5_b_glu": nrm((L, S5_WIDTH), 0.01),
        "lru_conv_w": nrm((L, LRU_CONV, LRU_WIDTH), LRU_CONV ** -0.5),
        "lru_conv_b": nrm((L, LRU_WIDTH), 0.01),
        "lru_w_a": nrm((L, LRU_BLOCKS, LRU_BLOCK_WIDTH, LRU_BLOCK_WIDTH), LRU_BLOCK_WIDTH ** -0.5),
        "lru_b_a": nrm((L, LRU_WIDTH), 0.01),
        "lru_w_i": nrm((L, LRU_BLOCKS, LRU_BLOCK_WIDTH, LRU_BLOCK_WIDTH), LRU_BLOCK_WIDTH ** -0.5),
        "lru_b_i": nrm((L, LRU_WIDTH), 0.01),
        "lru_lambda": jnp.log(lru_a0) - jnp.log1p(-lru_a0),
        "ret_norm_w": 1.0 + nrm((L, RET_HEADS * RET_DV), 0.02),
        "w_branch": nrm((L, N_BRANCH, BRANCH_WIDTH, D_MODEL), BRANCH_WIDTH ** -0.5),
        "w_out": nrm((L, D_MODEL, D_MODEL), D_MODEL ** -0.5),
        "ffn2_norm": 1.0 + nrm((L, D_MODEL), 0.02),
        "ffn2_w_gate": nrm((L, D_MODEL, D_FF), D_MODEL ** -0.5),
        "ffn2_w_up": nrm((L, D_MODEL, D_FF), D_MODEL ** -0.5),
        "ffn2_w_down": nrm((L, D_FF, D_MODEL), D_FF ** -0.5),
        "final_norm": 1.0 + nrm((D_MODEL,), 0.02),
    }

def reference(x, positions, ffn1_norm, ffn1_w_gate, ffn1_w_up, ffn1_w_down, mix_norm, w_in,
              gdn_conv_w, gdn_a_log, gdn_dt_bias, gdn_norm_w,
              s5_lambda_re, s5_lambda_im, s5_b_re, s5_b_im, s5_c_re, s5_c_im, s5_d, s5_log_dt,
              s5_w_glu, s5_b_glu, lru_conv_w, lru_conv_b, lru_w_a, lru_b_a, lru_w_i, lru_b_i,
              lru_lambda, ret_norm_w, w_branch, w_out,
              ffn2_norm, ffn2_w_gate, ffn2_w_up, ffn2_w_down, final_norm):
    for l in range(DEPTH):
        x = x + 0.5 * swiglu(rms_norm(x, ffn1_norm[l]), ffn1_w_gate[l], ffn1_w_up[l], ffn1_w_down[l])
        x = x + hybrid_mixer(
            rms_norm(x, mix_norm[l]), positions, w_in[l],
            gdn_conv_w[l], gdn_a_log[l], gdn_dt_bias[l], gdn_norm_w[l],
            s5_lambda_re[l], s5_lambda_im[l], s5_b_re[l], s5_b_im[l], s5_c_re[l], s5_c_im[l],
            s5_d[l], s5_log_dt[l], s5_w_glu[l], s5_b_glu[l],
            lru_conv_w[l], lru_conv_b[l], lru_w_a[l], lru_b_a[l], lru_w_i[l], lru_b_i[l], lru_lambda[l],
            ret_norm_w[l], w_branch[l], w_out[l])
        x = x + 0.5 * swiglu(rms_norm(x, ffn2_norm[l]), ffn2_w_gate[l], ffn2_w_up[l], ffn2_w_down[l])
    return rms_norm(x, final_norm)


_drawn_inputs = setup_inputs


def setup_inputs(seed=0):
    import zlib

    import numpy as np

    out = dict(_drawn_inputs(seed))
    spreads = {}
    factors = {'ffn1_norm': 3.827,
     'gdn_norm_w': 25.194,
     's5_lambda_re': 64.0,
     's5_lambda_im': 22.16,
     's5_b_re': 31.328,
     's5_b_im': 30.296,
     's5_c_re': 30.952,
     's5_c_im': 30.576,
     's5_log_dt': 21.76,
     's5_b_glu': 200.0,
     'lru_conv_b': 106.856,
     'lru_b_a': 200.0,
     'lru_b_i': 200.0,
     'ret_norm_w': 27.852,
     'ffn2_norm': 5.336,
     'final_norm': 25.307,
     's5_w_glu': 10.766,
     'lru_w_a': 23.96,
     'lru_lambda': 25.896,
     'lru_conv_w': 8.0,
     'lru_w_i': 8.0}
    for name, (base, spread) in spreads.items():
        noise = np.random.default_rng([zlib.crc32(name.encode()), seed]).standard_normal(out[name].shape)
        drawn = base * np.exp(spread * noise) if base else spread * noise
        out[name] = __import__('jax').numpy.asarray(drawn.astype(out[name].dtype))
    for name, factor in factors.items():
        out[name] = (out[name] * factor).astype(out[name].dtype)
    return out
```

```python
import math

import numpy as np
import concourse.bass as bass
from concourse import mybir
from contextlib import ExitStack

F32 = mybir.dt.float32
ALU = mybir.AluOpType
ACT = mybir.ActivationFunctionType

P = 128
SEQ, DM, DFF, DEPTH = 256, 1024, 2816, 2
KD = DM // P
MF = DFF // P
NB = 4
NH, DH = 4, 64
NCH = SEQ // 64
NST = 8
EPS = 1e-6
SLOTS = 4
SLOT = 2048
LEVELS = 6
GELU_C = math.sqrt(2.0 / math.pi)
TWO_PI = 2.0 * math.pi
ROUND = 12582912.0
GRID = 384.0
PI_C = [float(np.float32(x)) for x in (6.28125, 0.0019350051879882812, 3.0199159819567e-07)]
PI_SAFE = 3.1415925
SIN_SCALE = 6.283185

PCOLS = {}
_at = 0
for _name, _n in [("n1", 8), ("nm", 8), ("n2", 8), ("gconv", 24), ("dtb", 1), ("alog", 1), ("gnorm", 1),
                  ("lre", 8), ("lim", 8), ("ldt", 8), ("s5d", 2), ("bglu", 2), ("lconv", 8), ("lcb", 2),
                  ("lba", 2), ("lbi", 2), ("lam", 2), ("rnorm", 2), ("sbr", 1024), ("sbi", 1024),
                  ("scr", 256), ("sci", 256), ("wglu", 512), ("wa", 256), ("wi", 256)]:
    PCOLS[_name] = (_at, _at + _n)
    _at += _n
NPAR = _at

CCOLS = {}
_at = 0
for _name, _n in [("ident", 128), ("ones", 128), ("bo", 128), ("incl", 128), ("lev", 128 * LEVELS), ("perm", 128),
                  ("selg", 512), ("selb", 512), ("selp", 256), ("rmask", 4 * 384), ("tok", 256),
                  ("freq", 1), ("fnorm", 8)]:
    CCOLS[_name] = (_at, _at + _n)
    _at += _n
NCST = _at

PROJ = ["ba", "qkv0", "qkv1", "qkv2", "lx", "ly", "su", "z", "rq", "rk", "rg", "rv"]
CHUNKS = ([(f"gu1_{m}", 2048) for m in range(MF)] + [(f"dn1_{i}", 1408) for i in range(16)]
          + [(n, 1024 if n == "ba" else 2048) for n in PROJ] + [(f"g{i}", 2048) for i in range(16)]
          + [(f"wb{i}", 2048) for i in range(4)] + [(f"wo{i}", 2048) for i in range(4)]
          + [(f"gu2_{m}", 2048) for m in range(MF)] + [(f"dn2_{i}", 1408) for i in range(16)])
CHUNK_INDEX = {name: i for i, (name, _) in enumerate(CHUNKS)}
CHUNK_AT = {}
_at = 0
for _name, _n in CHUNKS:
    CHUNK_AT[_name] = _at
    _at += P * _n
LAYER_FLOATS = _at

MAIN = ([("ssq1", "act")] + [(f"gu1_{m}", "dve") for m in range(MF)] + [(f"dn1_{j}", "dve") for j in range(4)]
        + [("ssqm", "act")] + [(n, "act") for n in PROJ] + [(f"g{i}", "act") for i in range(16)]
        + [(f"mg{m}{ab}", "dve") for m in range(KD) for ab in "ab"] + [(f"wo{i}", "dve") for i in range(4)]
        + [("ssq2", "act")] + [(f"gu2_{m}", "dve") for m in range(MF)] + [(f"dn2_{j}", "dve") for j in range(4)])
SIDE = ([("lr", "act"), ("li", "act"), ("l2q", "act"), ("l2k", "act"), ("rowt", "act"), ("ktr", "dve"), ("vtr", "dve"),
         ("eb", "act")]
        + [(n, "dve") for n in ("gb0", "gb1", "kk0", "bb0", "kk1", "bb1", "qk0", "qk1")]
        + [u for lv in range(LEVELS) for u in
           ([(f"t0_{lv}", "act"), (f"t1_{lv}", "act")]
            + [(f"{n}_{lv}", "dve") for n in ("xt0", "ty0", "xt1", "ty1")]
            + [(f"pq{s}", "dve") for s in ([2 * lv, 2 * lv + 1] if lv < 4 else [])])]
        + [("rotq", "dve"), ("rotk", "dve"), ("u", "act"), ("w", "act"),
           ("su0", "dve"), ("sc0", "dve"), ("sc1", "dve"),
           ("ws1", "dve"), ("oi1", "act"), ("su1", "dve"), ("sc2", "dve"), ("sc3", "dve"),
           ("ws2", "dve"), ("oi2", "act"), ("su2", "dve"), ("ro", "act"),
           ("ws3", "dve"), ("oi3", "act"), ("rm", "dve"), ("oa0", "dve"), ("oa1", "dve"),
           ("rv2", "act"), ("gs", "act"), ("glu", "act")])


class Units:

    def __init__(self, order, banks):
        self.order, self.banks = order, banks
        self.index = {name: i for i, (name, _) in enumerate(order)}

    def bank(self, name):
        return self.banks[self.index[name] % len(self.banks)]

    def ready(self, name):
        return self.index[name] + 1

    def previous(self, name):
        i = self.index[name] - len(self.banks)
        return self.order[i] if i >= 0 else None

    def taken(self, name):
        i = self.index[name]
        return sum(1 for _, e in self.order[:i + 1] if e == self.order[i][1])


def trunk(nc, weights, params, consts, positions, x_in, y_out):
    ctx = ExitStack()
    with ctx:
        def sb(name, cols):
            return ctx.enter_context(nc.sbuf_tensor(name, [P, cols], F32))

        x = sb("x", KD * SEQ)[:].rearrange("p (k t) -> p k t", k=KD)
        xn = sb("xn", KD * SEQ)[:].rearrange("p (k t) -> p k t", k=KD)
        ring = sb("ring", SLOTS * SLOT)
        cst = sb("cst", NCST)
        par = sb("par", NPAR)
        wide = sb("wide", 32 * SEQ)[:].rearrange("p (k t) -> p k t", k=32)
        hidden = wide[:, 0:MF, :]
        gates = wide
        cosE = wide[:, 22:30, :]
        sinE = sb("sinE", 8 * SEQ)[:].rearrange("p (k t) -> p k t", k=8)

        def two(name, n=2, t=SEQ):
            return sb(name, n * t)[:].rearrange("p (k t) -> p k t", k=n)

        qkvp = two("qkvp", 6, SEQ + 3)
        qkv = two("qkv", 6)
        zz, su, ly = two("zz"), two("su"), two("ly")
        lxp = two("lxp", 2, SEQ + 3)
        rq, rk, rg, rv = two("rq"), two("rk"), two("rg"), two("rv")
        out_br = sb("out_br", NB * 2 * SEQ)[:].rearrange("p (n k t) -> p n k t", n=NB, k=2)
        big = sb("big", 24 * SEQ)

        def mats(i):
            return big[:, i * 8 * P:(i + 1) * 8 * P].rearrange("p (h t j c) -> p h t j c", h=2, t=2, j=2)

        dec, attn, low, my, mx, mt = (mats(i) for i in range(6))
        lowc = dec
        flat = lambda m: m.rearrange("p h t j c -> p h (t j c)")
        kbe, kdec, vb = (qkvp[:, 2 * i:2 * i + 2, 3:] for i in range(3))
        uu = big[:, 22 * SEQ:24 * SEQ].rearrange("p (k t) -> p k t", k=2)
        wT = big[:, 8 * SEQ:10 * SEQ].rearrange("p (k t) -> p k t", k=2)
        egb, qdec = two("egb"), two("qdec")
        state = two("state", 2, P)
        rows, rowT = two("rows", 1)[:, 0, :], two("rowT", 2, P)
        tmpA, tmpB, tmpC, tmpD, tmpE, tmpF, tmpG = (two("tmp" + c) for c in "ABCDEFG")
        small = sb("small", 256)
        ropec, ropes = two("ropec", 1)[:, 0, :], two("ropes", 1)[:, 0, :]
        mx_sq = mx.rearrange("p h t j c -> p (h t j c)").rearrange("p (k t) -> p k t", k=4)
        turns_a = big[:, 0:8 * SEQ].rearrange("p (k t) -> p k t", k=8)
        turns_b = big[:, 8 * SEQ:16 * SEQ].rearrange("p (k t) -> p k t", k=8)
        squared = turns_a
        s5n = lxp[:, :, 3:]
        go = ly
        scm = big[:, 16 * SEQ:16 * SEQ + 4 * 384].rearrange("p (h c) -> p h c", h=4)

        psum = [ctx.enter_context(nc.psum_tensor(f"bank{i}", [P, 512], F32)) for i in range(8)]
        main = Units(MAIN, psum[0:4])
        side = Units(SIDE, psum[4:7])
        ybank = psum[7]

        once = {n: nc.alloc_semaphore(n) for n in ("loads", "pre_dve", "pre_act", "pre_pool", "fin_dve", "fin_act",
                                                   "fin_pe", "stored")}
        per_layer = {}

        def S(name):
            if name not in per_layer:
                per_layer[name] = nc.alloc_semaphore(name)
            return per_layer[name]

        def par_(name, a=0, b=None):
            lo, hi = PCOLS[name]
            return par[:, lo + a:(lo + b if b is not None else hi)]

        def cst_(name, a=0, b=None):
            lo, hi = CCOLS[name]
            return cst[:, lo + a:(lo + b if b is not None else hi)]

        def halves(ap, n=2):
            return ap.rearrange("p (k t) -> p k t", k=n)

        def over(ap, n):
            return ap.unsqueeze(1).to_broadcast([P, n, ap.shape[-1]])

        ident, ones, bo = cst_("ident"), cst_("ones"), cst_("bo")
        sm = {}
        for i, n in enumerate(["dt", "lrdt", "th", "mag", "n1", "r1", "r2", "sn", "cs", "ai", "nr", "den", "cre",
                               "cim", "ph", "phl", "t1", "t2"]):
            sm[n] = small[:, 8 * i:8 * i + 8]
        eps_col = small[:, 150:151]
        nega = small[:, 151:152]
        gnh = small[:, 152:153]
        rnh = small[:, 154:156]
        hba, hbi, hbg = small[:, 156:158], small[:, 158:160], small[:, 160:162]
        sp4, ly_, ls_, ls2, lq = (small[:, 162 + 2 * i:164 + 2 * i] for i in range(5))

        def chunk_used(i):
            name = CHUNKS[i][0]
            if name[:2] == "dn":
                f, n = int(name[2]), int(name[4:])
                if n % 4 < 3:
                    return S("down"), 12 * (f - 1) + 3 * (n // 4) + n % 4 + 1
                name = f"dn{f}_{n // 4}"
            elif name[:2] == "wb":
                name = f"mg{2 * int(name[2]) + 1}b"
            return S("main"), main.ready(name)

        with nc.Block() as block:
            @block.sync
            def _(sp):
                sp.dma_start(cst[:], consts).then_inc(once["loads"], 16)
                sp.dma_start(ropec.bitcast(mybir.dt.int32), positions).then_inc(once["loads"], 16)
                sp.dma_start(x, x_in).then_inc(once["loads"], 16)

            @block.gpsimd
            def _(pool):
                nc.gpsimd.memset(qkvp[:, :, 0:3], 0.0)
                nc.gpsimd.memset(lxp[:, :, 0:3], 0.0)
                nc.gpsimd.memset(rows, 0.0)
                nc.gpsimd.memset(state, 0.0)
                nc.gpsimd.memset(eps_col, EPS).then_inc(once["pre_pool"], 1)

            @block.vector
            def _(dve):
                n = [0]

                def link(ins):
                    n[0] += 1
                    ins.then_inc(once["pre_dve"], 1)
                    dve.wait_ge(once["pre_dve"], n[0])

                ang, t, r = tmpA[:, 0, :], tmpA[:, 1, :], tmpB[:, 0, :]
                dve.wait_ge(once["loads"], 48)
                link(nc.vector.tensor_copy(ang, ropec.bitcast(mybir.dt.int32)))
                link(nc.vector.tensor_scalar(ang, ang, cst_("freq"), None, ALU.mult))
                for out, quarter in ((tmpC[:, 0, :], 0.0), (tmpC[:, 1, :], 0.25)):
                    link(nc.vector.tensor_scalar(t, ang, 1.0 / TWO_PI, quarter, ALU.mult, ALU.add))
                    link(nc.vector.tensor_scalar(t, t, ROUND, -ROUND, ALU.add, ALU.add))
                    link(nc.vector.scalar_tensor_tensor(r, t, -PI_C[0], ang, ALU.mult, ALU.add))
                    link(nc.vector.scalar_tensor_tensor(r, t, -PI_C[1], r, ALU.mult, ALU.add))
                    link(nc.vector.scalar_tensor_tensor(r, t, -PI_C[2], r, ALU.mult, ALU.add))
                    link(nc.vector.tensor_scalar(r, r, quarter * TWO_PI, PI_SAFE, ALU.add, ALU.min))
                    link(nc.vector.tensor_scalar(out, r, -PI_SAFE, None, ALU.max))

            @block.scalar
            def _(act):
                act.wait_ge(once["pre_dve"], 2 + 2 * 7)
                nc.scalar.activation(ropes, tmpC[:, 0, :], ACT.Sin)
                nc.scalar.activation(ropec, tmpC[:, 1, :], ACT.Sin).then_inc(once["pre_act"], 1)

        with nc.Fori(0, DEPTH) as layer:
            with nc.Block() as block:
                @block.sync
                def _(sp):
                    sp.dma_start(par[:], params[bass.ds(layer, 1), :, :].rearrange("a p n -> (a p) n")).then_inc(S("par"), 16)
                    for i, (name, n) in enumerate(CHUNKS):
                        if i >= SLOTS:
                            sp.wait_ge(*chunk_used(i - SLOTS))
                        at = CHUNK_AT[name]
                        src = weights[bass.ds(layer, 1), at:at + P * n].rearrange("a (p n) -> (a p) n", p=P)
                        s0 = (i % SLOTS) * SLOT
                        sp.dma_start(ring[:, s0:s0 + n], src).then_inc(S(f"slot{i % SLOTS}"), 16)

                @block.tensor
                def _(pe):
                    mm = nc.tensor.matmul

                    def chunk(name):
                        i = CHUNK_INDEX[name]
                        pe.wait_ge(S(f"slot{i % SLOTS}"), 16 * (i // SLOTS + 1))
                        s0 = (i % SLOTS) * SLOT
                        return ring[:, s0:s0 + CHUNKS[i][1]]

                    def main_bank(name):
                        if main.previous(name):
                            who = main.previous(name)
                            pe.wait_ge(S(f"main_{who[1]}"), main.taken(who[0]))
                        return main.bank(name)

                    def side_bank(name):
                        if side.previous(name):
                            who = side.previous(name)
                            pe.wait_ge(S(f"side_{who[1]}"), side.taken(who[0]))
                        return side.bank(name)

                    def ssq(unit, which):
                        ps = main_bank(unit)
                        for k in range(KD):
                            if k % 2 == 0:
                                pe.wait_ge(S("squares"), which * 4 + k // 2 + 1)
                            last = mm(ps[:, 0:SEQ], ones, squared[:, k, :], start=(k == 0), stop=(k == KD - 1))
                        last.then_inc(S("main"), 1)

                    def pair(unit, which=None):
                        w = chunk(unit).rearrange("p (o k m) -> p o k m", o=2, k=KD)
                        ps = main_bank(unit)
                        for o in range(2):
                            for k in range(KD):
                                if which is not None and o == 0:
                                    pe.wait_ge(S("normed"), which * KD + k + 1)
                                last = mm(ps[:, o * SEQ:(o + 1) * SEQ], w[:, o, k, :], xn[:, k, :], start=(k == 0), stop=(k == KD - 1))
                        last.then_inc(S("main"), 1)

                    def ffn(f, which):
                        for m in range(MF):
                            pair(f"gu{f}_{m}", which if m == 0 else None)
                        for j in range(4):
                            unit = f"dn{f}_{j}"
                            ps = main_bank(unit)
                            for o in range(2):
                                for half in range(2):
                                    w = chunk(f"dn{f}_{4 * j + 2 * o + half}").rearrange("p (k m) -> p k m", k=11)
                                    for k in range(11):
                                        m = 11 * half + k
                                        if j == 0 and o == 0:
                                            pe.wait_ge(S("main_dve"), main.taken(f"gu{f}_{m}"))
                                        last = mm(ps[:, o * SEQ:(o + 1) * SEQ], w[:, k, :], hidden[:, m, :],
                                                  start=(m == 0), stop=(m == MF - 1))
                                    if (o, half) != (1, 1):
                                        last.then_inc(S("down"), 1)
                            last.then_inc(S("main"), 1)

                    ssq("ssq1", 0)
                    ffn(1, 0)
                    ssq("ssqm", 1)
                    w = chunk("ba").rearrange("p (k m) -> p k m", k=KD)
                    ps = main_bank("ba")
                    for k in range(KD):
                        pe.wait_ge(S("normed"), KD + k + 1)
                        last = mm(ps[:, 0:SEQ], w[:, k, :], xn[:, k, :], start=(k == 0), stop=(k == KD - 1))
                    last.then_inc(S("main"), 1)
                    for unit in PROJ[1:11]:
                        pair(unit)
                    w = chunk("rv").rearrange("p (k m) -> p k m", k=KD)
                    ps = main_bank("rv")
                    for j in range(2):
                        for k in range(KD):
                            last = mm(ps[:, j * 256:(j + 1) * 256], xn[:, k, j * P:(j + 1) * P], w[:, k, :], start=(k == 0), stop=(k == KD - 1))
                    last.then_inc(S("main"), 1)

                    def gate(i):
                        pair(f"g{i}")

                    pe.wait_ge(S("par"), 16)
                    pe.wait_ge(S("lru_conv"), 1)
                    xc = tmpA
                    for unit, wname in (("lr", "wa"), ("li", "wi")):
                        ps = side_bank(unit)
                        for t in range(2):
                            last = mm(ps[:, t * SEQ:(t + 1) * SEQ], par_(wname, t * P, (t + 1) * P), xc[:, t, :], start=True, stop=True)
                        last.then_inc(S("side"), 1)
                    gate(0)
                    for unit, q0, ev in (("l2q", 0, 1), ("l2k", 2, 2)):
                        pe.wait_ge(S("qk_sq"), ev)
                        ps = side_bank(unit)
                        for t in range(2):
                            last = mm(ps[:, t * SEQ:(t + 1) * SEQ], bo, mx_sq[:, q0 + t, :], start=True, stop=True)
                        last.then_inc(S("side"), 1)
                    gate(1)
                    pe.wait_ge(S("rows"), 1)
                    ps = side_bank("rowt")
                    for j in range(2):
                        last = nc.tensor.transpose(ps[:, j * P:(j + 1) * P], rows[:, j * P:(j + 1) * P], ident)
                    last.then_inc(S("side"), 1)
                    pe.wait_ge(S("k_normed"), 1)
                    for unit, q0 in (("ktr", 2), ("vtr", 4)):
                        ps = side_bank(unit)
                        for j in range(2):
                            for t in range(2):
                                last = nc.tensor.transpose(ps[:, j * 256 + t * P:j * 256 + (t + 1) * P], qkv[:, q0 + t, j * P:(j + 1) * P], ident)
                        last.then_inc(S("side"), 1)
                    ps = side_bank("eb")
                    for t in range(2):
                        last = mm(ps[:, t * SEQ:(t + 1) * SEQ], cst_("selp", t * P, (t + 1) * P), rows, start=True, stop=True)
                    last.then_inc(S("side"), 1)
                    gate(2)

                    def over_all(unit, sel, hp):
                        ps = side_bank(unit)
                        for t in range(2):
                            h = 2 * t + hp
                            last = mm(ps[:, t * SEQ:(t + 1) * SEQ], cst_(sel, h * P, (h + 1) * P), rows, start=True, stop=True)
                        last.then_inc(S("side"), 1)

                    def against_k(unit, q0, hp):
                        ps = side_bank(unit)
                        r = slice(64 * hp, 64 * hp + 64)
                        for t in range(2):
                            for j in range(2):
                                c = slice(j * P, (j + 1) * P)
                                o = (t * 2 + j) * P
                                last = mm(ps[:, o:o + P], qkv[r, 2 + t, c], qkv[r, q0 + t, c], start=True, stop=True)
                        last.then_inc(S("side"), 1)

                    over_all("gb0", "selg", 0)
                    over_all("gb1", "selg", 1)
                    against_k("kk0", 2, 0)
                    over_all("bb0", "selb", 0)
                    against_k("kk1", 2, 1)
                    over_all("bb1", "selb", 1)
                    gate(3)
                    against_k("qk0", 0, 0)
                    against_k("qk1", 0, 1)
                    gate(4)

                    def s5_in(s):
                        ps = side_bank(f"pq{s}")
                        mm(ps[:, 0:SEQ], par_("sbr", s * P, (s + 1) * P), su[:, s // 4, :], start=True, stop=True)
                        mm(ps[:, SEQ:512], par_("sbi", s * P, (s + 1) * P), su[:, s // 4, :], start=True, stop=True).then_inc(S("side"), 1)

                    def s5_out(s):
                        pe.wait_ge(S("s5x"), s + 1)
                        q = 32 * (s % 4)
                        o = ybank[q:q + 32, (s // 4) * SEQ:(s // 4 + 1) * SEQ]
                        xs = (tmpE, tmpF)[s % 2]
                        mm(o, par_("scr", s * 32, s * 32 + 32), xs[:, 0, :], start=True, stop=False, tile_position=(0, q))
                        mm(o, par_("sci", s * 32, s * 32 + 32), xs[:, 1, :], start=False, stop=True, tile_position=(0, q)).then_inc(S("s5y"), 1)

                    pe.wait_ge(S("main_act"), main.taken("su"))
                    pe.wait_ge(S("xy_init"), 1)
                    for lv in range(LEVELS):
                        for hp in range(2):
                            pe.wait_ge(S("lowc"), 2 * lv + hp + 1)
                            if lv:
                                pe.wait_ge(S("side_dve"), side.taken(f"xt{hp}_{lv - 1}"))
                            ps = side_bank(f"t{hp}_{lv}")
                            for i in range(4):
                                t, j = i // 2, i % 2
                                last = mm(ps[:, i * P:(i + 1) * P], lowc[:, hp, t, j, :], mx[:, hp, t, j, :], start=True, stop=True)
                            last.then_inc(S("side"), 1)
                        gate(5 + lv)
                        for hp in range(2):
                            pe.wait_ge(S("side_act"), side.taken(f"t{hp}_{lv}"))
                            if lv:
                                pe.wait_ge(S("side_dve"), side.taken(f"ty{hp}_{lv - 1}"))
                            for unit in (f"xt{hp}_{lv}", f"ty{hp}_{lv}"):
                                ps = side_bank(unit)
                                for i in range(4):
                                    t, j = i // 2, i % 2
                                    a, b = (my, mt) if unit[0] == "x" else (mt, my)
                                    last = mm(ps[:, i * P:(i + 1) * P], a[:, hp, t, j, :], b[:, hp, t, j, :], start=True, stop=True)
                                last.then_inc(S("side"), 1)
                        if lv < 4:
                            s5_in(2 * lv)
                            s5_in(2 * lv + 1)
                        if 0 < lv < 5:
                            s5_out(2 * lv - 2)
                            s5_out(2 * lv - 1)
                    pe.wait_ge(S("main_act"), main.taken("rv"))
                    for unit, src in (("rotq", rq), ("rotk", rk)):
                        ps = side_bank(unit)
                        for t in range(2):
                            last = mm(ps[:, t * SEQ:(t + 1) * SEQ], cst_("perm"), src[:, t, :], start=True, stop=True)
                        last.then_inc(S("side"), 1)
                    pe.wait_ge(S("side_dve"), side.taken(f"ty1_{LEVELS - 1}"))
                    ps = side_bank("u")
                    for h in range(NH):
                        t, hp = h // 2, h % 2
                        for j in range(2):
                            o = j * 256 + h * DH
                            last = mm(ps[:, o:o + DH], my[:, hp, t, j, :], vb[:, j, h * DH:(h + 1) * DH], start=True, stop=True)
                    last.then_inc(S("side"), 1)
                    ps = side_bank("w")
                    for h in range(NH):
                        t, hp = h // 2, h % 2
                        for j in range(2):
                            o = t * SEQ + j * P
                            last = mm(ps[64 * hp:64 * hp + 64, o:o + P], kbe[:, j, h * DH:(h + 1) * DH], my[:, hp, t, j, :], start=True, stop=True)
                    last.then_inc(S("side"), 1)

                    def state_up(n):
                        j, r = n // 2, slice(64 * (n % 2), 64 * (n % 2) + 64)
                        if n == 0:
                            pe.wait_ge(S("side_act"), side.taken("u"))
                        else:
                            pe.wait_ge(S("side_dve"), side.taken(f"ws{n}"))
                        ps = side_bank(f"su{n}")
                        for t in range(2):
                            last = mm(ps[:, t * P:(t + 1) * P], kdec[r, j, t * P:(t + 1) * P], uu[r, j, t * P:(t + 1) * P], start=True, stop=True)
                        last.then_inc(S("side"), 1)

                    def from_state(n):
                        r0 = 64 * (n % 2)
                        c = slice(64 * n, 64 * n + 64)
                        pe.wait_ge(S("side_dve"), side.taken(f"su{n - 1}"))
                        pe.wait_ge(S("side_act"), side.taken("w"))
                        ps = side_bank(f"ws{n}")
                        for t in range(2):
                            last = mm(ps[r0:r0 + 64, t * P:(t + 1) * P], wT[:, t, c], state[:, t, :], start=True, stop=True)
                        last.then_inc(S("side"), 1)
                        ps = side_bank(f"oi{n}")
                        for t in range(2):
                            last = mm(ps[:, t * 64:(t + 1) * 64], state[:, t, :], qdec[:, t, c], start=True, stop=True)
                        last.then_inc(S("side"), 1)

                    def scores(h):
                        t, r = h // 2, slice(64 * (h % 2), 64 * (h % 2) + 64)
                        ps = side_bank(f"sc{h}")
                        mm(ps[:, 0:SEQ], rk[r, t, 0:P], rq[r, t, :], start=True, stop=True)
                        mm(ps[:, SEQ:384], rk[r, t, P:SEQ], rq[r, t, P:SEQ], start=True, stop=True).then_inc(S("side"), 1)

                    gate(11)
                    state_up(0)
                    pe.wait_ge(S("rotated"), 2)
                    scores(0)
                    scores(1)
                    gate(12)
                    from_state(1)
                    state_up(1)
                    scores(2)
                    scores(3)
                    gate(13)
                    from_state(2)
                    state_up(2)
                    pe.wait_ge(S("side_dve"), side.taken("sc3"))
                    ps = side_bank("ro")
                    for h in range(NH):
                        t, q = h // 2, 64 * (h % 2)
                        v = slice(h * DH, (h + 1) * DH)
                        mm(ps[q:q + 64, t * SEQ:(t + 1) * SEQ], rv[:, 0, v], scm[:, h, 0:SEQ], start=True, stop=False)
                        last = mm(ps[q:q + 64, t * SEQ + P:(t + 1) * SEQ], rv[:, 1, v], scm[:, h, SEQ:384], start=False, stop=True)
                    last.then_inc(S("side"), 1)
                    gate(14)
                    from_state(3)
                    pe.wait_ge(S("side_act"), side.taken("ro"))
                    ps = side_bank("rm")
                    for t in range(2):
                        last = mm(ps[:, t * SEQ:(t + 1) * SEQ], bo, tmpB[:, t, :], start=True, stop=True)
                    last.then_inc(S("side"), 1)
                    gate(15)
                    pe.wait_ge(S("side_dve"), side.taken("ws3"))
                    for j in range(2):
                        ps = side_bank(f"oa{j}")
                        for h in range(NH):
                            t, q = h // 2, 64 * (h % 2)
                            last = mm(ps[q:q + 64, t * P:(t + 1) * P], uu[:, j, h * DH:(h + 1) * DH], attn[:, h % 2, t, j, :], start=True, stop=True)
                        last.then_inc(S("side"), 1)
                    for unit, ev, src in (("rv2", "ro_sq", tmpC), ("gs", "go_sq", tmpD)):
                        pe.wait_ge(S(ev), 1)
                        ps = side_bank(unit)
                        for t in range(2):
                            last = mm(ps[:, t * SEQ:(t + 1) * SEQ], bo, src[:, t, :], start=True, stop=True)
                        last.then_inc(S("side"), 1)
                    pe.wait_ge(S("s5g"), 1)
                    ps = side_bank("glu")
                    for o in range(2):
                        for k in range(2):
                            c = k * 256 + o * P
                            last = mm(ps[:, o * SEQ:(o + 1) * SEQ], par_("wglu", c, c + P), tmpE[:, k, :], start=(k == 0), stop=(k == 1))
                    last.then_inc(S("side"), 1)

                    for b in range(NB):
                        pe.wait_ge(S(f"branch{b}"), 1)
                    for i in range(4):
                        w = chunk(f"wb{i}").rearrange("p (o n k m) -> p o n k m", o=2, n=NB, k=2)
                        for o in range(2):
                            for ab in range(2):
                                unit = f"mg{2 * i + o}{'ab'[ab]}"
                                ps = main_bank(unit)
                                for n2 in range(2):
                                    for k in range(2):
                                        last = mm(ps[:, n2 * SEQ:(n2 + 1) * SEQ], w[:, o, 2 * ab + n2, k, :], out_br[:, 2 * ab + n2, k, :],
                                                  start=(k == 0), stop=(k == 1))
                                last.then_inc(S("main"), 1)
                    for i in range(4):
                        w = chunk(f"wo{i}").rearrange("p (o k m) -> p o k m", o=2, k=KD)
                        ps = main_bank(f"wo{i}")
                        for o in range(2):
                            for k in range(KD):
                                if i == 0 and o == 0:
                                    pe.wait_ge(S("merged"), k + 1)
                                last = mm(ps[:, o * SEQ:(o + 1) * SEQ], w[:, o, k, :], xn[:, k, :], start=(k == 0), stop=(k == KD - 1))
                        last.then_inc(S("main"), 1)
                    ssq("ssq2", 2)
                    ffn(2, 2)

                @block.scalar
                def _(act):
                    A = nc.scalar.activation
                    chain = [0]

                    def link(ins):
                        chain[0] += 1
                        ins.then_inc(S("act"), 1)
                        act.wait_ge(S("act"), chain[0])

                    def squares(which):
                        for j in range(4):
                            if which:
                                act.wait_ge(S("main_dve"), main.taken((f"dn1_{j}", f"wo{j}")[which - 1]))
                            A(squared[:, 2 * j:2 * j + 2, :], x[:, 2 * j:2 * j + 2, :], ACT.Square).then_inc(S("squares"), 1)

                    def rms(unit, which):
                        squares(which)
                        act.wait_ge(S("main"), main.ready(unit))
                        A(tmpA[:, 0, :], main.bank(unit)[:, 0:SEQ], ACT.Sqrt, bias=eps_col, scale=1.0 / DM).then_inc(S("main_act"), 1)

                    def silus(f, ms):
                        for m in ms:
                            act.wait_ge(S("main"), main.ready(f"gu{f}_{m}"))
                            if m >= 2:
                                act.wait_ge(S("main_dve"), main.taken(f"gu{f}_{m - 2}"))
                            A(tmpB[:, m % 2, :], main.bank(f"gu{f}_{m}")[:, 0:SEQ], ACT.Silu).then_inc(S(f"silu{f}"), 1)

                    rms("ssq1", 0)
                    act.wait_ge(S("par"), 16)
                    A(sm["dt"], par_("ldt"), ACT.Exp)
                    A(nega, par_("alog"), ACT.Exp)
                    link(A(lq, par_("lam"), ACT.Abs))
                    A(ly_, lq, ACT.Exp, scale=-1.0).then_inc(S("pexp"), 1)
                    act.wait_ge(S("pmul"), 1)
                    A(sm["mag"], sm["lrdt"], ACT.Exp).then_inc(S("pexp"), 1)
                    silus(1, range(0, 4))
                    act.wait_ge(S("pang"), 1)
                    A(sm["sn"], sm["r1"], ACT.Sin)
                    A(sm["cs"], sm["r2"], ACT.Sin).then_inc(S("psin"), 1)
                    silus(1, range(4, 10))
                    act.wait_ge(S("turns"), 1)
                    A(sinE, turns_a, ACT.Sin, scale=SIN_SCALE).then_inc(S("tables"), 1)
                    silus(1, range(10, 11))
                    act.wait_ge(S("turns"), 2)
                    A(cosE, turns_b, ACT.Sin, scale=SIN_SCALE).then_inc(S("tables"), 1)
                    silus(1, range(11, MF))
                    rms("ssqm", 1)

                    act.wait_ge(S("main"), main.ready("ba"))
                    A(tmpG[:, 0, :], main.bank("ba")[:, 0:SEQ], ACT.Identity, bias=par_("dtb")).then_inc(S("main_act"), 1)
                    act.wait_ge(S("main_act"), main.taken("ba"))
                    link(A(tmpF[:, 0, :], tmpG[:, 0, :], ACT.Abs))
                    link(A(tmpF[:, 0, :], tmpF[:, 0, :], ACT.Exp, scale=-1.0))
                    A(tmpF[:, 1, :], tmpF[:, 0, :], ACT.Ln, bias=1.0).then_inc(S("ln1p"), 1)
                    A(tmpG[:, 1, :], tmpG[:, 0, :], ACT.Tanh, scale=0.5).then_inc(S("ln1p"), 1)
                    for i in range(3):
                        act.wait_ge(S("main"), main.ready(f"qkv{i}"))
                        A(qkvp[:, 2 * i:2 * i + 2, 3:], halves(main.bank(f"qkv{i}")[:]), ACT.Identity).then_inc(S("main_act"), 1)
                    act.wait_ge(S("gc"), 1)
                    A(tmpF[:, 0, :], tmpC[:, 0, :], ACT.Exp)
                    for n in range(NCH):
                        c = slice(64 * n, 64 * n + 64)
                        last = A(tmpF[:, 1, c], tmpC[:, 0, c], ACT.Exp, scale=-1.0, bias=tmpC[:, 0, 64 * n + 63:64 * n + 64])
                    last.then_inc(S("egc"), 1)
                    for unit, dst in (("lx", lxp[:, :, 3:]), ("ly", ly), ("su", su), ("z", zz)):
                        act.wait_ge(S("main"), main.ready(unit))
                        A(dst, halves(main.bank(unit)[:]), ACT.Identity).then_inc(S("main_act"), 1)
                    act.wait_ge(S("main_act"), main.taken("z"))
                    act.wait_ge(S("conv"), 1)
                    A(qkvp[:, :, 3:], qkv, ACT.Tanh, scale=0.5).then_inc(S("conv_t"), 1)
                    A(tmpG, zz, ACT.Tanh, scale=0.5).then_inc(S("zt"), 1)
                    for unit, dst in (("rq", rq), ("rk", rk), ("rg", rg), ("rv", rv)):
                        act.wait_ge(S("main"), main.ready(unit))
                        A(dst, halves(main.bank(unit)[:]), ACT.Identity).then_inc(S("main_act"), 1)
                    act.wait_ge(S("silu_q"), 1)
                    A(mx_sq[:, 0:2, :], qkv[:, 0:2, :], ACT.Square, scale=0.5).then_inc(S("qk_sq"), 1)
                    A(mx_sq[:, 2:4, :], qkv[:, 2:4, :], ACT.Square, scale=0.5).then_inc(S("qk_sq"), 1)

                    def gate(i):
                        act.wait_ge(S("main"), main.ready(f"g{i}"))
                        if i == 11:
                            act.wait_ge(S("s5x"), 8)
                        A(gates[:, 2 * i:2 * i + 2, :], halves(main.bank(f"g{i}")[:]), ACT.Tanh, scale=0.5).then_inc(S("main_act"), 1)

                    for unit, dst, hb in (("lr", tmpB, hba), ("li", tmpD, hbi)):
                        act.wait_ge(S("side"), side.ready(unit))
                        A(dst[:, 0, :], side.bank(unit)[:, 0:SEQ], ACT.Tanh, scale=0.5, bias=hb[:, 0:1])
                        A(dst[:, 1, :], side.bank(unit)[:, SEQ:512], ACT.Tanh, scale=0.5, bias=hb[:, 1:2]).then_inc(S("side_act"), 1)
                    act.wait_ge(S("log_a"), 1)
                    A(tmpE, tmpC, ACT.Tanh, scale=-1.0).then_inc(S("lru_t"), 1)
                    act.wait_ge(S("lru_t"), 1)
                    A(tmpC, tmpC, ACT.Exp).then_inc(S("lru_a"), 1)
                    gate(0)
                    for unit, dst in (("l2q", mx_sq[:, 0:2, :]), ("l2k", mx_sq[:, 2:4, :])):
                        act.wait_ge(S("side"), side.ready(unit))
                        A(dst, halves(side.bank(unit)[:]), ACT.Sqrt, scale=float(DH), bias=eps_col).then_inc(S("side_act"), 1)
                    act.wait_ge(S("lru_q"), 1)
                    A(tmpE, tmpE, ACT.Sqrt, scale=0.5).then_inc(S("lru_m"), 1)
                    gate(1)
                    act.wait_ge(S("side"), side.ready("rowt"))
                    A(rowT, halves(side.bank("rowt")[:, 0:SEQ]), ACT.Identity).then_inc(S("side_act"), 1)
                    act.wait_ge(S("gelu_in"), 1)
                    A(tmpD, tmpD, ACT.Tanh, scale=GELU_C).then_inc(S("gelu_t"), 1)
                    act.wait_ge(S("side"), side.ready("eb"))
                    A(egb, halves(side.bank("eb")[:]), ACT.Exp).then_inc(S("side_act"), 1)
                    gate(2)
                    for hp in range(2):
                        act.wait_ge(S("side_dve"), side.taken(f"gb{hp}"))
                        A(flat(dec)[:, hp, :], flat(dec)[:, hp, :], ACT.Exp).then_inc(S("dec"), 1)
                    gate(3)
                    gate(4)
                    for lv in range(LEVELS):
                        for hp in range(2):
                            act.wait_ge(S("side"), side.ready(f"t{hp}_{lv}"))
                            A(flat(mt)[:, hp, :], side.bank(f"t{hp}_{lv}")[:], ACT.Identity).then_inc(S("side_act"), 1)
                        gate(5 + lv)
                    act.wait_ge(S("side"), side.ready("u"))
                    A(uu, halves(side.bank("u")[:]), ACT.Identity).then_inc(S("side_act"), 1)
                    act.wait_ge(S("side"), side.ready("w"))
                    A(wT, halves(side.bank("w")[:]), ACT.Identity).then_inc(S("side_act"), 1)
                    gate(11)

                    def inter(n):
                        act.wait_ge(S("side"), side.ready(f"oi{n}"))
                        A(go[:, :, 64 * n:64 * n + 64], halves(side.bank(f"oi{n}")[:, 0:P]), ACT.Identity).then_inc(S("side_act"), 1)

                    gate(12)
                    inter(1)
                    act.wait_ge(S("rotated"), 2)
                    A(tmpA, rg, ACT.Tanh, scale=0.5).then_inc(S("rgt"), 1)
                    gate(13)
                    inter(2)
                    act.wait_ge(S("side"), side.ready("ro"))
                    A(tmpB, halves(side.bank("ro")[:]), ACT.Identity).then_inc(S("side_act"), 1)
                    gate(14)
                    inter(3)
                    act.wait_ge(S("side_dve"), side.taken("rm"))
                    A(tmpC, tmpB, ACT.Square).then_inc(S("ro_sq"), 1)
                    gate(15)
                    act.wait_ge(S("side_dve"), side.taken("oa1"))
                    A(tmpD, go, ACT.Square).then_inc(S("go_sq"), 1)
                    act.wait_ge(S("side"), side.ready("rv2"))
                    A(tmpC, halves(side.bank("rv2")[:]), ACT.Sqrt, bias=eps_col).then_inc(S("side_act"), 1)
                    act.wait_ge(S("side"), side.ready("gs"))
                    A(tmpD, halves(side.bank("gs")[:]), ACT.Sqrt, bias=eps_col).then_inc(S("side_act"), 1)
                    act.wait_ge(S("s5gin"), 1)
                    A(tmpE, tmpE, ACT.Tanh, scale=GELU_C).then_inc(S("s5gt"), 1)
                    act.wait_ge(S("side"), side.ready("glu"))
                    A(tmpF[:, 0, :], side.bank("glu")[:, 0:SEQ], ACT.Tanh, scale=0.25, bias=hbg[:, 0:1])
                    A(tmpF[:, 1, :], side.bank("glu")[:, SEQ:512], ACT.Tanh, scale=0.25, bias=hbg[:, 1:2]).then_inc(S("side_act"), 1)
                    rms("ssq2", 2)
                    silus(2, range(MF))

                @block.gpsimd
                def _(pool):
                    tt = nc.gpsimd.tensor_tensor
                    pool.wait_ge(S("k_normed"), 1)
                    for m in (mx, my):
                        last = nc.gpsimd.tensor_copy(m.rearrange("p h t j c -> p (h t j) c"), over(ident, 8))
                    last.then_inc(S("xy_init"), 1)

                    def level_blocks(lv):
                        for hp in range(2):
                            if lv == 0:
                                pool.wait_ge(S("side_dve"), side.taken(f"qk{hp}"))
                            else:
                                pool.wait_ge(S("side"), side.ready(f"t{hp}_{lv - 1}"))
                            tt(lowc[:, hp].rearrange("p t j c -> p (t j) c"), low[:, hp].rearrange("p t j c -> p (t j) c"),
                               over(cst_("lev", lv * P, (lv + 1) * P), 4), ALU.mult).then_inc(S("lowc"), 1)

                    def s5_back(s):
                        ss, xs = (tmpC, tmpD)[s % 2], (tmpE, tmpF)[s % 2]
                        pool.wait_ge(S("s5s"), s + 1)
                        if s >= 1:
                            pool.wait_ge(S("s5x"), s)
                        if s >= 2:
                            pool.wait_ge(S("s5y"), s - 1)
                        tt(xs, ss, over(cosE[:, s, :], 2), ALU.mult)
                        tt(s5n, ss, over(sinE[:, s, :], 2), ALU.mult).then_inc(S("pool"), 1)
                        pool.wait_ge(S("pool"), s + 1)
                        tt(xs[:, 0, :], xs[:, 0, :], s5n[:, 1, :], ALU.subtract)
                        tt(xs[:, 1, :], xs[:, 1, :], s5n[:, 0, :], ALU.add).then_inc(S("s5x"), 1)

                    level_blocks(0)
                    for lv in range(LEVELS):
                        if lv + 1 < LEVELS:
                            level_blocks(lv + 1)
                        if lv < 4:
                            s5_back(2 * lv)
                            s5_back(2 * lv + 1)

                @block.vector
                def _(dve):
                    V = nc.vector
                    chain = [0]

                    def link(ins):
                        chain[0] += 1
                        ins.then_inc(S("dve"), 1)
                        dve.wait_ge(S("dve"), chain[0])

                    def normed(unit, which, wname):
                        dve.wait_ge(S("main_act"), main.taken(unit))
                        link(V.reciprocal(tmpA[:, 1, :], tmpA[:, 0, :]))
                        for k in range(KD):
                            V.scalar_tensor_tensor(xn[:, k, :], x[:, k, :], par_(wname, k, k + 1), tmpA[:, 1, :], ALU.mult, ALU.mult).then_inc(S("normed"), 1)

                    def up(f, ms):
                        for m in ms:
                            dve.wait_ge(S(f"silu{f}"), m + 1)
                            ps = main.bank(f"gu{f}_{m}")
                            V.tensor_tensor(hidden[:, m, :], tmpB[:, m % 2, :], ps[:, SEQ:512], ALU.mult).then_inc(S("main_dve"), 1)

                    def down(units, scale):
                        for j, unit in enumerate(units):
                            dve.wait_ge(S("main"), main.ready(unit))
                            V.scalar_tensor_tensor(x[:, 2 * j:2 * j + 2, :], halves(main.bank(unit)[:]), scale, x[:, 2 * j:2 * j + 2, :],
                                                   ALU.mult, ALU.add).then_inc(S("main_dve"), 1)

                    dve.wait_ge(S("par"), 16)
                    normed("ssq1", 0, "n1")
                    lre, lim = par_("lre"), par_("lim")
                    dve.wait_ge(S("pexp"), 1)
                    V.tensor_tensor(sm["lrdt"], lre, sm["dt"], ALU.mult).then_inc(S("pmul"), 1)
                    link(V.tensor_tensor(sm["th"], lim, sm["dt"], ALU.mult))
                    for r, quarter in ((sm["r1"], 0.0), (sm["r2"], 0.25)):
                        link(V.tensor_scalar(sm["n1"], sm["th"], 1.0 / TWO_PI, quarter, ALU.mult, ALU.add))
                        link(V.tensor_scalar(sm["n1"], sm["n1"], ROUND, -ROUND, ALU.add, ALU.add))
                        link(V.scalar_tensor_tensor(r, sm["n1"], -PI_C[0], sm["th"], ALU.mult, ALU.add))
                        link(V.scalar_tensor_tensor(r, sm["n1"], -PI_C[1], r, ALU.mult, ALU.add))
                        link(V.scalar_tensor_tensor(r, sm["n1"], -PI_C[2], r, ALU.mult, ALU.add))
                        link(V.tensor_scalar(r, r, quarter * TWO_PI, PI_SAFE, ALU.add, ALU.min))
                        link(V.tensor_scalar(r, r, -PI_SAFE, None, ALU.max))
                    link(V.tensor_scalar(sm["ph"], sm["r1"], 1.0 / TWO_PI, None, ALU.mult))
                    link(V.tensor_scalar(sm["t1"], sm["ph"], GRID, -GRID, ALU.add, ALU.add))
                    V.tensor_tensor(sm["phl"], sm["ph"], sm["t1"], ALU.subtract).then_inc(S("pang"), 1)
                    dve.wait_ge(S("pang"), 1)
                    up(1, range(0, 3))
                    dve.wait_ge(S("pmul"), 1)
                    V.tensor_scalar(nega, nega, -1.0, None, ALU.mult)
                    V.tensor_scalar(gnh, par_("gnorm"), 0.5, None, ALU.mult)
                    V.tensor_scalar(rnh, par_("rnorm"), 0.5, None, ALU.mult)
                    V.tensor_scalar(hba, par_("lba"), 0.5, None, ALU.mult)
                    V.tensor_scalar(hbi, par_("lbi"), 0.5, None, ALU.mult)
                    link(V.tensor_scalar(hbg, par_("bglu"), 0.5, None, ALU.mult))
                    link(V.tensor_scalar(ls_, ly_, 2.0, None, ALU.add))
                    link(V.reciprocal(ls_, ls_))
                    link(V.tensor_tensor(ls_, ls_, ly_, ALU.mult))
                    link(V.tensor_tensor(ls2, ls_, ls_, ALU.mult))
                    link(V.tensor_scalar(lq, ls2, 1.0 / 19, None, ALU.mult))
                    for k in range(17, 2, -2):
                        link(V.scalar_tensor_tensor(lq, lq, 1.0 / k, ls2, ALU.add, ALU.mult))
                    link(V.scalar_tensor_tensor(lq, lq, 1.0, ls_, ALU.add, ALU.mult))
                    link(V.tensor_scalar(sp4, par_("lam"), -1.0, 0.0, ALU.mult, ALU.max))
                    link(V.scalar_tensor_tensor(sp4, lq, 2.0, sp4, ALU.mult, ALU.add))
                    link(V.tensor_scalar(sp4, sp4, -4.0, None, ALU.mult))
                    dve.wait_ge(S("psin"), 1)
                    dve.wait_ge(S("pexp"), 2)
                    link(V.tensor_tensor(sm["ai"], sm["mag"], sm["sn"], ALU.mult))
                    link(V.tensor_tensor(sm["nr"], sm["mag"], sm["cs"], ALU.mult))
                    link(V.tensor_scalar(sm["nr"], sm["nr"], -1.0, None, ALU.add))
                    link(V.tensor_tensor(sm["den"], lre, lre, ALU.mult))
                    link(V.tensor_tensor(sm["t2"], lim, lim, ALU.mult))
                    link(V.tensor_tensor(sm["den"], sm["den"], sm["t2"], ALU.add))
                    link(V.reciprocal(sm["den"], sm["den"]))
                    link(V.tensor_tensor(sm["cre"], sm["nr"], lre, ALU.mult))
                    link(V.tensor_tensor(sm["t2"], sm["ai"], lim, ALU.mult))
                    link(V.tensor_tensor(sm["cre"], sm["cre"], sm["t2"], ALU.add))
                    link(V.tensor_tensor(sm["cre"], sm["cre"], sm["den"], ALU.mult))
                    link(V.tensor_tensor(sm["cim"], sm["ai"], lre, ALU.mult))
                    link(V.tensor_tensor(sm["t2"], sm["nr"], lim, ALU.mult))
                    link(V.tensor_tensor(sm["cim"], sm["cim"], sm["t2"], ALU.subtract))
                    link(V.tensor_tensor(sm["cim"], sm["cim"], sm["den"], ALU.mult))
                    up(1, range(3, 5))
                    cr, ci = halves(par_("scr"), 8), halves(par_("sci"), 8)
                    bre = sm["cre"].unsqueeze(2).to_broadcast([P, 8, 32])
                    bim = sm["cim"].unsqueeze(2).to_broadcast([P, 8, 32])
                    c1, c2 = halves(tmpC[:, 0, :], 8), halves(tmpC[:, 1, :], 8)
                    link(V.tensor_tensor(c1, ci, bim, ALU.mult))
                    link(V.tensor_tensor(c2, cr, bim, ALU.mult))
                    link(V.tensor_tensor(cr, cr, bre, ALU.mult))
                    link(V.tensor_tensor(cr, cr, c1, ALU.subtract))
                    link(V.tensor_tensor(ci, ci, bre, ALU.mult))
                    link(V.scalar_tensor_tensor(ci, ci, -1.0, c2, ALU.mult, ALU.subtract))
                    up(1, range(5, 7))
                    ta, tb = turns_a, turns_b
                    tok = over(cst_("tok"), 8)
                    link(V.tensor_tensor(ta, tok, sm["t1"].unsqueeze(2).to_broadcast([P, 8, SEQ]), ALU.mult))
                    link(V.tensor_scalar(tb, ta, ROUND, -ROUND, ALU.add, ALU.add))
                    up(1, range(7, 8))
                    link(V.tensor_tensor(ta, ta, tb, ALU.subtract))
                    link(V.tensor_tensor(tb, tok, sm["phl"].unsqueeze(2).to_broadcast([P, 8, SEQ]), ALU.mult))
                    up(1, range(8, 9))
                    link(V.tensor_tensor(tb, ta, tb, ALU.add))
                    link(V.tensor_scalar(ta, tb, ROUND, -ROUND, ALU.add, ALU.add))
                    up(1, range(9, 10))
                    V.tensor_tensor(ta, tb, ta, ALU.subtract).then_inc(S("turns"), 1)
                    link(V.tensor_scalar(tb, tb, 0.25, None, ALU.add))
                    up(1, range(10, 11))
                    dve.wait_ge(S("tables"), 1)
                    link(V.tensor_scalar(ta, tb, ROUND, -ROUND, ALU.add, ALU.add))
                    V.tensor_tensor(tb, tb, ta, ALU.subtract).then_inc(S("turns"), 1)
                    up(1, range(11, MF))
                    down([f"dn1_{j}" for j in range(4)], 0.5)

                    normed("ssqm", 1, "nm")
                    dve.wait_ge(S("ln1p"), 1)
                    link(V.scalar_tensor_tensor(tmpC[:, 1, :], tmpG[:, 0, :], 0.0, tmpF[:, 1, :], ALU.max, ALU.add))
                    link(V.tensor_scalar(tmpC[:, 1, :], tmpC[:, 1, :], nega, None, ALU.mult))
                    for n in range(NCH):
                        c = slice(64 * n, 64 * n + 64)
                        last = V.tensor_tensor_scan(tmpC[:, 0, c], ones[:, 0:64], tmpC[:, 1, c], 0.0, ALU.mult, ALU.add)
                    last.then_inc(S("gc"), 1)
                    dve.wait_ge(S("ln1p"), 2)
                    dve.wait_ge(S("gc"), 1)
                    link(V.tensor_scalar(tmpC[:, 1, :], tmpG[:, 1, :], 1.0, 0.5, ALU.add, ALU.mult))
                    V.tensor_copy(rows[32:36, :], tmpC[32:36, 1, :])
                    link(V.tensor_copy(rows[64:68, :], tmpC[32:36, 1, :]))
                    V.tensor_copy(rows[0:4, :], tmpC[0:4, 0, :])
                    dve.wait_ge(S("egc"), 1)
                    V.tensor_tensor(rows[64:68, :], rows[64:68, :], tmpF[64:68, 0, :], ALU.mult)
                    V.tensor_copy(rows[96:100, :], tmpF[96:100, 1, :]).then_inc(S("rows"), 1)
                    gw = lambda k, t: par_("gconv", 6 * k + t, 6 * k + t + 1)
                    for k in range(4):
                        for t in range(6):
                            if k == 0:
                                if t % 2 == 0:
                                    dve.wait_ge(S("main_act"), main.taken(f"qkv{t // 2}"))
                                last = V.tensor_scalar(qkv[:, t, :], qkvp[:, t, 0:SEQ], gw(0, t), None, ALU.mult)
                            else:
                                last = V.scalar_tensor_tensor(qkv[:, t, :], qkvp[:, t, k:k + SEQ], gw(k, t), qkv[:, t, :], ALU.mult, ALU.add)
                        if k < 3:
                            link(last)
                    last.then_inc(S("conv"), 1)
                    xc = tmpA
                    dve.wait_ge(S("main_act"), main.taken("lx"))
                    lw = lambda k, t: par_("lconv", 2 * k + t, 2 * k + t + 1)
                    for k in range(4):
                        for t in range(2):
                            if k == 0:
                                last = V.tensor_scalar(xc[:, t, :], lxp[:, t, 0:SEQ], lw(0, t), par_("lcb", t, t + 1), ALU.mult, ALU.add)
                            else:
                                last = V.scalar_tensor_tensor(xc[:, t, :], lxp[:, t, k:k + SEQ], lw(k, t), xc[:, t, :], ALU.mult, ALU.add)
                        if k < 3:
                            link(last)
                    last.then_inc(S("lru_conv"), 1)
                    dve.wait_ge(S("conv_t"), 1)
                    V.scalar_tensor_tensor(qkv, qkvp[:, :, 3:], 1.0, qkv, ALU.add, ALU.mult).then_inc(S("silu_q"), 1)
                    dve.wait_ge(S("zt"), 1)
                    V.scalar_tensor_tensor(zz, tmpG, 1.0, zz, ALU.add, ALU.mult)
                    dve.wait_ge(S("side_act"), side.taken("li"))
                    for t in range(2):
                        last = V.tensor_scalar(tmpC[:, t, :], tmpB[:, t, :], 1.0, sp4[:, t:t + 1], ALU.add, ALU.mult)
                    last.then_inc(S("log_a"), 1)
                    dve.wait_ge(S("log_a"), 1)
                    link(V.scalar_tensor_tensor(tmpB, tmpD, 1.0, xc, ALU.add, ALU.mult))
                    dve.wait_ge(S("lru_t"), 1)
                    link(V.tensor_scalar(tmpF, tmpE, 1.0, None, ALU.add))
                    link(V.reciprocal(tmpF, tmpF))
                    V.tensor_tensor(tmpE, tmpE, tmpF, ALU.mult).then_inc(S("lru_q"), 1)
                    dve.wait_ge(S("main_act"), main.taken("ly"))
                    dve.wait_ge(S("lru_q"), 1)
                    link(V.tensor_tensor(tmpD, ly, ly, ALU.mult))
                    link(V.tensor_scalar(tmpD, tmpD, 0.044715, 1.0, ALU.mult, ALU.add))
                    V.tensor_tensor(tmpD, tmpD, ly, ALU.mult).then_inc(S("gelu_in"), 1)
                    dve.wait_ge(S("side_act"), side.taken("l2k"))
                    link(V.reciprocal(mx_sq, mx_sq))
                    V.scalar_tensor_tensor(qkv[:, 0:2, :], qkv[:, 0:2, :], 0.5 * DH ** -0.5, mx_sq[:, 0:2, :], ALU.mult, ALU.mult)
                    V.scalar_tensor_tensor(qkv[:, 2:4, :], qkv[:, 2:4, :], 0.5, mx_sq[:, 2:4, :], ALU.mult, ALU.mult).then_inc(S("k_normed"), 1)
                    dve.wait_ge(S("k_normed"), 1)
                    dve.wait_ge(S("lru_m"), 1)
                    dve.wait_ge(S("lru_a"), 1)
                    link(V.tensor_tensor(tmpB, tmpB, tmpE, ALU.mult))
                    for t in range(2):
                        last = V.tensor_tensor_scan(tmpF[:, t, :], tmpC[:, t, :], tmpB[:, t, :], 0.0, ALU.mult, ALU.add)
                    link(last)
                    dve.wait_ge(S("side"), side.ready("ktr"))
                    dve.wait_ge(S("side_act"), side.taken("rowt"))

                    def cols(r, j):
                        return rowT[:, j, 32 * r:32 * r + 4].unsqueeze(2).to_broadcast([P, 4, DH])

                    def heads(ap):
                        return ap.rearrange("p (h d) -> p h d", h=4)

                    for j in range(2):
                        ps = side.bank("ktr")[:, j * 256:(j + 1) * 256]
                        V.tensor_tensor(heads(kbe[:, j, :]), heads(ps), cols(2, j), ALU.mult)
                        last = V.tensor_tensor(heads(kdec[:, j, :]), heads(ps), cols(3, j), ALU.mult)
                    last.then_inc(S("side_dve"), 1)
                    dve.wait_ge(S("side"), side.ready("vtr"))
                    for j in range(2):
                        ps = side.bank("vtr")[:, j * 256:(j + 1) * 256]
                        last = V.scalar_tensor_tensor(heads(vb[:, j, :]), heads(ps), 0.5, cols(1, j), ALU.mult, ALU.mult)
                    last.then_inc(S("side_dve"), 1)
                    dve.wait_ge(S("gelu_t"), 1)
                    link(V.scalar_tensor_tensor(tmpD, tmpD, 1.0, ly, ALU.add, ALU.mult))
                    V.scalar_tensor_tensor(out_br[:, 2], tmpF, 0.5, tmpD, ALU.mult, ALU.mult).then_inc(S("branch2"), 1)
                    dve.wait_ge(S("side_act"), side.taken("eb"))
                    V.tensor_tensor(qdec, qkv[:, 0:2, :], egb, ALU.mult).then_inc(S("dve_q"), 1)
                    for hp in range(2):
                        ps = side.bank(f"gb{hp}")
                        dve.wait_ge(S("side"), side.ready(f"gb{hp}"))
                        for t in range(2):
                            for j in range(2):
                                o = (t * 2 + j) * P
                                h = 2 * t + hp
                                last = V.tensor_scalar(dec[:, hp, t, j, :], ps[:, o:o + P], rowT[:, j, h:h + 1], 0.0, ALU.subtract, ALU.min)
                        last.then_inc(S("side_dve"), 1)
                    tj = lambda m, hp: m[:, hp].rearrange("p t j c -> p (t j) c")
                    for hp in range(2):
                        dve.wait_ge(S("dec"), hp + 1)
                        link(V.tensor_tensor(tj(dec, hp), tj(dec, hp), over(cst_("incl"), 4), ALU.mult))
                        dve.wait_ge(S("side"), side.ready(f"kk{hp}"))
                        V.tensor_tensor(flat(low)[:, hp, :], side.bank(f"kk{hp}")[:], flat(dec)[:, hp, :], ALU.mult).then_inc(S("side_dve"), 1)
                        dve.wait_ge(S("side_dve"), side.taken(f"kk{hp}"))
                        dve.wait_ge(S("side"), side.ready(f"bb{hp}"))
                        V.tensor_tensor(flat(low)[:, hp, :], side.bank(f"bb{hp}")[:], flat(low)[:, hp, :], ALU.mult).then_inc(S("side_dve"), 1)
                    for hp in range(2):
                        dve.wait_ge(S("side"), side.ready(f"qk{hp}"))
                        V.tensor_tensor(flat(attn)[:, hp, :], side.bank(f"qk{hp}")[:], flat(dec)[:, hp, :], ALU.mult).then_inc(S("side_dve"), 1)

                    def s5_state(s):
                        ps = halves(side.bank(f"pq{s}")[:])
                        dve.wait_ge(S("side"), side.ready(f"pq{s}"))
                        if s:
                            dve.wait_ge(S("s5s"), s)
                        V.tensor_tensor(tmpA, ps, over(cosE[:, s, :], 2), ALU.mult)
                        V.tensor_tensor(tmpB, ps, over(sinE[:, s, :], 2), ALU.mult).then_inc(S("side_dve"), 1)
                        dve.wait_ge(S("side_dve"), side.taken(f"pq{s}"))
                        V.tensor_tensor(tmpA[:, 0, :], tmpA[:, 0, :], tmpB[:, 1, :], ALU.add)
                        link(V.tensor_tensor(tmpA[:, 1, :], tmpA[:, 1, :], tmpB[:, 0, :], ALU.subtract))
                        ss = (tmpC, tmpD)[s % 2]
                        if s >= 2:
                            dve.wait_ge(S("s5x"), s - 1)
                        mag = sm["mag"][:, s:s + 1].to_broadcast([P, SEQ])
                        V.tensor_tensor_scan(ss[:, 0, :], mag, tmpA[:, 0, :], 0.0, ALU.mult, ALU.add)
                        V.tensor_tensor_scan(ss[:, 1, :], mag, tmpA[:, 1, :], 0.0, ALU.mult, ALU.add).then_inc(S("s5s"), 1)

                    dve.wait_ge(S("tables"), 2)
                    dve.wait_ge(S("xy_init"), 1)
                    for lv in range(LEVELS):
                        for hp in range(2):
                            for unit, m in ((f"xt{hp}_{lv}", mx), (f"ty{hp}_{lv}", my)):
                                dve.wait_ge(S("side"), side.ready(unit))
                                V.tensor_tensor(flat(m)[:, hp, :], flat(m)[:, hp, :], side.bank(unit)[:], ALU.subtract).then_inc(S("side_dve"), 1)
                        if lv < 4:
                            s5_state(2 * lv)
                            s5_state(2 * lv + 1)
                    dve.wait_ge(S("s5s"), NST)
                    for i, (unit, src) in enumerate((("rotq", rq), ("rotk", rk))):
                        dve.wait_ge(S("side"), side.ready(unit))
                        if i:
                            dve.wait_ge(S("rotated"), i)
                        V.tensor_tensor(tmpA, halves(side.bank(unit)[:]), over(ropes, 2), ALU.mult).then_inc(S("side_dve"), 1)
                        link(V.tensor_tensor(src, src, over(ropec, 2), ALU.mult))
                        dve.wait_ge(S("side_dve"), side.taken(unit))
                        V.tensor_tensor(src, src, tmpA, ALU.add).then_inc(S("rotated"), 1)

                    def state_up(n):
                        ps = side.bank(f"su{n}")
                        dve.wait_ge(S("side"), side.ready(f"su{n}"))
                        for t in range(2):
                            for hp in range(2):
                                r, c = slice(64 * hp, 64 * hp + 64), slice(64 * hp, 64 * hp + 64)
                                pc = slice(t * P + 64 * hp, t * P + 64 * hp + 64)
                                if n == 0:
                                    last = V.tensor_copy(state[r, t, c], ps[r, pc])
                                else:
                                    last = V.scalar_tensor_tensor(state[r, t, c], state[r, t, c], egb[r, t, 64 * n + 63:64 * n + 64], ps[r, pc],
                                                                  ALU.mult, ALU.add)
                        last.then_inc(S("side_dve"), 1)

                    def values(n):
                        r, j = slice(64 * (n % 2), 64 * (n % 2) + 64), n // 2
                        dve.wait_ge(S("side"), side.ready(f"ws{n}"))
                        V.tensor_tensor(uu[r, j, :], uu[r, j, :], side.bank(f"ws{n}")[r, 0:256], ALU.subtract).then_inc(S("side_dve"), 1)

                    def masked(h):
                        dve.wait_ge(S("side"), side.ready(f"sc{h}"))
                        V.tensor_tensor(scm[:, h, :], side.bank(f"sc{h}")[:, 0:384], cst_("rmask", 384 * h, 384 * h + 384), ALU.mult).then_inc(S("side_dve"), 1)

                    state_up(0)
                    masked(0)
                    masked(1)
                    values(1)
                    state_up(1)
                    masked(2)
                    masked(3)
                    values(2)
                    state_up(2)
                    values(3)
                    dve.wait_ge(S("s5y"), 8)
                    for t in range(2):
                        last = V.scalar_tensor_tensor(su[:, t, :], su[:, t, :], par_("s5d", t, t + 1), ybank[:, t * SEQ:(t + 1) * SEQ], ALU.mult, ALU.add)
                    link(last)
                    link(V.tensor_tensor(tmpE, su, su, ALU.mult))
                    link(V.tensor_scalar(tmpE, tmpE, 0.044715, 1.0, ALU.mult, ALU.add))
                    V.tensor_tensor(tmpE, tmpE, su, ALU.mult).then_inc(S("s5gin"), 1)
                    dve.wait_ge(S("rgt"), 1)
                    link(V.scalar_tensor_tensor(rg, tmpA, 1.0, rg, ALU.add, ALU.mult))
                    dve.wait_ge(S("side"), side.ready("rm"))
                    V.tensor_tensor(tmpB, tmpB, halves(side.bank("rm")[:]), ALU.subtract).then_inc(S("side_dve"), 1)
                    dve.wait_ge(S("side_act"), side.taken("oi3"))
                    for j in range(2):
                        dve.wait_ge(S("side"), side.ready(f"oa{j}"))
                        ps = halves(side.bank(f"oa{j}")[:, 0:256])
                        if j == 0:
                            V.tensor_copy(go[:, :, 0:64], ps[:, :, 0:64])
                            V.tensor_tensor(go[:, :, 64:P], go[:, :, 64:P], ps[:, :, 64:P], ALU.add).then_inc(S("side_dve"), 1)
                        else:
                            V.tensor_tensor(go[:, :, P:SEQ], go[:, :, P:SEQ], ps, ALU.add).then_inc(S("side_dve"), 1)
                    dve.wait_ge(S("side_act"), side.taken("rv2"))
                    link(V.reciprocal(tmpC, tmpC))
                    link(V.tensor_tensor(tmpB, tmpB, tmpC, ALU.mult))
                    for t in range(2):
                        last = V.scalar_tensor_tensor(out_br[:, 3, t, :], tmpB[:, t, :], rnh[:, t:t + 1], rg[:, t, :], ALU.mult, ALU.mult)
                    last.then_inc(S("branch3"), 1)
                    dve.wait_ge(S("side_act"), side.taken("gs"))
                    link(V.reciprocal(tmpD, tmpD))
                    link(V.tensor_tensor(go, go, tmpD, ALU.mult))
                    V.scalar_tensor_tensor(out_br[:, 0], go, gnh, zz, ALU.mult, ALU.mult).then_inc(S("branch0"), 1)
                    dve.wait_ge(S("s5gt"), 1)
                    V.scalar_tensor_tensor(tmpE, tmpE, 1.0, su, ALU.add, ALU.mult).then_inc(S("s5g"), 1)
                    dve.wait_ge(S("side_act"), side.taken("glu"))
                    link(V.scalar_tensor_tensor(tmpF, tmpF, 1.0, tmpE, ALU.add, ALU.mult))
                    V.tensor_scalar(out_br[:, 1], tmpF, 0.25, None, ALU.mult).then_inc(S("branch1"), 1)
                    gbr = gates.rearrange("p (n m) t -> p n m t", n=NB)
                    dve.wait_ge(S("main_act"), main.taken("g15"))
                    for m in range(KD):
                        for ab, t in enumerate((tmpA, tmpB)):
                            unit = f"mg{m}{'ab'[ab]}"
                            dve.wait_ge(S("main"), main.ready(unit))
                            V.scalar_tensor_tensor(t, gbr[:, 2 * ab:2 * ab + 2, m, :], 1.0, halves(main.bank(unit)[:]), ALU.add, ALU.mult).then_inc(S("main_dve"), 1)
                        dve.wait_ge(S("main_dve"), main.taken(f"mg{m}b"))
                        link(V.tensor_tensor(tmpA, tmpA, tmpB, ALU.add))
                        V.tensor_tensor(xn[:, m, :], tmpA[:, 0, :], tmpA[:, 1, :], ALU.add).then_inc(S("merged"), 1)
                        dve.wait_ge(S("merged"), m + 1)
                    down([f"wo{i}" for i in range(4)], 0.5)
                    normed("ssq2", 2, "n2")
                    up(2, range(MF))
                    down([f"dn2_{j}" for j in range(4)], 0.5)

            handles = [per_layer[n].num for n in per_layer]
            assert sorted(handles) == list(range(min(handles), max(handles) + 1))
            nc.all_engine_barrier(sems_to_clear=range(min(handles), max(handles) + 1))

        with nc.Block() as block:
            @block.scalar
            def _(act):
                nc.scalar.activation(xn, x, ACT.Square).then_inc(once["fin_act"], 1)
                act.wait_ge(once["fin_pe"], 1)
                nc.scalar.activation(tmpA[:, 0, :], psum[0][:, 0:SEQ], ACT.Sqrt, bias=eps_col, scale=1.0 / DM).then_inc(once["fin_act"], 1)

            @block.tensor
            def _(pe):
                pe.wait_ge(once["fin_act"], 1)
                for k in range(KD):
                    last = nc.tensor.matmul(psum[0][:, 0:SEQ], ones, xn[:, k, :], start=(k == 0), stop=(k == KD - 1))
                last.then_inc(once["fin_pe"], 1)

            @block.vector
            def _(dve):
                dve.wait_ge(once["fin_act"], 2)
                nc.vector.reciprocal(tmpA[:, 1, :], tmpA[:, 0, :]).then_inc(once["fin_dve"], 1)
                dve.wait_ge(once["fin_dve"], 1)
                for k in range(KD):
                    nc.vector.scalar_tensor_tensor(xn[:, k, :], x[:, k, :], cst_("fnorm", k, k + 1), tmpA[:, 1, :], ALU.mult, ALU.mult).then_inc(once["fin_dve"], 1)

            @block.sync
            def _(sp):
                for j in range(2):
                    sp.wait_ge(once["fin_dve"], 1 + 4 * (j + 1))
                    sp.dma_start(y_out[:, 4 * j:4 * j + 4, :], xn[:, 4 * j:4 * j + 4, :]).then_inc(once["stored"], 16)
                sp.wait_ge(once["stored"], 32)


def _weight_stream(a, l):
    def tiles(w):
        k, m = w.shape
        return w.reshape(k // P, P, m // P, P).transpose(1, 2, 0, 3)

    out = {}
    for f in (1, 2):
        g, u, d = (tiles(a[f"ffn{f}_{n}"][l]) for n in ("w_gate", "w_up", "w_down"))
        for m in range(MF):
            out[f"gu{f}_{m}"] = np.stack([g[:, m], u[:, m]], axis=1)
        for i in range(16):
            out[f"dn{f}_{i}"] = d[:, i // 2, 11 * (i % 2):11 * (i % 2) + 11]
    w = a["w_in"][l]
    offs = np.cumsum([0, 768, 256, 4, 4, 256, 256, 256, 256, 256, 256, 256, 4096])
    col = {n: w[:, offs[i]:offs[i + 1]] for i, n in enumerate(["qkv", "z", "b", "a", "su", "lx", "ly", "rq", "rk", "rv", "rg", "g"])}
    ba = np.zeros((DM, P), np.float32)
    for r in (0, 64, 96):
        ba[:, r:r + 4] = col["a"]
    ba[:, 32:36] = col["b"]
    out["ba"] = tiles(ba)
    for i in range(3):
        out[f"qkv{i}"] = tiles(col["qkv"][:, 256 * i:256 * i + 256])
    for n in ("z", "su", "lx", "ly", "rq", "rk", "rg"):
        out[n] = tiles(col[n])
    out["rv"] = col["rv"].reshape(KD, P, 256).transpose(1, 0, 2)
    for i in range(16):
        out[f"g{i}"] = tiles(col["g"][:, 256 * i:256 * i + 256])
    wb = a["w_branch"][l].reshape(NB, 2, P, KD, P).transpose(2, 3, 0, 1, 4)
    wo = tiles(a["w_out"][l])
    for i in range(4):
        out[f"wb{i}"] = wb[:, 2 * i:2 * i + 2]
        out[f"wo{i}"] = wo[:, 2 * i:2 * i + 2]
    return np.concatenate([np.ascontiguousarray(out[n]).reshape(-1) for n, _ in CHUNKS])


def _params(a, l):
    p = np.zeros((P, NPAR), np.float32)

    def put(name, v):
        lo, hi = PCOLS[name]
        p[:, lo:hi] = v.reshape(P, hi - lo)

    feat = lambda v: v.reshape(-1, P).T
    put("n1", feat(a["ffn1_norm"][l]))
    put("nm", feat(a["mix_norm"][l]))
    put("n2", feat(a["ffn2_norm"][l]))
    put("gconv", feat(a["gdn_conv_w"][l]))
    for name, v in (("dtb", a["gdn_dt_bias"][l]), ("alog", a["gdn_a_log"][l])):
        for r in (0, 64, 96):
            p[r:r + 4, PCOLS[name][0]] = v
    put("gnorm", np.concatenate([a["gdn_norm_w"][l]] * 2))
    put("lre", feat(a["s5_lambda_re"][l]))
    put("lim", feat(a["s5_lambda_im"][l]))
    put("ldt", feat(np.repeat(a["s5_log_dt"][l], 64)))
    put("s5d", feat(a["s5_d"][l]))
    put("bglu", feat(a["s5_b_glu"][l]))
    put("lconv", feat(a["lru_conv_w"][l]))
    put("lcb", feat(a["lru_conv_b"][l]))
    put("lba", feat(a["lru_b_a"][l]))
    put("lbi", feat(a["lru_b_i"][l]))
    put("lam", feat(a["lru_lambda"][l]))
    put("rnorm", feat(a["ret_norm_w"][l]))
    for name, b in (("sbr", a["s5_b_re"][l]), ("sbi", a["s5_b_im"][l])):
        w = np.zeros((P, NST, P), np.float32)
        for g in range(16):
            w[16 * (g % 8):16 * (g % 8) + 16, g // 2, 64 * (g % 2):64 * (g % 2) + 64] = b[g].T
        put(name, w)
    for name, c in (("scr", a["s5_c_re"][l]), ("sci", a["s5_c_im"][l])):
        w = np.zeros((P, NST, 32), np.float32)
        for g in range(16):
            w[64 * (g % 2):64 * (g % 2) + 64, g // 2, 16 * (g % 2):16 * (g % 2) + 16] = c[g].T
        put(name, w)
    put("wglu", a["s5_w_glu"][l].reshape(2, P, 256).transpose(1, 0, 2))
    for name, b in (("wa", a["lru_w_a"][l]), ("wi", a["lru_w_i"][l])):
        w = np.zeros((P, 2, P), np.float32)
        for n in range(4):
            r = 64 * (n % 2)
            w[r:r + 64, n // 2, r:r + 64] = b[n]
        put(name, w)
    return p


def _constants(fnorm):
    c = np.zeros((P, NCST), np.float32)

    def put(name, v):
        lo, hi = CCOLS[name]
        c[:, lo:hi] = np.asarray(v, np.float64).reshape(P, hi - lo)

    i = np.arange(P)
    put("ident", np.eye(P))
    put("ones", np.ones((P, P)))
    put("bo", (i[:, None] // 64 == i[None] // 64) / 64.0)
    put("incl", (i[:, None] // 64 == i[None] // 64) & (i[:, None] <= i[None]))
    lev = []
    for s in (1, 2, 4, 8, 16, 32):
        m, cc = i[:, None], i[None]
        lev.append((m // (2 * s) == cc // (2 * s)) & (m % (2 * s) < s) & (cc % (2 * s) >= s))
    put("lev", np.stack(lev, axis=1))
    perm = np.zeros((P, P))
    for r in range(P):
        if r % 64 < 32:
            perm[r + 32, r] = -1.0
        else:
            perm[r - 32, r] = 1.0
    put("perm", perm)
    selg, selb, selp = np.zeros((P, 4, P)), np.zeros((P, 4, P)), np.zeros((P, 2, P))
    for h in range(4):
        selg[h, h] = 1.0
        selb[32 + h, h] = 1.0
        selp[h, h // 2, 64 * (h % 2):64 * (h % 2) + 64] = 1.0
    put("selg", selg)
    put("selb", selb)
    put("selp", selp)
    rmask = np.zeros((P, 4, 384))
    for h in range(4):
        lg = np.log1p(-np.exp2(-5.0 - h))
        m, q = i[:, None], np.arange(SEQ)[None]
        full = np.where(q >= m, np.exp(np.maximum(q - m, 0) * lg), 0.0) * DH ** -0.5
        rmask[:, h, :SEQ] = full
        rmask[:, h, SEQ:] = full[:, :P]
    put("rmask", rmask)
    put("tok", np.broadcast_to(np.arange(SEQ), (P, SEQ)))
    put("freq", (10000.0 ** (-(i % 32) / 32.0)))
    lo, hi = CCOLS["fnorm"]
    c[:, lo:hi] = fnorm.reshape(KD, P).T
    return c


def kernel(**inputs):
    import concourse.bacc as _bacc
    from concourse import mybir as _mybir
    from concourse.bass_utils import run_bass_kernel_spmd as _run

    a = {k: np.asarray(v) for k, v in inputs.items()}
    arrays = {
        "weights": np.stack([_weight_stream(a, l) for l in range(DEPTH)]),
        "params": np.stack([_params(a, l) for l in range(DEPTH)]),
        "consts": _constants(a["final_norm"]),
        "positions": np.ascontiguousarray(np.broadcast_to(a["positions"].reshape(1, SEQ), (P, SEQ))),
        "x_in": np.ascontiguousarray(a["x"].reshape(SEQ, KD, P).transpose(2, 1, 0)),
    }
    nc = _bacc.Bacc("TRN2", target_bir_lowering=False, num_devices=1)
    args = [nc.dram_tensor(n, v.shape, _mybir.dt.from_np(v.dtype), kind="ExternalInput").ap() for n, v in arrays.items()]
    args.append(nc.dram_tensor("y_out", (P, KD, SEQ), F32, kind="ExternalOutput").ap())
    trunk(nc, *args)
    r = _run(nc, [arrays], core_ids=[0])
    return r.results[0]["y_out"].transpose(2, 1, 0).reshape(1, SEQ, DM)
```

```python
import math

import numpy as np
import concourse.bass as bass
from concourse import mybir
from contextlib import ExitStack

F32 = mybir.dt.float32
F32R = mybir.dt.float32r
ALU = mybir.AluOpType
ACT = mybir.ActivationFunctionType

P = 128
SEQ, DM, DFF, DEPTH = 256, 1024, 2816, 2
KD = DM // P
MF = DFF // P
NB = 4
NH, DH = 4, 64
NCH = SEQ // 64
NST = 8
EPS = 1e-6
RAW_SLOTS = 3
SLOTS = 4
SLOT = 1024
LEVELS = 6
GELU_C = math.sqrt(2.0 / math.pi)
TWO_PI = 2.0 * math.pi
ROUND = 12582912.0
GRID = 384.0
PI_C = [float(np.float32(x)) for x in (6.28125, 0.0019350051879882812, 3.0199159819567e-07)]
PI_SAFE = 3.1415925
SIN_SCALE = 6.283185

PCOLS = {}
_at = 0
for _name, _n in [("n1", 8), ("nm", 8), ("n2", 8), ("gconv", 24), ("dtb", 1), ("alog", 1), ("gnorm", 1),
                  ("lre", 8), ("lim", 8), ("ldt", 8), ("s5d", 2), ("bglu", 2), ("lconv", 8), ("lcb", 2),
                  ("lba", 2), ("lbi", 2), ("lam", 2), ("rnorm", 2), ("sbr", 256), ("sbi", 256),
                  ("scr", 256), ("sci", 256), ("wglu", 512), ("wa", 256), ("wi", 256)]:
    PCOLS[_name] = (_at, _at + _n)
    _at += _n
NPAR = _at

CCOLS = {}
_at = 0
for _name, _n in [("ident", 128), ("one", 1), ("bo", 128), ("incl", 128), ("lev", 128 * LEVELS), ("perm", 128),
                  ("rmask", 4 * 256),
                  ("freq", 1), ("fnorm", 8)]:
    CCOLS[_name] = (_at, _at + _n)
    _at += _n
NCST = _at

PROJ = ["ba", "qkv0", "qkv1", "qkv2", "lx", "ly", "su", "z", "rq", "rk", "rg", "rv"]
SLAB = 53152

DOWN_K = [(0, 8), (8, 15), (15, 22)]


def _pieces():
    out = []

    def pair(name):
        out.extend([(f"{name}.0", 8, None), (f"{name}.1", 8, name)])

    def ffn(f):
        for m in range(MF):
            pair(f"gu{f}_{m}")
        for j in range(4):
            for o in range(2):
                for n, (a, b) in enumerate(DOWN_K):
                    out.append((f"dn{f}_{j}.{3 * o + n}", b - a, f"dn{f}_{j}" if (o, n) == (1, 2) else None))

    ffn(1)
    for name in PROJ:
        if name == "ba":
            out.append(("ba.0", 8, "ba"))
        else:
            pair(name)
    for i in range(16):
        pair(f"g{i}")
    for m in range(KD):
        out.append((f"mg{m}.0", 8, f"mg{m}b"))
    for i in range(4):
        pair(f"wo{i}")
    ffn(2)
    return out


PIECES = _pieces()
PIECE_INDEX = {name: i for i, (name, _, _) in enumerate(PIECES)}
UNIT_PIECES = {}
for _i, (_name, _, _) in enumerate(PIECES):
    UNIT_PIECES.setdefault(_name.split(".")[0], []).append(_i)
UNIT_ORDER = list(UNIT_PIECES)
PIECE_AT = {}
_at = 0
for _name, _n, _ in PIECES:
    PIECE_AT[_name] = _at
    _at += P * P * _n
LAYER_FLOATS = _at

MAIN = ([("ssq1", "act")] + [(f"gu1_{m}", "dve") for m in range(MF)] + [(f"dn1_{j}", "dve") for j in range(4)]
        + [("ssqm", "act")] + [(n, "act") for n in PROJ] + [(f"g{i}", "act") for i in range(16)]
        + [(f"mg{m}{ab}", "dve") for m in range(KD) for ab in "ab"] + [(f"wo{i}", "dve") for i in range(4)]
        + [("ssq2", "act")] + [(f"gu2_{m}", "dve") for m in range(MF)] + [(f"dn2_{j}", "dve") for j in range(4)])
LEVEL_UNITS = [()] + [("xt", "ty")] * (LEVELS - 2) + [("ty",)]
SIDE = ([("lr", "act"), ("li", "act"), ("l2q", "act"), ("l2k", "act"), ("rowt", "act"), ("ktr", "dve"), ("vtr", "dve"),
         ("eb", "act")]
        + [(n, "dve") for n in ("gb0", "gb1", "kk0", "bb0", "kk1", "bb1", "qk0", "qk1")]
        + [u for lv in range(LEVELS) for u in
           ([(f"t0_{lv}", "act"), (f"t1_{lv}", "act")]
            + [(f"{n}{hp}_{lv}", "dve") for hp in range(2) for n in LEVEL_UNITS[lv]]
            + [(f"pq{s}", "dve") for s in ([2 * lv, 2 * lv + 1] if lv < 4 else [])])]
        + [("rotq", "dve"), ("rotk", "dve"), ("u", "act"), ("w", "act"),
           ("su0", "dve"), ("sc0", "dve"), ("sc1", "dve"),
           ("ws1", "dve"), ("oi1", "act"), ("su1", "dve"), ("sc2", "dve"), ("sc3", "dve"),
           ("ws2", "dve"), ("oi2", "act"), ("su2", "dve"), ("ro", "act"),
           ("ws3", "dve"), ("oi3", "act"), ("rm", "dve"), ("oa0", "dve"), ("oa1", "dve"),
           ("rv2", "act"), ("gs", "act"), ("glu", "act")])


class Units:

    def __init__(self, order, banks):
        self.order, self.banks = order, banks
        self.index = {name: i for i, (name, _) in enumerate(order)}

    def bank(self, name):
        return self.banks[self.index[name] % len(self.banks)]

    def ready(self, name):
        return self.index[name] + 1

    def previous(self, name):
        i = self.index[name] - len(self.banks)
        return self.order[i] if i >= 0 else None

    def taken(self, name):
        i = self.index[name]
        return sum(1 for _, e in self.order[:i + 1] if e == self.order[i][1])


def trunk(nc, weights, params, consts, positions, x_in, y_out):
    ctx = ExitStack()
    with ctx:
        base = -(-nc.sbuf_base // 32) * 32
        ctx.enter_context(nc.sbuf_tensor("slab", [P, SLAB + 8], F32))
        place = {"": 0}

        def sb(name, cols, dt=F32, over=None, skip=0):
            if over is None:
                place[name] = place[""]
                place[""] += -(-cols // 8) * 8
                assert place[""] <= SLAB, place[""]
            else:
                place[name] = place[over] + skip
            return nc.alloc_sbuf_tensor_at(name, [P, cols], dt, offset=base + 4 * place[name])

        def two(name, n=2, t=SEQ, dt=F32, over=None, skip=0):
            return sb(name, n * t, dt, over, skip)[:].rearrange("p (k t) -> p k t", k=n)

        x = sb("x", KD * SEQ)[:].rearrange("p (k t) -> p k t", k=KD)
        xh, xl = two("xh", KD, dt=F32R), two("xl", KD, dt=F32R)
        raw = sb("raw", RAW_SLOTS * SLOT)
        whi, wlo = sb("whi", SLOTS * SLOT, F32R), sb("wlo", SLOTS * SLOT, F32R)
        cst = sb("cst", NCST)
        par = sb("par", NPAR)
        wide = sb("wide", 32 * SEQ)[:].rearrange("p (k t) -> p k t", k=32)
        hh = two("hh", MF, dt=F32R, over="wide")
        gates = wide
        griffin = wide[:, 30:32, :]
        cosE = wide[:, 22:30, :]
        sinE = sb("sinE", 8 * SEQ)[:].rearrange("p (k t) -> p k t", k=8)

        qkvp = two("qkvp", 6, SEQ + 3)
        qkv = two("qkv", 6)
        zz, su, ly = two("zz"), two("su"), two("ly")
        lxp = two("lxp", 2, SEQ + 3)
        ret = two("ret", 8)
        rq, rk, rg, rv = (ret[:, 2 * i:2 * i + 2, :] for i in range(4))
        flat8 = two("flat8", 8)
        brh = sb("brh", 8 * SEQ, F32R, over="flat8")[:].rearrange("p (n k t) -> p n k t", n=NB, k=2)
        big = sb("big", 24 * SEQ)
        hl = two("hl", MF, dt=F32R, over="big")

        def mats(i):
            return big[:, i * 8 * P:(i + 1) * 8 * P].rearrange("p (h t j c) -> p h t j c", h=2, t=2, j=2)

        dec, attn, low, my, mx, mt = (mats(i) for i in range(6))
        lowc = dec
        flat = lambda m: m.rearrange("p h t j c -> p h (t j c)")
        kbe, kdec, vb = (qkvp[:, 2 * i:2 * i + 2, 3:] for i in range(3))
        uu = big[:, 22 * SEQ:24 * SEQ].rearrange("p (k t) -> p k t", k=2)
        wT = big[:, 8 * SEQ:10 * SEQ].rearrange("p (k t) -> p k t", k=2)
        state = big[:, 10 * SEQ:11 * SEQ].rearrange("p (t c) -> p t c", t=2)
        egb, qdec = two("egb"), two("qdec")
        rows, rowT = two("rows", 1)[:, 0, :], two("rowT", 2, P)
        tmpA, tmpB, tmpC, tmpD, tmpE, tmpF = (two("tmp" + c) for c in "ABCDEF")
        brl = [two("brl0", dt=F32R, over="qkv"), two("brl1", dt=F32R, over="qkv", skip=2 * SEQ),
               two("brl2", dt=F32R, over="egb"), two("brl3", dt=F32R, over="qkv", skip=4 * SEQ)]
        small = sb("small", 176)
        ropec, ropes = two("ropec", 1)[:, 0, :], two("ropes", 1)[:, 0, :]
        mx_sq = mx.rearrange("p h t j c -> p (h t j c)").rearrange("p (k t) -> p k t", k=4)
        turns_a, turns_b = flat8, ret
        squared = flat8
        s5n = lxp[:, :, 3:]
        go = ly
        scm = big[:, 16 * SEQ:16 * SEQ + 4 * 384].rearrange("p (h c) -> p h c", h=4)

        psum = [ctx.enter_context(nc.psum_tensor(f"bank{i}", [P, 512], F32)) for i in range(8)]
        main = Units(MAIN, psum[0:4])
        side = Units(SIDE, psum[4:7])
        ybank = psum[7]

        once = {n: nc.alloc_semaphore(n) for n in ("loads", "pre_dve", "pre_act", "pre_pool", "fin_dve", "fin_act",
                                                   "fin_pe", "stored")}
        per_layer = {}

        def S(name):
            if name not in per_layer:
                per_layer[name] = nc.alloc_semaphore(name)
            return per_layer[name]

        def par_(name, a=0, b=None):
            lo, hi = PCOLS[name]
            return par[:, lo + a:(lo + b if b is not None else hi)]

        def cst_(name, a=0, b=None):
            lo, hi = CCOLS[name]
            return cst[:, lo + a:(lo + b if b is not None else hi)]

        def halves(ap, n=2):
            return ap.rearrange("p (k t) -> p k t", k=n)

        def over(ap, n):
            return ap.unsqueeze(1).to_broadcast([P, n, ap.shape[-1]])

        ident, bo = cst_("ident"), cst_("bo")
        ones = cst_("one").to_broadcast([P, P])
        sm = {}
        for i, n in enumerate(["dt", "lrdt", "th", "mag", "n1", "r1", "r2", "sn", "cs", "ai", "nr", "den", "cre",
                               "cim", "ph", "phl", "t1", "t2"]):
            sm[n] = small[:, 8 * i:8 * i + 8]
        eps_col = small[:, 150:151]
        nega = small[:, 151:152]
        gnh = small[:, 152:153]
        rnh = small[:, 154:156]
        hba, hbi, hbg = small[:, 156:158], small[:, 158:160], small[:, 160:162]
        sp4, ly_, ls_, ls2, lq = (small[:, 162 + 2 * i:164 + 2 * i] for i in range(5))

        def piece_used(i):
            if PIECES[i][2]:
                return S("main"), main.ready(PIECES[i][2])
            return S("part"), sum(1 for _, _, unit in PIECES[:i + 1] if unit is None)

        def slot(ring, i):
            s0 = (i % (RAW_SLOTS if ring is raw else SLOTS)) * SLOT
            return ring[:, s0:s0 + P * PIECES[i][1]]

        def r32(ap):
            return ap.bitcast(F32)

        with nc.Block() as block:
            @block.sync
            def _(sp):
                sp.dma_start(cst[:], consts).then_inc(once["loads"], 16)
                sp.dma_start(ropec.bitcast(mybir.dt.int32), positions).then_inc(once["loads"], 16)
                sp.dma_start(x, x_in).then_inc(once["loads"], 16)

            @block.gpsimd
            def _(pool):
                nc.gpsimd.memset(qkvp[:, :, 0:3], 0.0)
                nc.gpsimd.memset(lxp[:, :, 0:3], 0.0)
                nc.gpsimd.memset(rows, 0.0)
                nc.gpsimd.memset(eps_col, EPS).then_inc(once["pre_pool"], 1)

            @block.vector
            def _(dve):
                n = [0]

                def link(ins):
                    n[0] += 1
                    ins.then_inc(once["pre_dve"], 1)
                    dve.wait_ge(once["pre_dve"], n[0])

                ang, t, r = tmpA[:, 0, :], tmpA[:, 1, :], tmpB[:, 0, :]
                dve.wait_ge(once["loads"], 48)
                link(nc.vector.tensor_copy(ang, ropec.bitcast(mybir.dt.int32)))
                link(nc.vector.tensor_scalar(ang, ang, cst_("freq"), None, ALU.mult))
                for out, quarter in ((tmpC[:, 0, :], 0.0), (tmpC[:, 1, :], 0.25)):
                    link(nc.vector.tensor_scalar(t, ang, 1.0 / TWO_PI, quarter, ALU.mult, ALU.add))
                    link(nc.vector.tensor_scalar(t, t, ROUND, -ROUND, ALU.add, ALU.add))
                    link(nc.vector.scalar_tensor_tensor(r, t, -PI_C[0], ang, ALU.mult, ALU.add))
                    link(nc.vector.scalar_tensor_tensor(r, t, -PI_C[1], r, ALU.mult, ALU.add))
                    link(nc.vector.scalar_tensor_tensor(r, t, -PI_C[2], r, ALU.mult, ALU.add))
                    link(nc.vector.tensor_scalar(r, r, quarter * TWO_PI, PI_SAFE, ALU.add, ALU.min))
                    link(nc.vector.tensor_scalar(out, r, -PI_SAFE, None, ALU.max))

            @block.scalar
            def _(act):
                act.wait_ge(once["pre_dve"], 2 + 2 * 7)
                nc.scalar.activation(ropes, tmpC[:, 0, :], ACT.Sin)
                nc.scalar.activation(ropec, tmpC[:, 1, :], ACT.Sin).then_inc(once["pre_act"], 1)

        with nc.Fori(0, DEPTH) as layer:
            with nc.Block() as block:
                @block.sync
                def _(sp):
                    sp.dma_start(par[:], params[bass.ds(layer, 1), :, :].rearrange("a p n -> (a p) n")).then_inc(S("par"), 16)
                    for i, (name, n, _) in enumerate(PIECES):
                        if i >= RAW_SLOTS:
                            sp.wait_ge(S("low"), i - RAW_SLOTS + 1)
                        at = PIECE_AT[name]
                        src = weights[bass.ds(layer, 1), at:at + P * P * n].rearrange("a (p n) -> (a p) n", p=P)
                        sp.dma_start(slot(raw, i), src).then_inc(S(f"raw{i % RAW_SLOTS}"), 16)

                @block.tensor
                def _(pe):
                    mm = nc.tensor.matmul

                    def piece(name):
                        i = PIECE_INDEX[name]
                        pe.wait_ge(S("low"), i + 1)
                        return [slot(ring, i).rearrange("p (k m) -> p k m", m=P) for ring in (whi, wlo)]

                    def product(out, w, a, start, stop):
                        mm(out, w[0], a[0], start=start, stop=False)
                        mm(out, w[0], a[1], start=False, stop=False)
                        return mm(out, w[1], a[0], start=False, stop=stop)

                    def main_bank(name):
                        if main.previous(name):
                            who = main.previous(name)
                            pe.wait_ge(S(f"main_{who[1]}"), main.taken(who[0]))
                        return main.bank(name)

                    def side_bank(name):
                        if side.previous(name):
                            who = side.previous(name)
                            pe.wait_ge(S(f"side_{who[1]}"), side.taken(who[0]))
                        return side.bank(name)

                    def ssq(unit, which):
                        ps = main_bank(unit)
                        for k in range(KD):
                            if k % 2 == 0:
                                pe.wait_ge(S("squares"), which * 4 + k // 2 + 1)
                            last = mm(ps[:, 0:SEQ], ones, squared[:, k, :], start=(k == 0), stop=(k == KD - 1))
                        last.then_inc(S("main"), 1)

                    def pair(unit, normed=None, merged=False):
                        ps = main_bank(unit)
                        for o in range(len(UNIT_PIECES[unit])):
                            wh, wl = piece(f"{unit}.{o}")
                            for k in range(KD):
                                if normed is not None and o == 0:
                                    pe.wait_ge(S("normed"), normed * KD + k + 1)
                                last = product(ps[:, o * SEQ:(o + 1) * SEQ], (wh[:, k, :], wl[:, k, :]), (xh[:, k, :], xl[:, k, :]),
                                               k == 0, k == KD - 1)
                            if o == 0 and unit != "ba":
                                last.then_inc(S("part"), 1)
                        last.then_inc(S("main"), 1)

                    def ffn(f, which):
                        for m in range(MF):
                            pair(f"gu{f}_{m}", which if m == 0 else None)
                        for j in range(4):
                            unit = f"dn{f}_{j}"
                            ps = main_bank(unit)
                            for o in range(2):
                                for n, (k0, k1) in enumerate(DOWN_K):
                                    wh, wl = piece(f"{unit}.{3 * o + n}")
                                    for m in range(k0, k1):
                                        if j == 0 and o == 0:
                                            pe.wait_ge(S("hidden"), MF * (f - 1) + m + 1)
                                        last = product(ps[:, o * SEQ:(o + 1) * SEQ], (wh[:, m - k0, :], wl[:, m - k0, :]),
                                                       (hh[:, m, :], hl[:, m, :]), m == 0, m == MF - 1)
                                    if (o, n) != (1, 2):
                                        last.then_inc(S("part"), 1)
                            last.then_inc(S("main"), 1)

                    ssq("ssq1", 0)
                    ffn(1, 0)
                    ssq("ssqm", 1)
                    pair("ba", normed=1)
                    for unit in PROJ[1:11]:
                        pair(unit)
                    ps = main_bank("rv")
                    for o in range(2):
                        wh, wl = piece(f"rv.{o}")
                        for j in range(2):
                            c, q = slice(j * P, (j + 1) * P), j * SEQ + o * P
                            for k in range(KD):
                                last = product(ps[:, q:q + P], (xh[:, k, c], xl[:, k, c]), (wh[:, k, :], wl[:, k, :]), k == 0, k == KD - 1)
                        last.then_inc(S("main" if o else "part"), 1)

                    def gate(i):
                        pair(f"g{i}")

                    pe.wait_ge(S("par"), 16)
                    pe.wait_ge(S("lru_conv"), 1)
                    xc = tmpA
                    for unit, wname in (("lr", "wa"), ("li", "wi")):
                        ps = side_bank(unit)
                        for t in range(2):
                            last = mm(ps[:, t * SEQ:(t + 1) * SEQ], par_(wname, t * P, (t + 1) * P), xc[:, t, :], start=True, stop=True)
                        last.then_inc(S("side"), 1)
                    gate(0)
                    for unit, q0, ev in (("l2q", 0, 1), ("l2k", 2, 2)):
                        pe.wait_ge(S("qk_sq"), ev)
                        ps = side_bank(unit)
                        for t in range(2):
                            last = mm(ps[:, t * SEQ:(t + 1) * SEQ], bo, mx_sq[:, q0 + t, :], start=True, stop=True)
                        last.then_inc(S("side"), 1)
                    gate(1)
                    pe.wait_ge(S("rows"), 1)
                    ps = side_bank("rowt")
                    for j in range(2):
                        last = nc.tensor.transpose(ps[:, j * P:(j + 1) * P], rows[:, j * P:(j + 1) * P], ident)
                    last.then_inc(S("side"), 1)
                    pe.wait_ge(S("k_normed"), 1)
                    for unit, q0 in (("ktr", 2), ("vtr", 4)):
                        ps = side_bank(unit)
                        for j in range(2):
                            for t in range(2):
                                last = nc.tensor.transpose(ps[:, j * 256 + t * P:j * 256 + (t + 1) * P], qkv[:, q0 + t, j * P:(j + 1) * P], ident)
                        last.then_inc(S("side"), 1)
                    ps = side_bank("eb")
                    for t in range(2):
                        for hp in range(2):
                            h = 2 * t + hp
                            last = mm(ps[64 * hp:64 * hp + 64, t * SEQ:(t + 1) * SEQ], ident[:, h:h + 1].to_broadcast([P, 64]), rows, start=True, stop=True)
                    last.then_inc(S("side"), 1)
                    gate(2)

                    def over_all(unit, row, hp):
                        ps = side_bank(unit)
                        for t in range(2):
                            h = 2 * t + hp
                            last = mm(ps[:, t * SEQ:(t + 1) * SEQ], ident[:, row + h:row + h + 1].to_broadcast([P, P]), rows, start=True, stop=True)
                        last.then_inc(S("side"), 1)

                    def against_k(unit, q0, hp):
                        ps = side_bank(unit)
                        r = slice(64 * hp, 64 * hp + 64)
                        for t in range(2):
                            for j in range(2):
                                c = slice(j * P, (j + 1) * P)
                                o = (t * 2 + j) * P
                                last = mm(ps[:, o:o + P], qkv[r, 2 + t, c], qkv[r, q0 + t, c], start=True, stop=True)
                        last.then_inc(S("side"), 1)

                    over_all("gb0", 0, 0)
                    over_all("gb1", 0, 1)
                    against_k("kk0", 2, 0)
                    over_all("bb0", 32, 0)
                    against_k("kk1", 2, 1)
                    over_all("bb1", 32, 1)
                    gate(3)
                    against_k("qk0", 0, 0)
                    against_k("qk1", 0, 1)
                    gate(4)

                    def s5_in(s):
                        ps = side_bank(f"pq{s}")
                        r, c = slice(32 * (s % 4), 32 * (s % 4) + 32), (s // 4) * P
                        mm(ps[:, 0:SEQ], par_("sbr", c, c + P)[r], su[r, s // 4, :], start=True, stop=True)
                        mm(ps[:, SEQ:512], par_("sbi", c, c + P)[r], su[r, s // 4, :], start=True, stop=True).then_inc(S("side"), 1)

                    def s5_out(s):
                        pe.wait_ge(S("s5x"), s + 1)
                        q = 32 * (s % 4)
                        o = ybank[q:q + 32, (s // 4) * SEQ:(s // 4 + 1) * SEQ]
                        xs = (tmpE, tmpF)[s % 2]
                        mm(o, par_("scr", s * 32, s * 32 + 32), xs[:, 0, :], start=True, stop=False, tile_position=(0, q))
                        mm(o, par_("sci", s * 32, s * 32 + 32), xs[:, 1, :], start=False, stop=True, tile_position=(0, q)).then_inc(S("s5y"), 1)

                    pe.wait_ge(S("main_act"), main.taken("su"))
                    for lv in range(LEVELS):
                        for hp in range(2):
                            if lv == 0:
                                pe.wait_ge(S("y_first"), hp + 1)
                            else:
                                pe.wait_ge(S("lowc"), 2 * lv + hp + 1)
                            if lv == 1:
                                pe.wait_ge(S("side_act"), side.taken(f"t{hp}_0"))
                            if lv > 1:
                                pe.wait_ge(S("side_dve"), side.taken(f"xt{hp}_{lv - 1}"))
                            ps = side_bank(f"t{hp}_{lv}")
                            for i in range(4):
                                t, j = i // 2, i % 2
                                if lv == 0:
                                    last = nc.tensor.transpose(ps[:, i * P:(i + 1) * P], my[:, hp, t, j, :], ident)
                                else:
                                    last = mm(ps[:, i * P:(i + 1) * P], lowc[:, hp, t, j, :], mx[:, hp, t, j, :], start=True, stop=True)
                            last.then_inc(S("side"), 1)
                        gate(5 + lv)
                        for hp in range(2):
                            if lv:
                                pe.wait_ge(S("side_act"), side.taken(f"t{hp}_{lv}"))
                            if lv > 1:
                                pe.wait_ge(S("side_dve"), side.taken(f"ty{hp}_{lv - 1}"))
                            for n in LEVEL_UNITS[lv]:
                                ps = side_bank(f"{n}{hp}_{lv}")
                                for i in range(4):
                                    t, j = i // 2, i % 2
                                    a, b = (my, mt) if n == "xt" else (mt, my)
                                    last = mm(ps[:, i * P:(i + 1) * P], a[:, hp, t, j, :], b[:, hp, t, j, :], start=True, stop=True)
                                last.then_inc(S("side"), 1)
                        if lv < 4:
                            s5_in(2 * lv)
                            s5_in(2 * lv + 1)
                        if 0 < lv < 5:
                            s5_out(2 * lv - 2)
                            s5_out(2 * lv - 1)
                    pe.wait_ge(S("main_act"), main.taken("rv"))
                    for unit, src in (("rotq", rq), ("rotk", rk)):
                        ps = side_bank(unit)
                        for t in range(2):
                            last = mm(ps[:, t * SEQ:(t + 1) * SEQ], cst_("perm"), src[:, t, :], start=True, stop=True)
                        last.then_inc(S("side"), 1)
                    pe.wait_ge(S("side_dve"), side.taken(f"ty1_{LEVELS - 1}"))
                    ps = side_bank("u")
                    for h in range(NH):
                        t, hp = h // 2, h % 2
                        for j in range(2):
                            o = j * 256 + h * DH
                            last = mm(ps[:, o:o + DH], my[:, hp, t, j, :], vb[:, j, h * DH:(h + 1) * DH], start=True, stop=True)
                    last.then_inc(S("side"), 1)
                    ps = side_bank("w")
                    for h in range(NH):
                        t, hp = h // 2, h % 2
                        for j in range(2):
                            o = t * SEQ + j * P
                            last = mm(ps[64 * hp:64 * hp + 64, o:o + P], kbe[:, j, h * DH:(h + 1) * DH], my[:, hp, t, j, :], start=True, stop=True)
                    last.then_inc(S("side"), 1)

                    def state_up(n):
                        j, r = n // 2, slice(64 * (n % 2), 64 * (n % 2) + 64)
                        if n == 0:
                            pe.wait_ge(S("side_act"), side.taken("u"))
                        else:
                            pe.wait_ge(S("side_dve"), side.taken(f"ws{n}"))
                        ps = side_bank(f"su{n}")
                        for t in range(2):
                            last = mm(ps[:, t * P:(t + 1) * P], kdec[r, j, t * P:(t + 1) * P], uu[r, j, t * P:(t + 1) * P], start=True, stop=True)
                        last.then_inc(S("side"), 1)

                    def from_state(n):
                        r0 = 64 * (n % 2)
                        c = slice(64 * n, 64 * n + 64)
                        pe.wait_ge(S("side_dve"), side.taken(f"su{n - 1}"))
                        pe.wait_ge(S("side_act"), side.taken("w"))
                        ps = side_bank(f"ws{n}")
                        for t in range(2):
                            last = mm(ps[r0:r0 + 64, t * P:(t + 1) * P], wT[:, t, c], state[:, t, :], start=True, stop=True)
                        last.then_inc(S("side"), 1)
                        ps = side_bank(f"oi{n}")
                        for t in range(2):
                            last = mm(ps[:, t * 64:(t + 1) * 64], state[:, t, :], qdec[:, t, c], start=True, stop=True)
                        last.then_inc(S("side"), 1)

                    def scores(h):
                        t, r = h // 2, slice(64 * (h % 2), 64 * (h % 2) + 64)
                        ps = side_bank(f"sc{h}")
                        mm(ps[:, 0:SEQ], rk[r, t, 0:P], rq[r, t, :], start=True, stop=True)
                        mm(ps[:, SEQ:384], rk[r, t, P:SEQ], rq[r, t, P:SEQ], start=True, stop=True).then_inc(S("side"), 1)

                    gate(11)
                    state_up(0)
                    pe.wait_ge(S("rotated"), 2)
                    scores(0)
                    scores(1)
                    gate(12)
                    from_state(1)
                    state_up(1)
                    scores(2)
                    scores(3)
                    gate(13)
                    from_state(2)
                    state_up(2)
                    pe.wait_ge(S("side_dve"), side.taken("sc3"))
                    ps = side_bank("ro")
                    for h in range(NH):
                        t, q = h // 2, 64 * (h % 2)
                        v = slice(h * DH, (h + 1) * DH)
                        mm(ps[q:q + 64, t * SEQ:(t + 1) * SEQ], rv[:, 0, v], scm[:, h, 0:SEQ], start=True, stop=False)
                        last = mm(ps[q:q + 64, t * SEQ + P:(t + 1) * SEQ], rv[:, 1, v], scm[:, h, SEQ:384], start=False, stop=True)
                    last.then_inc(S("side"), 1)
                    gate(14)
                    from_state(3)
                    pe.wait_ge(S("side_act"), side.taken("ro"))
                    ps = side_bank("rm")
                    for t in range(2):
                        last = mm(ps[:, t * SEQ:(t + 1) * SEQ], bo, tmpB[:, t, :], start=True, stop=True)
                    last.then_inc(S("side"), 1)
                    gate(15)
                    pe.wait_ge(S("side_dve"), side.taken("ws3"))
                    for j in range(2):
                        ps = side_bank(f"oa{j}")
                        for h in range(NH):
                            t, q = h // 2, 64 * (h % 2)
                            last = mm(ps[q:q + 64, t * P:(t + 1) * P], uu[:, j, h * DH:(h + 1) * DH], attn[:, h % 2, t, j, :], start=True, stop=True)
                        last.then_inc(S("side"), 1)
                    for unit, ev, src in (("rv2", "ro_sq", tmpC), ("gs", "go_sq", tmpD)):
                        pe.wait_ge(S(ev), 1)
                        ps = side_bank(unit)
                        for t in range(2):
                            last = mm(ps[:, t * SEQ:(t + 1) * SEQ], bo, src[:, t, :], start=True, stop=True)
                        last.then_inc(S("side"), 1)
                    pe.wait_ge(S("s5g"), 1)
                    ps = side_bank("glu")
                    for o in range(2):
                        for k in range(2):
                            c = k * 256 + o * P
                            last = mm(ps[:, o * SEQ:(o + 1) * SEQ], par_("wglu", c, c + P), tmpE[:, k, :], start=(k == 0), stop=(k == 1))
                    last.then_inc(S("side"), 1)

                    for b in range(NB):
                        pe.wait_ge(S(f"branch{b}"), 1)
                    for m in range(KD):
                        wh, wl = piece(f"mg{m}.0")
                        for ab in range(2):
                            ps = main_bank(f"mg{m}{'ab'[ab]}")
                            for n2 in range(2):
                                n = 2 * ab + n2
                                for k in range(2):
                                    last = product(ps[:, n2 * SEQ:(n2 + 1) * SEQ], (wh[:, 2 * n + k, :], wl[:, 2 * n + k, :]),
                                                   (brh[:, n, k, :], brl[n][:, k, :]), k == 0, k == 1)
                            last.then_inc(S("main"), 1)
                    for i in range(4):
                        pair(f"wo{i}", normed=2 if i == 0 else None)
                    ssq("ssq2", 2)
                    ffn(2, 3)

                @block.scalar
                def _(act):
                    A = nc.scalar.activation
                    chain = [0]

                    def link(ins):
                        chain[0] += 1
                        ins.then_inc(S("act"), 1)
                        act.wait_ge(S("act"), chain[0])

                    split = [0]

                    def split_to(n):
                        for i in range(split[0], min(n, len(PIECES))):
                            act.wait_ge(S(f"raw{i % RAW_SLOTS}"), 16 * (i // RAW_SLOTS + 1))
                            if i >= SLOTS:
                                act.wait_ge(*piece_used(i - SLOTS))
                            A(slot(whi, i), slot(raw, i), ACT.Copy).then_inc(S("high"), 1)
                        split[0] = max(split[0], n)

                    def ahead(unit):
                        split_to(UNIT_PIECES[unit][-1] + 3)

                    def square(which, j):
                        if which:
                            act.wait_ge(S("main_dve"), main.taken((f"dn1_{j}", f"wo{j}")[which - 1]))
                        A(squared[:, 2 * j:2 * j + 2, :], x[:, 2 * j:2 * j + 2, :], ACT.Square).then_inc(S("squares"), 1)

                    def high_inputs(which):
                        src = ret if which == 2 else flat8
                        for k in range(KD):
                            if which == 2:
                                ahead(f"mg{k}")
                            act.wait_ge(S("xf"), which * KD + k + 1)
                            A(xh[:, k, :], src[:, k, :], ACT.Copy).then_inc(S("xh"), 1)

                    def rms(unit, which):
                        act.wait_ge(S("main"), main.ready(unit))
                        A(tmpA[:, 0, :], main.bank(unit)[:, 0:SEQ], ACT.Sqrt, bias=eps_col, scale=1.0 / DM).then_inc(S("main_act"), 1)
                        high_inputs(which)

                    def high_hidden(f, m):
                        act.wait_ge(S("main_dve"), main.taken(f"gu{f}_{m}"))
                        A(hh[:, m, :], tmpC[:, m % 2, :], ACT.Copy).then_inc(S("hh"), 1)

                    def silus(f, ms):
                        for m in ms:
                            ahead(f"gu{f}_{m}")
                            act.wait_ge(S("main"), main.ready(f"gu{f}_{m}"))
                            if m >= 2:
                                act.wait_ge(S("main_dve"), main.taken(f"gu{f}_{m - 2}"))
                            A(tmpB[:, m % 2, :], main.bank(f"gu{f}_{m}")[:, 0:SEQ], ACT.Silu).then_inc(S(f"silu{f}"), 1)
                            if m:
                                high_hidden(f, m - 1)
                        if m == MF - 1:
                            high_hidden(f, m)

                    for j in range(4):
                        square(0, j)
                    split_to(3)
                    rms("ssq1", 0)
                    act.wait_ge(S("par"), 16)
                    A(sm["dt"], par_("ldt"), ACT.Exp)
                    A(nega, par_("alog"), ACT.Exp)
                    link(A(lq, par_("lam"), ACT.Abs))
                    A(ly_, lq, ACT.Exp, scale=-1.0).then_inc(S("pexp"), 1)
                    act.wait_ge(S("pmul"), 1)
                    A(sm["mag"], sm["lrdt"], ACT.Exp).then_inc(S("pexp"), 1)
                    silus(1, range(0, 4))
                    act.wait_ge(S("pang"), 1)
                    A(sm["sn"], sm["r1"], ACT.Sin)
                    A(sm["cs"], sm["r2"], ACT.Sin).then_inc(S("psin"), 1)
                    silus(1, range(4, 10))
                    act.wait_ge(S("turns"), 1)
                    A(sinE, turns_a, ACT.Sin, scale=SIN_SCALE).then_inc(S("tables"), 1)
                    silus(1, range(10, 11))
                    act.wait_ge(S("turns"), 2)
                    A(cosE, turns_b, ACT.Sin, scale=SIN_SCALE).then_inc(S("tables"), 1)
                    silus(1, range(11, MF))
                    for j in range(4):
                        ahead(f"dn1_{j}")
                        square(1, j)
                    rms("ssqm", 1)

                    ahead("ba")
                    act.wait_ge(S("main"), main.ready("ba"))
                    A(tmpB[:, 0, :], main.bank("ba")[:, 0:SEQ], ACT.Identity, bias=par_("dtb")).then_inc(S("main_act"), 1)
                    act.wait_ge(S("main_act"), main.taken("ba"))
                    link(A(tmpF[:, 0, :], tmpB[:, 0, :], ACT.Abs))
                    link(A(tmpF[:, 0, :], tmpF[:, 0, :], ACT.Exp, scale=-1.0))
                    A(tmpF[:, 1, :], tmpF[:, 0, :], ACT.Ln, bias=1.0).then_inc(S("ln1p"), 1)
                    A(tmpB[:, 1, :], tmpB[:, 0, :], ACT.Tanh, scale=0.5).then_inc(S("ln1p"), 1)
                    for i in range(3):
                        ahead(f"qkv{i}")
                        act.wait_ge(S("main"), main.ready(f"qkv{i}"))
                        A(qkvp[:, 2 * i:2 * i + 2, 3:], halves(main.bank(f"qkv{i}")[:]), ACT.Identity).then_inc(S("main_act"), 1)
                    act.wait_ge(S("gc"), 1)
                    A(tmpF[:, 0, :], tmpC[:, 0, :], ACT.Exp)
                    for n in range(NCH):
                        c = slice(64 * n, 64 * n + 64)
                        last = A(tmpF[:, 1, c], tmpC[:, 0, c], ACT.Exp, scale=-1.0, bias=tmpC[:, 0, 64 * n + 63:64 * n + 64])
                    last.then_inc(S("egc"), 1)
                    for unit, dst in (("lx", lxp[:, :, 3:]), ("ly", ly), ("su", su), ("z", zz)):
                        ahead(unit)
                        act.wait_ge(S("main"), main.ready(unit))
                        A(dst, halves(main.bank(unit)[:]), ACT.Identity).then_inc(S("main_act"), 1)
                    act.wait_ge(S("main_act"), main.taken("z"))
                    act.wait_ge(S("conv"), 1)
                    A(qkvp[:, :, 3:], qkv, ACT.Tanh, scale=0.5).then_inc(S("conv_t"), 1)
                    A(tmpE, zz, ACT.Tanh, scale=0.5).then_inc(S("zt"), 1)
                    for unit, dst in (("rq", rq), ("rk", rk), ("rg", rg), ("rv", rv)):
                        ahead(unit)
                        act.wait_ge(S("main"), main.ready(unit))
                        A(dst, halves(main.bank(unit)[:]), ACT.Identity).then_inc(S("main_act"), 1)
                    act.wait_ge(S("silu_q"), 1)
                    A(mx_sq[:, 0:2, :], qkv[:, 0:2, :], ACT.Square, scale=0.5).then_inc(S("qk_sq"), 1)
                    A(mx_sq[:, 2:4, :], qkv[:, 2:4, :], ACT.Square, scale=0.5).then_inc(S("qk_sq"), 1)

                    def gate(i):
                        ahead(f"g{i}")
                        act.wait_ge(S("main"), main.ready(f"g{i}"))
                        if i == 11:
                            act.wait_ge(S("s5x"), 8)
                        if i == 15:
                            act.wait_ge(S("branch2"), 1)
                        A(gates[:, 2 * i:2 * i + 2, :], halves(main.bank(f"g{i}")[:]), ACT.Tanh, scale=0.5).then_inc(S("main_act"), 1)

                    for unit, dst, hb in (("lr", tmpB, hba), ("li", tmpD, hbi)):
                        act.wait_ge(S("side"), side.ready(unit))
                        A(dst[:, 0, :], side.bank(unit)[:, 0:SEQ], ACT.Tanh, scale=0.5, bias=hb[:, 0:1])
                        A(dst[:, 1, :], side.bank(unit)[:, SEQ:512], ACT.Tanh, scale=0.5, bias=hb[:, 1:2]).then_inc(S("side_act"), 1)
                    act.wait_ge(S("log_a"), 1)
                    A(tmpF, tmpC, ACT.Exp, scale=2.0)
                    A(tmpE, tmpC, ACT.Tanh, scale=-1.0).then_inc(S("lru_t"), 1)
                    act.wait_ge(S("lru_t"), 1)
                    A(tmpC, tmpC, ACT.Exp).then_inc(S("lru_a"), 1)
                    gate(0)
                    for unit, dst in (("l2q", mx_sq[:, 0:2, :]), ("l2k", mx_sq[:, 2:4, :])):
                        act.wait_ge(S("side"), side.ready(unit))
                        A(dst, halves(side.bank(unit)[:]), ACT.Sqrt, scale=float(DH), bias=eps_col).then_inc(S("side_act"), 1)
                    act.wait_ge(S("lru_q"), 1)
                    A(tmpE, tmpE, ACT.Sqrt, scale=0.25).then_inc(S("lru_m"), 1)
                    gate(1)
                    act.wait_ge(S("side"), side.ready("rowt"))
                    A(rowT, halves(side.bank("rowt")[:, 0:SEQ]), ACT.Identity).then_inc(S("side_act"), 1)
                    act.wait_ge(S("gelu_in"), 1)
                    A(tmpD, tmpD, ACT.Tanh, scale=GELU_C).then_inc(S("gelu_t"), 1)
                    act.wait_ge(S("side"), side.ready("eb"))
                    A(egb, halves(side.bank("eb")[:]), ACT.Exp).then_inc(S("side_act"), 1)
                    gate(2)
                    for hp in range(2):
                        act.wait_ge(S("side_dve"), side.taken(f"gb{hp}"))
                        A(flat(dec)[:, hp, :], flat(dec)[:, hp, :], ACT.Exp).then_inc(S("dec"), 1)
                    gate(3)
                    gate(4)
                    for lv in range(LEVELS):
                        for hp in range(2):
                            act.wait_ge(S("side"), side.ready(f"t{hp}_{lv}"))
                            A(flat(mt if lv else mx)[:, hp, :], side.bank(f"t{hp}_{lv}")[:], ACT.Identity).then_inc(S("side_act"), 1)
                        gate(5 + lv)
                    act.wait_ge(S("side"), side.ready("u"))
                    A(uu, halves(side.bank("u")[:]), ACT.Identity).then_inc(S("side_act"), 1)
                    act.wait_ge(S("side"), side.ready("w"))
                    A(wT, halves(side.bank("w")[:]), ACT.Identity).then_inc(S("side_act"), 1)
                    gate(11)

                    def inter(n):
                        act.wait_ge(S("side"), side.ready(f"oi{n}"))
                        A(go[:, :, 64 * n:64 * n + 64], halves(side.bank(f"oi{n}")[:, 0:P]), ACT.Identity).then_inc(S("side_act"), 1)

                    gate(12)
                    inter(1)
                    act.wait_ge(S("rotated"), 2)
                    A(tmpA, rg, ACT.Tanh, scale=0.5).then_inc(S("rgt"), 1)
                    gate(13)
                    inter(2)
                    act.wait_ge(S("side"), side.ready("ro"))
                    A(tmpB, halves(side.bank("ro")[:]), ACT.Identity).then_inc(S("side_act"), 1)
                    gate(14)
                    inter(3)
                    act.wait_ge(S("side_dve"), side.taken("rm"))
                    A(tmpC, tmpB, ACT.Square).then_inc(S("ro_sq"), 1)
                    gate(15)
                    act.wait_ge(S("side_dve"), side.taken("oa1"))
                    A(tmpD, go, ACT.Square).then_inc(S("go_sq"), 1)
                    act.wait_ge(S("side"), side.ready("rv2"))
                    A(tmpC, halves(side.bank("rv2")[:]), ACT.Sqrt, bias=eps_col).then_inc(S("side_act"), 1)
                    act.wait_ge(S("side"), side.ready("gs"))
                    A(tmpD, halves(side.bank("gs")[:]), ACT.Sqrt, bias=eps_col).then_inc(S("side_act"), 1)
                    act.wait_ge(S("s5gin"), 1)
                    A(tmpE, tmpE, ACT.Tanh, scale=GELU_C).then_inc(S("s5gt"), 1)
                    act.wait_ge(S("side"), side.ready("glu"))
                    A(tmpF[:, 0, :], side.bank("glu")[:, 0:SEQ], ACT.Tanh, scale=0.25, bias=hbg[:, 0:1])
                    A(tmpF[:, 1, :], side.bank("glu")[:, SEQ:512], ACT.Tanh, scale=0.25, bias=hbg[:, 1:2]).then_inc(S("side_act"), 1)
                    high_inputs(2)
                    for i in range(4):
                        ahead(f"wo{i}")
                        square(2, i)
                    rms("ssq2", 3)
                    silus(2, range(MF))
                    for j in range(4):
                        ahead(f"dn2_{j}")

                @block.gpsimd
                def _(pool):
                    tt = nc.gpsimd.tensor_tensor
                    def level_blocks(lv):
                        for hp in range(2):
                            if lv == 0:
                                pool.wait_ge(S("side_dve"), side.taken(f"qk{hp}"))
                            elif lv == 1:
                                pool.wait_ge(S("y_first"), hp + 1)
                            else:
                                pool.wait_ge(S("side"), side.ready(f"t{hp}_{lv - 1}"))
                            tt(lowc[:, hp].rearrange("p t j c -> p (t j) c"), low[:, hp].rearrange("p t j c -> p (t j) c"),
                               over(cst_("lev", lv * P, (lv + 1) * P), 4), ALU.mult).then_inc(S("lowc"), 1)

                    def s5_back(s):
                        ss, xs = (tmpC, tmpD)[s % 2], (tmpE, tmpF)[s % 2]
                        pool.wait_ge(S("s5s"), s + 1)
                        if s >= 1:
                            pool.wait_ge(S("s5x"), s)
                        if s >= 2:
                            pool.wait_ge(S("s5y"), s - 1)
                        tt(xs, ss, over(cosE[:, s, :], 2), ALU.mult)
                        tt(s5n, ss, over(sinE[:, s, :], 2), ALU.mult).then_inc(S("pool"), 1)
                        pool.wait_ge(S("pool"), s + 1)
                        tt(xs[:, 0, :], xs[:, 0, :], s5n[:, 1, :], ALU.subtract)
                        tt(xs[:, 1, :], xs[:, 1, :], s5n[:, 0, :], ALU.add).then_inc(S("s5x"), 1)

                    level_blocks(0)
                    for hp in range(2):
                        pool.wait_ge(S("lowc"), hp + 1)
                        tt(my[:, hp].rearrange("p t j c -> p (t j) c"), over(ident, 4), lowc[:, hp].rearrange("p t j c -> p (t j) c"),
                           ALU.subtract).then_inc(S("y_first"), 1)
                    for lv in range(LEVELS):
                        if lv + 1 < LEVELS:
                            level_blocks(lv + 1)
                        if lv + 2 == LEVELS:
                            pool.wait_ge(S("lowc"), 2 * LEVELS)
                            nc.gpsimd.memset(state, 0.0).then_inc(S("state_zero"), 1)
                        if lv < 4:
                            s5_back(2 * lv)
                            s5_back(2 * lv + 1)

                @block.vector
                def _(dve):
                    V = nc.vector
                    chain = [0]

                    def link(ins):
                        chain[0] += 1
                        ins.then_inc(S("dve"), 1)
                        dve.wait_ge(S("dve"), chain[0])

                    split = [0]

                    def split_to(n):
                        for i in range(split[0], min(n, len(PIECES))):
                            dve.wait_ge(S("high"), i + 1)
                            V.tensor_tensor(slot(wlo, i), slot(raw, i), r32(slot(whi, i)), ALU.subtract).then_inc(S("low"), 1)
                        split[0] = max(split[0], n)

                    def ahead(unit):
                        split_to(UNIT_PIECES[unit][-1] + 3)

                    def low_input(which, k):
                        src = ret if which == 2 else flat8
                        dve.wait_ge(S("xh"), which * KD + k + 1)
                        V.tensor_tensor(xl[:, k, :], src[:, k, :], r32(xh[:, k, :]), ALU.subtract).then_inc(S("normed"), 1)

                    def normed(unit, which, wname):
                        dve.wait_ge(S("main_act"), main.taken(unit))
                        link(V.reciprocal(tmpA[:, 1, :], tmpA[:, 0, :]))
                        for k in range(KD):
                            V.scalar_tensor_tensor(flat8[:, k, :], x[:, k, :], par_(wname, k, k + 1), tmpA[:, 1, :], ALU.mult, ALU.mult).then_inc(S("xf"), 1)
                            if k:
                                low_input(which, k - 1)
                        low_input(which, KD - 1)

                    def low_hidden(f, m):
                        dve.wait_ge(S("hh"), MF * (f - 1) + m + 1)
                        V.tensor_tensor(hl[:, m, :], tmpC[:, m % 2, :], r32(hh[:, m, :]), ALU.subtract).then_inc(S("hidden"), 1)

                    def up(f, ms):
                        for m in ms:
                            ahead(f"gu{f}_{m}")
                            dve.wait_ge(S(f"silu{f}"), m + 1)
                            if m >= 2:
                                dve.wait_ge(S("hidden"), MF * (f - 1) + m - 1)
                            ps = main.bank(f"gu{f}_{m}")
                            V.tensor_tensor(tmpC[:, m % 2, :], tmpB[:, m % 2, :], ps[:, SEQ:512], ALU.mult).then_inc(S("main_dve"), 1)
                            if m:
                                low_hidden(f, m - 1)
                        if m == MF - 1:
                            low_hidden(f, m)

                    def down(units, scale):
                        for j, unit in enumerate(units):
                            ahead(unit)
                            dve.wait_ge(S("main"), main.ready(unit))
                            V.scalar_tensor_tensor(x[:, 2 * j:2 * j + 2, :], halves(main.bank(unit)[:]), scale, x[:, 2 * j:2 * j + 2, :],
                                                   ALU.mult, ALU.add).then_inc(S("main_dve"), 1)

                    split_to(2)
                    dve.wait_ge(S("par"), 16)
                    normed("ssq1", 0, "n1")
                    lre, lim = par_("lre"), par_("lim")
                    dve.wait_ge(S("pexp"), 1)
                    V.tensor_tensor(sm["lrdt"], lre, sm["dt"], ALU.mult).then_inc(S("pmul"), 1)
                    link(V.tensor_tensor(sm["th"], lim, sm["dt"], ALU.mult))
                    for r, quarter in ((sm["r1"], 0.0), (sm["r2"], 0.25)):
                        link(V.tensor_scalar(sm["n1"], sm["th"], 1.0 / TWO_PI, quarter, ALU.mult, ALU.add))
                        link(V.tensor_scalar(sm["n1"], sm["n1"], ROUND, -ROUND, ALU.add, ALU.add))
                        link(V.scalar_tensor_tensor(r, sm["n1"], -PI_C[0], sm["th"], ALU.mult, ALU.add))
                        link(V.scalar_tensor_tensor(r, sm["n1"], -PI_C[1], r, ALU.mult, ALU.add))
                        link(V.scalar_tensor_tensor(r, sm["n1"], -PI_C[2], r, ALU.mult, ALU.add))
                        link(V.tensor_scalar(r, r, quarter * TWO_PI, PI_SAFE, ALU.add, ALU.min))
                        link(V.tensor_scalar(r, r, -PI_SAFE, None, ALU.max))
                    link(V.tensor_scalar(sm["ph"], sm["r1"], 1.0 / TWO_PI, None, ALU.mult))
                    link(V.tensor_scalar(sm["t1"], sm["ph"], GRID, -GRID, ALU.add, ALU.add))
                    V.tensor_tensor(sm["phl"], sm["ph"], sm["t1"], ALU.subtract).then_inc(S("pang"), 1)
                    dve.wait_ge(S("pang"), 1)
                    up(1, range(0, 3))
                    dve.wait_ge(S("pmul"), 1)
                    V.tensor_scalar(nega, nega, -1.0, None, ALU.mult)
                    V.tensor_scalar(gnh, par_("gnorm"), 0.5, None, ALU.mult)
                    V.tensor_scalar(rnh, par_("rnorm"), 0.5, None, ALU.mult)
                    V.tensor_scalar(hba, par_("lba"), 0.5, None, ALU.mult)
                    V.tensor_scalar(hbi, par_("lbi"), 0.5, None, ALU.mult)
                    link(V.tensor_scalar(hbg, par_("bglu"), 0.5, None, ALU.mult))
                    link(V.tensor_scalar(ls_, ly_, 2.0, None, ALU.add))
                    link(V.reciprocal(ls_, ls_))
                    link(V.tensor_tensor(ls_, ls_, ly_, ALU.mult))
                    link(V.tensor_tensor(ls2, ls_, ls_, ALU.mult))
                    link(V.tensor_scalar(lq, ls2, 1.0 / 19, None, ALU.mult))
                    for k in range(17, 2, -2):
                        link(V.scalar_tensor_tensor(lq, lq, 1.0 / k, ls2, ALU.add, ALU.mult))
                    link(V.scalar_tensor_tensor(lq, lq, 1.0, ls_, ALU.add, ALU.mult))
                    link(V.tensor_scalar(sp4, par_("lam"), -1.0, 0.0, ALU.mult, ALU.max))
                    link(V.scalar_tensor_tensor(sp4, lq, 2.0, sp4, ALU.mult, ALU.add))
                    link(V.tensor_scalar(sp4, sp4, -4.0, None, ALU.mult))
                    dve.wait_ge(S("psin"), 1)
                    dve.wait_ge(S("pexp"), 2)
                    link(V.tensor_tensor(sm["ai"], sm["mag"], sm["sn"], ALU.mult))
                    link(V.tensor_tensor(sm["nr"], sm["mag"], sm["cs"], ALU.mult))
                    link(V.tensor_scalar(sm["nr"], sm["nr"], -1.0, None, ALU.add))
                    link(V.tensor_tensor(sm["den"], lre, lre, ALU.mult))
                    link(V.tensor_tensor(sm["t2"], lim, lim, ALU.mult))
                    link(V.tensor_tensor(sm["den"], sm["den"], sm["t2"], ALU.add))
                    link(V.reciprocal(sm["den"], sm["den"]))
                    link(V.tensor_tensor(sm["cre"], sm["nr"], lre, ALU.mult))
                    link(V.tensor_tensor(sm["t2"], sm["ai"], lim, ALU.mult))
                    link(V.tensor_tensor(sm["cre"], sm["cre"], sm["t2"], ALU.add))
                    link(V.tensor_tensor(sm["cre"], sm["cre"], sm["den"], ALU.mult))
                    link(V.tensor_tensor(sm["cim"], sm["ai"], lre, ALU.mult))
                    link(V.tensor_tensor(sm["t2"], sm["nr"], lim, ALU.mult))
                    link(V.tensor_tensor(sm["cim"], sm["cim"], sm["t2"], ALU.subtract))
                    link(V.tensor_tensor(sm["cim"], sm["cim"], sm["den"], ALU.mult))
                    up(1, range(3, 5))
                    cr, ci = halves(par_("scr"), 8), halves(par_("sci"), 8)
                    bre = sm["cre"].unsqueeze(2).to_broadcast([P, 8, 32])
                    bim = sm["cim"].unsqueeze(2).to_broadcast([P, 8, 32])
                    c1, c2 = halves(tmpD[:, 0, :], 8), halves(tmpD[:, 1, :], 8)
                    link(V.tensor_tensor(c1, ci, bim, ALU.mult))
                    link(V.tensor_tensor(c2, cr, bim, ALU.mult))
                    link(V.tensor_tensor(cr, cr, bre, ALU.mult))
                    link(V.tensor_tensor(cr, cr, c1, ALU.subtract))
                    link(V.tensor_tensor(ci, ci, bre, ALU.mult))
                    link(V.scalar_tensor_tensor(ci, ci, -1.0, c2, ALU.mult, ALU.subtract))
                    up(1, range(5, 7))
                    ta, tb = turns_a, turns_b
                    one = cst_("one").to_broadcast([P, SEQ])
                    link(V.tensor_tensor_scan(tmpF[:, 0, :], one, one, -1.0, ALU.mult, ALU.add))
                    tok = over(tmpF[:, 0, :], 8)
                    link(V.tensor_tensor(ta, tok, sm["t1"].unsqueeze(2).to_broadcast([P, 8, SEQ]), ALU.mult))
                    link(V.tensor_scalar(tb, ta, ROUND, -ROUND, ALU.add, ALU.add))
                    up(1, range(7, 8))
                    link(V.tensor_tensor(ta, ta, tb, ALU.subtract))
                    link(V.tensor_tensor(tb, tok, sm["phl"].unsqueeze(2).to_broadcast([P, 8, SEQ]), ALU.mult))
                    up(1, range(8, 9))
                    link(V.tensor_tensor(tb, ta, tb, ALU.add))
                    link(V.tensor_scalar(ta, tb, ROUND, -ROUND, ALU.add, ALU.add))
                    up(1, range(9, 10))
                    V.tensor_tensor(ta, tb, ta, ALU.subtract).then_inc(S("turns"), 1)
                    link(V.tensor_scalar(tb, tb, 0.25, None, ALU.add))
                    up(1, range(10, 11))
                    dve.wait_ge(S("tables"), 1)
                    link(V.tensor_scalar(ta, tb, ROUND, -ROUND, ALU.add, ALU.add))
                    V.tensor_tensor(tb, tb, ta, ALU.subtract).then_inc(S("turns"), 1)
                    up(1, range(11, MF))
                    down([f"dn1_{j}" for j in range(4)], 0.5)

                    normed("ssqm", 1, "nm")
                    split_to(PIECE_INDEX["qkv1.1"] + 1)
                    dve.wait_ge(S("ln1p"), 1)
                    link(V.scalar_tensor_tensor(tmpC[:, 1, :], tmpB[:, 0, :], 0.0, tmpF[:, 1, :], ALU.max, ALU.add))
                    link(V.tensor_scalar(tmpC[:, 1, :], tmpC[:, 1, :], nega, None, ALU.mult))
                    for n in range(NCH):
                        c = slice(64 * n, 64 * n + 64)
                        last = V.tensor_tensor_scan(tmpC[:, 0, c], cst_("one").to_broadcast([P, 64]), tmpC[:, 1, c], 0.0, ALU.mult, ALU.add)
                    last.then_inc(S("gc"), 1)
                    split_to(PIECE_INDEX["lx.0"])
                    dve.wait_ge(S("ln1p"), 2)
                    dve.wait_ge(S("gc"), 1)
                    link(V.tensor_scalar(tmpC[:, 1, :], tmpB[:, 1, :], 1.0, 0.5, ALU.add, ALU.mult))
                    V.tensor_copy(rows[32:36, :], tmpC[32:36, 1, :])
                    link(V.tensor_copy(rows[64:68, :], tmpC[32:36, 1, :]))
                    V.tensor_copy(rows[0:4, :], tmpC[0:4, 0, :])
                    ahead("qkv2")
                    dve.wait_ge(S("egc"), 1)
                    V.tensor_tensor(rows[64:68, :], rows[64:68, :], tmpF[64:68, 0, :], ALU.mult)
                    V.tensor_copy(rows[96:100, :], tmpF[96:100, 1, :]).then_inc(S("rows"), 1)
                    ahead("lx")
                    gw = lambda k, t: par_("gconv", 6 * k + t, 6 * k + t + 1)
                    for k in range(4):
                        for t in range(6):
                            if k == 0:
                                if t % 2 == 0:
                                    dve.wait_ge(S("main_act"), main.taken(f"qkv{t // 2}"))
                                last = V.tensor_scalar(qkv[:, t, :], qkvp[:, t, 0:SEQ], gw(0, t), None, ALU.mult)
                            else:
                                last = V.scalar_tensor_tensor(qkv[:, t, :], qkvp[:, t, k:k + SEQ], gw(k, t), qkv[:, t, :], ALU.mult, ALU.add)
                        if k < 3:
                            link(last)
                        if k == 1:
                            ahead("ly")
                    last.then_inc(S("conv"), 1)
                    ahead("su")
                    xc = tmpA
                    dve.wait_ge(S("main_act"), main.taken("lx"))
                    lw = lambda k, t: par_("lconv", 2 * k + t, 2 * k + t + 1)
                    for k in range(4):
                        for t in range(2):
                            if k == 0:
                                last = V.tensor_scalar(xc[:, t, :], lxp[:, t, 0:SEQ], lw(0, t), par_("lcb", t, t + 1), ALU.mult, ALU.add)
                            else:
                                last = V.scalar_tensor_tensor(xc[:, t, :], lxp[:, t, k:k + SEQ], lw(k, t), xc[:, t, :], ALU.mult, ALU.add)
                        if k < 3:
                            link(last)
                    last.then_inc(S("lru_conv"), 1)
                    ahead("z")
                    dve.wait_ge(S("conv_t"), 1)
                    V.scalar_tensor_tensor(qkv, qkvp[:, :, 3:], 1.0, qkv, ALU.add, ALU.mult).then_inc(S("silu_q"), 1)
                    ahead("rq")
                    dve.wait_ge(S("zt"), 1)
                    V.scalar_tensor_tensor(zz, tmpE, 1.0, zz, ALU.add, ALU.mult)
                    ahead("rk")
                    ahead("rg")
                    ahead("rv")
                    dve.wait_ge(S("side_act"), side.taken("li"))
                    for t in range(2):
                        last = V.tensor_scalar(tmpC[:, t, :], tmpB[:, t, :], 1.0, sp4[:, t:t + 1], ALU.add, ALU.mult)
                    last.then_inc(S("log_a"), 1)
                    dve.wait_ge(S("log_a"), 1)
                    link(V.scalar_tensor_tensor(tmpB, tmpD, 1.0, xc, ALU.add, ALU.mult))
                    dve.wait_ge(S("lru_t"), 1)
                    V.scalar_tensor_tensor(tmpE, tmpF, 1.0, tmpE, ALU.add, ALU.mult).then_inc(S("lru_q"), 1)
                    dve.wait_ge(S("main_act"), main.taken("ly"))
                    dve.wait_ge(S("lru_q"), 1)
                    link(V.tensor_tensor(tmpD, ly, ly, ALU.mult))
                    link(V.tensor_scalar(tmpD, tmpD, 0.044715, 1.0, ALU.mult, ALU.add))
                    V.tensor_tensor(tmpD, tmpD, ly, ALU.mult).then_inc(S("gelu_in"), 1)
                    ahead("g0")
                    dve.wait_ge(S("side_act"), side.taken("l2k"))
                    link(V.reciprocal(mx_sq, mx_sq))
                    V.scalar_tensor_tensor(qkv[:, 0:2, :], qkv[:, 0:2, :], 0.5 * DH ** -0.5, mx_sq[:, 0:2, :], ALU.mult, ALU.mult)
                    V.scalar_tensor_tensor(qkv[:, 2:4, :], qkv[:, 2:4, :], 0.5, mx_sq[:, 2:4, :], ALU.mult, ALU.mult).then_inc(S("k_normed"), 1)
                    dve.wait_ge(S("k_normed"), 1)
                    dve.wait_ge(S("lru_m"), 1)
                    dve.wait_ge(S("lru_a"), 1)
                    link(V.tensor_tensor(tmpB, tmpB, tmpE, ALU.mult))
                    for t in range(2):
                        last = V.tensor_tensor_scan(tmpF[:, t, :], tmpC[:, t, :], tmpB[:, t, :], 0.0, ALU.mult, ALU.add)
                    link(last)
                    ahead("g1")
                    dve.wait_ge(S("side"), side.ready("ktr"))
                    dve.wait_ge(S("side_act"), side.taken("rowt"))

                    def cols(r, j):
                        return rowT[:, j, 32 * r:32 * r + 4].unsqueeze(2).to_broadcast([P, 4, DH])

                    def heads(ap):
                        return ap.rearrange("p (h d) -> p h d", h=4)

                    for j in range(2):
                        ps = side.bank("ktr")[:, j * 256:(j + 1) * 256]
                        V.tensor_tensor(heads(kbe[:, j, :]), heads(ps), cols(2, j), ALU.mult)
                        last = V.tensor_tensor(heads(kdec[:, j, :]), heads(ps), cols(3, j), ALU.mult)
                    last.then_inc(S("side_dve"), 1)
                    dve.wait_ge(S("side"), side.ready("vtr"))
                    for j in range(2):
                        ps = side.bank("vtr")[:, j * 256:(j + 1) * 256]
                        last = V.scalar_tensor_tensor(heads(vb[:, j, :]), heads(ps), 0.5, cols(1, j), ALU.mult, ALU.mult)
                    last.then_inc(S("side_dve"), 1)
                    dve.wait_ge(S("gelu_t"), 1)
                    link(V.scalar_tensor_tensor(tmpD, tmpD, 1.0, ly, ALU.add, ALU.mult))
                    V.scalar_tensor_tensor(griffin, tmpF, 0.5, tmpD, ALU.mult, ALU.mult)

                    def branch(n, src):
                        link(V.tensor_copy(brh[:, n], src))
                        V.tensor_tensor(brl[n], src, r32(brh[:, n]), ALU.subtract).then_inc(S(f"branch{n}"), 1)

                    dve.wait_ge(S("side_act"), side.taken("eb"))
                    V.tensor_tensor(qdec, qkv[:, 0:2, :], egb, ALU.mult).then_inc(S("dve_q"), 1)
                    ahead("g2")
                    for hp in range(2):
                        ps = side.bank(f"gb{hp}")
                        dve.wait_ge(S("side"), side.ready(f"gb{hp}"))
                        for t in range(2):
                            for j in range(2):
                                o = (t * 2 + j) * P
                                h = 2 * t + hp
                                last = V.tensor_scalar(dec[:, hp, t, j, :], ps[:, o:o + P], rowT[:, j, h:h + 1], 0.0, ALU.subtract, ALU.min)
                        last.then_inc(S("side_dve"), 1)
                    tj = lambda m, hp: m[:, hp].rearrange("p t j c -> p (t j) c")
                    for hp in range(2):
                        dve.wait_ge(S("dec"), hp + 1)
                        link(V.tensor_tensor(tj(dec, hp), tj(dec, hp), over(cst_("incl"), 4), ALU.mult))
                        dve.wait_ge(S("side"), side.ready(f"kk{hp}"))
                        V.tensor_tensor(flat(low)[:, hp, :], side.bank(f"kk{hp}")[:], flat(dec)[:, hp, :], ALU.mult).then_inc(S("side_dve"), 1)
                        dve.wait_ge(S("side_dve"), side.taken(f"kk{hp}"))
                        dve.wait_ge(S("side"), side.ready(f"bb{hp}"))
                        V.tensor_tensor(flat(low)[:, hp, :], side.bank(f"bb{hp}")[:], flat(low)[:, hp, :], ALU.mult).then_inc(S("side_dve"), 1)
                    ahead("g3")
                    for hp in range(2):
                        dve.wait_ge(S("side"), side.ready(f"qk{hp}"))
                        V.tensor_tensor(flat(attn)[:, hp, :], side.bank(f"qk{hp}")[:], flat(dec)[:, hp, :], ALU.mult).then_inc(S("side_dve"), 1)

                    def s5_state(s):
                        ps = halves(side.bank(f"pq{s}")[:])
                        dve.wait_ge(S("side"), side.ready(f"pq{s}"))
                        if s:
                            dve.wait_ge(S("s5s"), s)
                        V.tensor_tensor(tmpA, ps, over(cosE[:, s, :], 2), ALU.mult)
                        V.tensor_tensor(tmpB, ps, over(sinE[:, s, :], 2), ALU.mult).then_inc(S("side_dve"), 1)
                        dve.wait_ge(S("side_dve"), side.taken(f"pq{s}"))
                        V.tensor_tensor(tmpA[:, 0, :], tmpA[:, 0, :], tmpB[:, 1, :], ALU.add)
                        link(V.tensor_tensor(tmpA[:, 1, :], tmpA[:, 1, :], tmpB[:, 0, :], ALU.subtract))
                        ss = (tmpC, tmpD)[s % 2]
                        if s >= 2:
                            dve.wait_ge(S("s5x"), s - 1)
                        mag = sm["mag"][:, s:s + 1].to_broadcast([P, SEQ])
                        V.tensor_tensor_scan(ss[:, 0, :], mag, tmpA[:, 0, :], 0.0, ALU.mult, ALU.add)
                        V.tensor_tensor_scan(ss[:, 1, :], mag, tmpA[:, 1, :], 0.0, ALU.mult, ALU.add).then_inc(S("s5s"), 1)

                    dve.wait_ge(S("tables"), 2)
                    ahead("g4")
                    for lv in range(LEVELS):
                        ahead(f"g{5 + lv}")
                        for hp in range(2):
                            for n in LEVEL_UNITS[lv]:
                                m = mx if n == "xt" else my
                                unit = f"{n}{hp}_{lv}"
                                dve.wait_ge(S("side"), side.ready(unit))
                                V.tensor_tensor(flat(m)[:, hp, :], flat(m)[:, hp, :], side.bank(unit)[:], ALU.subtract).then_inc(S("side_dve"), 1)
                        if lv < 4:
                            s5_state(2 * lv)
                            s5_state(2 * lv + 1)
                    dve.wait_ge(S("s5s"), NST)
                    for i, (unit, src) in enumerate((("rotq", rq), ("rotk", rk))):
                        dve.wait_ge(S("side"), side.ready(unit))
                        if i:
                            dve.wait_ge(S("rotated"), i)
                        V.tensor_tensor(tmpA, halves(side.bank(unit)[:]), over(ropes, 2), ALU.mult).then_inc(S("side_dve"), 1)
                        link(V.tensor_tensor(src, src, over(ropec, 2), ALU.mult))
                        dve.wait_ge(S("side_dve"), side.taken(unit))
                        V.tensor_tensor(src, src, tmpA, ALU.add).then_inc(S("rotated"), 1)

                    def state_up(n):
                        ps = side.bank(f"su{n}")
                        dve.wait_ge(S("side"), side.ready(f"su{n}"))
                        for t in range(2):
                            for hp in range(2):
                                r, c = slice(64 * hp, 64 * hp + 64), slice(64 * hp, 64 * hp + 64)
                                pc = slice(t * P + 64 * hp, t * P + 64 * hp + 64)
                                if n == 0:
                                    if t == 0 and hp == 0:
                                        dve.wait_ge(S("state_zero"), 1)
                                    last = V.tensor_copy(state[r, t, c], ps[r, pc])
                                else:
                                    last = V.scalar_tensor_tensor(state[r, t, c], state[r, t, c], egb[r, t, 64 * n + 63:64 * n + 64], ps[r, pc],
                                                                  ALU.mult, ALU.add)
                        last.then_inc(S("side_dve"), 1)

                    def values(n):
                        r, j = slice(64 * (n % 2), 64 * (n % 2) + 64), n // 2
                        dve.wait_ge(S("side"), side.ready(f"ws{n}"))
                        V.tensor_tensor(uu[r, j, :], uu[r, j, :], side.bank(f"ws{n}")[r, 0:256], ALU.subtract).then_inc(S("side_dve"), 1)

                    def masked(h):
                        dve.wait_ge(S("side"), side.ready(f"sc{h}"))
                        mask = cst_("rmask", SEQ * h, SEQ * (h + 1))
                        V.tensor_tensor(scm[:, h, 0:SEQ], side.bank(f"sc{h}")[:, 0:SEQ], mask, ALU.mult)
                        V.tensor_tensor(scm[:, h, SEQ:384], side.bank(f"sc{h}")[:, SEQ:384], mask[:, 0:P], ALU.mult).then_inc(S("side_dve"), 1)

                    ahead("g11")
                    state_up(0)
                    masked(0)
                    masked(1)
                    ahead("g12")
                    values(1)
                    state_up(1)
                    masked(2)
                    masked(3)
                    ahead("g13")
                    values(2)
                    state_up(2)
                    branch(2, griffin)
                    ahead("g14")
                    values(3)
                    dve.wait_ge(S("s5y"), 8)
                    for t in range(2):
                        last = V.scalar_tensor_tensor(su[:, t, :], su[:, t, :], par_("s5d", t, t + 1), ybank[:, t * SEQ:(t + 1) * SEQ], ALU.mult, ALU.add)
                    link(last)
                    link(V.tensor_tensor(tmpE, su, su, ALU.mult))
                    link(V.tensor_scalar(tmpE, tmpE, 0.044715, 1.0, ALU.mult, ALU.add))
                    V.tensor_tensor(tmpE, tmpE, su, ALU.mult).then_inc(S("s5gin"), 1)
                    dve.wait_ge(S("rgt"), 1)
                    link(V.scalar_tensor_tensor(rg, tmpA, 1.0, rg, ALU.add, ALU.mult))
                    dve.wait_ge(S("side"), side.ready("rm"))
                    V.tensor_tensor(tmpB, tmpB, halves(side.bank("rm")[:]), ALU.subtract).then_inc(S("side_dve"), 1)
                    ahead("g15")
                    dve.wait_ge(S("side_act"), side.taken("oi3"))
                    for j in range(2):
                        dve.wait_ge(S("side"), side.ready(f"oa{j}"))
                        ps = halves(side.bank(f"oa{j}")[:, 0:256])
                        if j == 0:
                            V.tensor_copy(go[:, :, 0:64], ps[:, :, 0:64])
                            V.tensor_tensor(go[:, :, 64:P], go[:, :, 64:P], ps[:, :, 64:P], ALU.add).then_inc(S("side_dve"), 1)
                        else:
                            V.tensor_tensor(go[:, :, P:SEQ], go[:, :, P:SEQ], ps, ALU.add).then_inc(S("side_dve"), 1)
                    dve.wait_ge(S("side_act"), side.taken("rv2"))
                    link(V.reciprocal(tmpC, tmpC))
                    link(V.tensor_tensor(tmpB, tmpB, tmpC, ALU.mult))
                    for t in range(2):
                        last = V.scalar_tensor_tensor(tmpB[:, t, :], tmpB[:, t, :], rnh[:, t:t + 1], rg[:, t, :], ALU.mult, ALU.mult)
                    link(last)
                    branch(3, tmpB)
                    dve.wait_ge(S("side_act"), side.taken("gs"))
                    link(V.reciprocal(tmpD, tmpD))
                    link(V.tensor_tensor(go, go, tmpD, ALU.mult))
                    link(V.scalar_tensor_tensor(go, go, gnh, zz, ALU.mult, ALU.mult))
                    branch(0, go)
                    dve.wait_ge(S("s5gt"), 1)
                    V.scalar_tensor_tensor(tmpE, tmpE, 1.0, su, ALU.add, ALU.mult).then_inc(S("s5g"), 1)
                    dve.wait_ge(S("side_act"), side.taken("glu"))
                    link(V.scalar_tensor_tensor(tmpF, tmpF, 1.0, tmpE, ALU.add, ALU.mult))
                    link(V.tensor_scalar(tmpF, tmpF, 0.25, None, ALU.mult))
                    branch(1, tmpF)
                    gbr = gates.rearrange("p (n m) t -> p n m t", n=NB)
                    dve.wait_ge(S("main_act"), main.taken("g15"))
                    for m in range(KD):
                        ahead(f"mg{m}")
                        for ab, t in enumerate((tmpA, tmpB)):
                            unit = f"mg{m}{'ab'[ab]}"
                            dve.wait_ge(S("main"), main.ready(unit))
                            V.scalar_tensor_tensor(t, gbr[:, 2 * ab:2 * ab + 2, m, :], 1.0, halves(main.bank(unit)[:]), ALU.add, ALU.mult).then_inc(S("main_dve"), 1)
                        dve.wait_ge(S("main_dve"), main.taken(f"mg{m}b"))
                        link(V.tensor_tensor(tmpA, tmpA, tmpB, ALU.add))
                        V.tensor_tensor(ret[:, m, :], tmpA[:, 0, :], tmpA[:, 1, :], ALU.add).then_inc(S("xf"), 1)
                        if m:
                            low_input(2, m - 1)
                        dve.wait_ge(S("xf"), 2 * KD + m + 1)
                    low_input(2, KD - 1)
                    down([f"wo{i}" for i in range(4)], 0.5)
                    normed("ssq2", 3, "n2")
                    up(2, range(MF))
                    down([f"dn2_{j}" for j in range(4)], 0.5)

            handles = [per_layer[n].num for n in per_layer]
            assert sorted(handles) == list(range(min(handles), max(handles) + 1))
            nc.all_engine_barrier(sems_to_clear=range(min(handles), max(handles) + 1))

        with nc.Block() as block:
            @block.scalar
            def _(act):
                nc.scalar.activation(flat8, x, ACT.Square).then_inc(once["fin_act"], 1)
                act.wait_ge(once["fin_pe"], 1)
                nc.scalar.activation(tmpA[:, 0, :], psum[0][:, 0:SEQ], ACT.Sqrt, bias=eps_col, scale=1.0 / DM).then_inc(once["fin_act"], 1)

            @block.tensor
            def _(pe):
                pe.wait_ge(once["fin_act"], 1)
                for k in range(KD):
                    last = nc.tensor.matmul(psum[0][:, 0:SEQ], ones, flat8[:, k, :], start=(k == 0), stop=(k == KD - 1))
                last.then_inc(once["fin_pe"], 1)

            @block.vector
            def _(dve):
                dve.wait_ge(once["fin_act"], 2)
                nc.vector.reciprocal(tmpA[:, 1, :], tmpA[:, 0, :]).then_inc(once["fin_dve"], 1)
                dve.wait_ge(once["fin_dve"], 1)
                for k in range(KD):
                    nc.vector.scalar_tensor_tensor(ret[:, k, :], x[:, k, :], cst_("fnorm", k, k + 1), tmpA[:, 1, :], ALU.mult, ALU.mult).then_inc(once["fin_dve"], 1)

            @block.sync
            def _(sp):
                for j in range(2):
                    sp.wait_ge(once["fin_dve"], 1 + 4 * (j + 1))
                    sp.dma_start(y_out[:, 4 * j:4 * j + 4, :], ret[:, 4 * j:4 * j + 4, :]).then_inc(once["stored"], 16)
                sp.wait_ge(once["stored"], 32)


def _weight_stream(a, l):
    def tiles(w):
        k, m = w.shape
        return w.reshape(k // P, P, m // P, P).transpose(1, 2, 0, 3)

    out = {}

    def pair(name, w):
        for o in range(w.shape[1]):
            out[f"{name}.{o}"] = w[:, o]

    for f in (1, 2):
        g, u, d = (tiles(a[f"ffn{f}_{n}"][l]) for n in ("w_gate", "w_up", "w_down"))
        for m in range(MF):
            pair(f"gu{f}_{m}", np.stack([g[:, m], u[:, m]], axis=1))
        for j in range(4):
            for o in range(2):
                for n, (k0, k1) in enumerate(DOWN_K):
                    out[f"dn{f}_{j}.{3 * o + n}"] = d[:, 2 * j + o, k0:k1]
    w = a["w_in"][l]
    offs = np.cumsum([0, 768, 256, 4, 4, 256, 256, 256, 256, 256, 256, 256, 4096])
    col = {n: w[:, offs[i]:offs[i + 1]] for i, n in enumerate(["qkv", "z", "b", "a", "su", "lx", "ly", "rq", "rk", "rv", "rg", "g"])}
    ba = np.zeros((DM, P), np.float32)
    for r in (0, 64, 96):
        ba[:, r:r + 4] = col["a"]
    ba[:, 32:36] = col["b"]
    pair("ba", tiles(ba))
    for i in range(3):
        pair(f"qkv{i}", tiles(col["qkv"][:, 256 * i:256 * i + 256]))
    for n in ("z", "su", "lx", "ly", "rq", "rk", "rg", "rv"):
        pair(n, tiles(col[n]))
    for i in range(16):
        pair(f"g{i}", tiles(col["g"][:, 256 * i:256 * i + 256]))
    wb = a["w_branch"][l].reshape(NB, 2, P, KD, P).transpose(2, 3, 0, 1, 4).reshape(P, KD, NB * 2, P)
    wo = tiles(a["w_out"][l])
    for m in range(KD):
        out[f"mg{m}.0"] = wb[:, m]
    for i in range(4):
        pair(f"wo{i}", wo[:, 2 * i:2 * i + 2])
    return np.concatenate([np.ascontiguousarray(out[n]).reshape(-1) for n, _, _ in PIECES])


def _params(a, l):
    p = np.zeros((P, NPAR), np.float32)

    def put(name, v):
        lo, hi = PCOLS[name]
        p[:, lo:hi] = v.reshape(P, hi - lo)

    feat = lambda v: v.reshape(-1, P).T
    put("n1", feat(a["ffn1_norm"][l]))
    put("nm", feat(a["mix_norm"][l]))
    put("n2", feat(a["ffn2_norm"][l]))
    put("gconv", feat(a["gdn_conv_w"][l]))
    for name, v in (("dtb", a["gdn_dt_bias"][l]), ("alog", a["gdn_a_log"][l])):
        for r in (0, 64, 96):
            p[r:r + 4, PCOLS[name][0]] = v
    put("gnorm", np.concatenate([a["gdn_norm_w"][l]] * 2))
    put("lre", feat(a["s5_lambda_re"][l]))
    put("lim", feat(a["s5_lambda_im"][l]))
    put("ldt", feat(np.repeat(a["s5_log_dt"][l], 64)))
    put("s5d", feat(a["s5_d"][l]))
    put("bglu", feat(a["s5_b_glu"][l]))
    put("lconv", feat(a["lru_conv_w"][l]))
    put("lcb", feat(a["lru_conv_b"][l]))
    put("lba", feat(a["lru_b_a"][l]))
    put("lbi", feat(a["lru_b_i"][l]))
    put("lam", feat(a["lru_lambda"][l]))
    put("rnorm", feat(a["ret_norm_w"][l]))
    for name, b in (("sbr", a["s5_b_re"][l]), ("sbi", a["s5_b_im"][l])):
        w = np.zeros((P, 2, P), np.float32)
        for g in range(16):
            w[16 * (g % 8):16 * (g % 8) + 16, g // 8, 64 * (g % 2):64 * (g % 2) + 64] = b[g].T
        put(name, w)
    for name, c in (("scr", a["s5_c_re"][l]), ("sci", a["s5_c_im"][l])):
        w = np.zeros((P, NST, 32), np.float32)
        for g in range(16):
            w[64 * (g % 2):64 * (g % 2) + 64, g // 2, 16 * (g % 2):16 * (g % 2) + 16] = c[g].T
        put(name, w)
    put("wglu", a["s5_w_glu"][l].reshape(2, P, 256).transpose(1, 0, 2))
    for name, b in (("wa", a["lru_w_a"][l]), ("wi", a["lru_w_i"][l])):
        w = np.zeros((P, 2, P), np.float32)
        for n in range(4):
            r = 64 * (n % 2)
            w[r:r + 64, n // 2, r:r + 64] = b[n]
        put(name, w)
    return p


def _constants(fnorm):
    c = np.zeros((P, NCST), np.float32)

    def put(name, v):
        lo, hi = CCOLS[name]
        c[:, lo:hi] = np.asarray(v, np.float64).reshape(P, hi - lo)

    i = np.arange(P)
    put("ident", np.eye(P))
    put("one", np.ones(P))
    put("bo", (i[:, None] // 64 == i[None] // 64) / 64.0)
    put("incl", (i[:, None] // 64 == i[None] // 64) & (i[:, None] <= i[None]))
    lev = []
    for s in (1, 2, 4, 8, 16, 32):
        m, cc = i[:, None], i[None]
        lev.append((m // (2 * s) == cc // (2 * s)) & (m % (2 * s) < s) & (cc % (2 * s) >= s))
    put("lev", np.stack(lev, axis=1))
    perm = np.zeros((P, P))
    for r in range(P):
        if r % 64 < 32:
            perm[r + 32, r] = -1.0
        else:
            perm[r - 32, r] = 1.0
    put("perm", perm)
    rmask = np.zeros((P, 4, SEQ))
    for h in range(4):
        lg = np.log1p(-np.exp2(-5.0 - h))
        m, q = i[:, None], np.arange(SEQ)[None]
        rmask[:, h] = np.where(q >= m, np.exp(np.maximum(q - m, 0) * lg), 0.0) * DH ** -0.5
    put("rmask", rmask)
    put("freq", (10000.0 ** (-(i % 32) / 32.0)))
    lo, hi = CCOLS["fnorm"]
    c[:, lo:hi] = fnorm.reshape(KD, P).T
    return c


def kernel(**inputs):
    import concourse.bacc as _bacc
    from concourse import mybir as _mybir
    from concourse.bass_utils import run_bass_kernel_spmd as _run

    a = {k: np.asarray(v) for k, v in inputs.items()}
    arrays = {
        "weights": np.stack([_weight_stream(a, l) for l in range(DEPTH)]),
        "params": np.stack([_params(a, l) for l in range(DEPTH)]),
        "consts": _constants(a["final_norm"]),
        "positions": np.ascontiguousarray(np.broadcast_to(a["positions"].reshape(1, SEQ), (P, SEQ))),
        "x_in": np.ascontiguousarray(a["x"].reshape(SEQ, KD, P).transpose(2, 1, 0)),
    }
    nc = _bacc.Bacc("TRN2", target_bir_lowering=False, num_devices=1)
    args = [nc.dram_tensor(n, v.shape, _mybir.dt.from_np(v.dtype), kind="ExternalInput").ap() for n, v in arrays.items()]
    args.append(nc.dram_tensor("y_out", (P, KD, SEQ), F32, kind="ExternalOutput").ap())
    trunk(nc, *args)
    r = _run(nc, [arrays], core_ids=[0])
    return r.results[0]["y_out"].transpose(2, 1, 0).reshape(1, SEQ, DM)
```

```python
import math

import numpy as np
import concourse.bass as bass
from concourse import mybir
from contextlib import ExitStack

F32 = mybir.dt.float32
F32R = mybir.dt.float32r
ALU = mybir.AluOpType
ACT = mybir.ActivationFunctionType

P = 128
SEQ, DM, DFF, DEPTH = 256, 1024, 2816, 2
KD = DM // P
MF = DFF // P
NB = 4
NH, DH = 4, 64
NCH = SEQ // 64
NST = 8
EPS = 1e-6
RAW_SLOTS = 3
SLOTS = 4
SLOT = 1024
LEVELS = 6
GELU_C = math.sqrt(2.0 / math.pi)
TWO_PI = 2.0 * math.pi
ROUND = 12582912.0
GRID = 384.0
PI_C = [float(np.float32(x)) for x in (6.28125, 0.0019350051879882812, 3.0199159819567e-07)]
PI_SAFE = 3.1415925
SIN_SCALE = 6.283185

PCOLS = {}
_at = 0
for _name, _n in [("n1", 8), ("nm", 8), ("n2", 8), ("gconv", 24), ("dtb", 1), ("alog", 1), ("gnorm", 1),
                  ("lre", 8), ("lim", 8), ("ldt", 8), ("s5d", 2), ("bglu", 2), ("lconv", 8), ("lcb", 2),
                  ("lba", 2), ("lbi", 2), ("lam", 2), ("rnorm", 2), ("sbr", 256), ("sbi", 256),
                  ("scr", 256), ("sci", 256), ("wglu", 512), ("wa", 256), ("wi", 256)]:
    PCOLS[_name] = (_at, _at + _n)
    _at += _n
NPAR = _at
NORMS = PCOLS["gconv"][0]

CCOLS = {}
_at = 0
for _name, _n in [("ident", 128), ("one", 1), ("freq", 1), ("fnorm", 8), ("bo", 128), ("incl", 128),
                  ("lev", 128 * LEVELS), ("perm", 128), ("rmask", 4 * 256)]:
    CCOLS[_name] = (_at, _at + _n)
    _at += _n
NCST = _at
EARLY = CCOLS["bo"][0]

PROJ = ["ba", "qkv0", "qkv1", "qkv2", "lx", "ly", "su", "z", "rq", "rk", "rg", "rv"]
SLAB = 53152

DOWN_K = [(0, 8), (8, 15), (15, 22)]


def _pieces():
    out = []

    def pair(name):
        out.extend([(f"{name}.0", 8, None), (f"{name}.1", 8, name)])

    def first_two(a, b):
        out.extend((f"{name}.{o}", 8, name if o else None) for o in range(2) for name in (a, b))

    def ffn(f):
        first_two(f"gu{f}_0", f"gu{f}_1")
        for m in range(2, MF):
            pair(f"gu{f}_{m}")
        for j in range(4):
            for o in range(2):
                for n, (a, b) in enumerate(DOWN_K):
                    if j == 3:
                        unit = f"dn{f}_3{'ab'[o]}" if n == 2 else None
                    else:
                        unit = f"dn{f}_{j}" if (o, n) == (1, 2) else None
                    out.append((f"dn{f}_{j}.{3 * o + n}", b - a, unit))

    ffn(1)
    for name in PROJ:
        if name == "ba":
            out.append(("ba.0", 8, "ba"))
        else:
            pair(name)
    for i in range(16):
        pair(f"g{i}")
    for m in range(KD):
        out.append((f"mg{m}.0", 8, f"mg{m}b"))
    first_two("wo0", "wo1")
    pair("wo2")
    out.extend([("wo3.0", 8, "wo3a"), ("wo3.1", 8, "wo3b")])
    ffn(2)
    return out


PIECES = _pieces()
PIECE_INDEX = {name: i for i, (name, _, _) in enumerate(PIECES)}
UNIT_PIECES = {}
for _i, (_name, _, _) in enumerate(PIECES):
    UNIT_PIECES.setdefault(_name.split(".")[0], []).append(_i)
UNIT_ORDER = list(UNIT_PIECES)
STREAM = PIECES[RAW_SLOTS:] + PIECES[:RAW_SLOTS]
PIECE_AT = {}
_at = 0
for _name, _n, _ in STREAM:
    PIECE_AT[_name] = _at
    _at += P * P * _n

BY_POOL = [i for i, (_n, _, _) in enumerate(PIECES)
           if _n.startswith("mg") or (_n.split(".")[0] in PROJ[1:] + ["g0", "g1", "g2", "g3"] and _n.endswith(".1"))
           or _n in [f"g{_k}.1" for _k in range(11, 16)] + ["gu1_0.0", "rv.0", "g0.0", "g1.0", "wo0.0", "wo1.0"]]
BY_DVE = [i for i in range(len(PIECES)) if i not in BY_POOL]

MAIN = ([("inv1", "dve")] + [(f"gu1_{m}", "dve") for m in range(MF)] + [(f"dn1_{j}", "dve") for j in ("0", "1", "2", "3a", "3b")]
        + [("invm", "dve")] + [(n, "act") for n in PROJ] + [(f"g{i}", "act") for i in range(16)]
        + [(f"mg{m}{ab}", "dve") for m in range(KD) for ab in "ab"] + [(f"wo{i}", "dve") for i in ("0", "1", "2", "3a", "3b")]
        + [("inv2", "dve")] + [(f"gu2_{m}", "dve") for m in range(MF)] + [(f"dn2_{j}", "dve") for j in ("0", "1", "2", "3a", "3b")])
LEVEL_UNITS = [()] + [("xt", "ty")] * (LEVELS - 2) + [("ty",)]
SIDE = ([("lr", "act"), ("li", "act"), ("l2q", "act"), ("l2k", "act"), ("rowt", "act"), ("eb", "act"),
         ("ktr", "dve"), ("vtr", "dve")]
        + [(n, "dve") for n in ("gb0", "gb1", "kk0", "bb0", "kk1", "bb1", "qk0", "qk1")]
        + [u for lv in range(LEVELS) for u in
           ([(f"t0_{lv}", "act"), (f"t1_{lv}", "act")]
            + [(f"{n}{hp}_{lv}", "dve") for hp in range(2) for n in LEVEL_UNITS[lv]]
            + [(f"pq{s}", "dve") for s in ([2 * lv, 2 * lv + 1] if lv < 4 else [])]
            + ([("rotq", "dve"), ("rotk", "dve")] if lv == 4 else []))]
        + [("u", "act"), ("w", "act"),
           ("su0", "dve"), ("sc0", "dve"), ("sc1", "dve"),
           ("ws1", "dve"), ("oi1", "act"), ("su1", "dve"), ("sc2", "dve"), ("sc3", "dve"),
           ("ws2", "dve"), ("oi2", "act"), ("su2", "dve"), ("ro", "act"),
           ("ws3", "dve"), ("oi3", "act"), ("glu", "act"), ("rm", "dve"),
           ("oa0", "dve"), ("oa1", "dve"), ("gs", "act"), ("rv2", "act")])


class Units:

    def __init__(self, order, banks):
        self.order, self.banks = order, banks
        self.index = {name: i for i, (name, _) in enumerate(order)}

    def bank(self, name):
        return self.banks[self.index[name] % len(self.banks)]

    def ready(self, name):
        return self.index[name] + 1

    def previous(self, name):
        i = self.index[name] - len(self.banks)
        return self.order[i] if i >= 0 else None

    def taken(self, name):
        i = self.index[name]
        return sum(1 for _, e in self.order[:i + 1] if e == self.order[i][1])


def trunk(nc, weights, params, consts, positions, x_in, y_out):
    ctx = ExitStack()
    with ctx:
        base = -(-nc.sbuf_base // 32) * 32
        ctx.enter_context(nc.sbuf_tensor("slab", [P, SLAB + 8], F32))
        place = {"": 0}

        def sb(name, cols, dt=F32, over=None, skip=0):
            if over is None:
                place[name] = place[""]
                place[""] += -(-cols // 8) * 8
                assert place[""] <= SLAB, place[""]
            else:
                place[name] = place[over] + skip
            return nc.alloc_sbuf_tensor_at(name, [P, cols], dt, offset=base + 4 * place[name])

        def two(name, n=2, t=SEQ, dt=F32, over=None, skip=0):
            return sb(name, n * t, dt, over, skip)[:].rearrange("p (k t) -> p k t", k=n)

        x = sb("x", KD * SEQ)[:].rearrange("p (k t) -> p k t", k=KD)
        xh, xl = two("xh", KD, dt=F32R), two("xl", KD, dt=F32R)
        raw = sb("raw", RAW_SLOTS * SLOT)
        whi, wlo = sb("whi", SLOTS * SLOT, F32R), sb("wlo", SLOTS * SLOT, F32R)
        cst = sb("cst", NCST)
        par = sb("par", NPAR)
        wide = sb("wide", 32 * SEQ)[:].rearrange("p (k t) -> p k t", k=32)
        hh = two("hh", MF, dt=F32R, over="wide")
        gates = wide
        griffin = wide[:, 30:32, :]
        cosE = wide[:, 22:30, :]
        sinE = sb("sinE", 8 * SEQ)[:].rearrange("p (k t) -> p k t", k=8)

        qkvp = two("qkvp", 6, SEQ + 3)
        qkv = two("qkv", 6)
        zz, su, ly = two("zz"), two("su"), two("ly")
        lxp = two("lxp", 2, SEQ + 3)
        ret = two("ret", 8)
        rq, rk, rg, rv = (ret[:, 2 * i:2 * i + 2, :] for i in range(4))
        flat8 = two("flat8", 8)
        brh = sb("brh", 8 * SEQ, F32R, over="flat8")[:].rearrange("p (n k t) -> p n k t", n=NB, k=2)
        big = sb("big", 24 * SEQ)
        hl = two("hl", MF, dt=F32R, over="big")

        def mats(i):
            return big[:, i * 8 * P:(i + 1) * 8 * P].rearrange("p (h t j c) -> p h t j c", h=2, t=2, j=2)

        dec, attn, low, my, mx, mt = (mats(i) for i in range(6))
        lowc = dec
        flat = lambda m: m.rearrange("p h t j c -> p h (t j c)")
        kbe, kdec, vb = (qkvp[:, 2 * i:2 * i + 2, 3:] for i in range(3))
        uu = big[:, 22 * SEQ:24 * SEQ].rearrange("p (k t) -> p k t", k=2)
        wT = big[:, 8 * SEQ:10 * SEQ].rearrange("p (k t) -> p k t", k=2)
        state = big[:, 10 * SEQ:11 * SEQ].rearrange("p (t c) -> p t c", t=2)
        egb, qdec = two("egb"), two("qdec")
        rows, rowT = two("rows", 1)[:, 0, :], two("rowT", 2, P)
        tmpA, tmpB, tmpC, tmpD, tmpE, tmpF = (two("tmp" + c) for c in "ABCDEF")
        brl = [two("brl0", dt=F32R, over="qkv"), two("brl1", dt=F32R, over="qkv", skip=2 * SEQ),
               two("brl2", dt=F32R, over="egb"), two("brl3", dt=F32R, over="qkv", skip=4 * SEQ)]
        small = sb("small", 176)
        ropec, ropes = two("ropec", 1)[:, 0, :], two("ropes", 1)[:, 0, :]
        mx_sq = mx.rearrange("p h t j c -> p (h t j c)").rearrange("p (k t) -> p k t", k=4)
        turns_a, turns_b = flat8, ret
        squared = flat8
        s5n = lxp[:, :, 3:]
        go = ly
        scm = big[:, 16 * SEQ:16 * SEQ + 4 * 384].rearrange("p (h c) -> p h c", h=4)

        psum = [ctx.enter_context(nc.psum_tensor(f"bank{i}", [P, 512], F32)) for i in range(8)]
        main = Units(MAIN, psum[0:4])
        side = Units(SIDE, psum[4:7])
        ybank = psum[7]
        sum_banks = psum[6:8]

        once = {n: nc.alloc_semaphore(n) for n in (
            "small_loads", "x_load", "norms", "first0", "first1", "first2", "par", "tables_load", "pre_dve", "remainders",
            "squares_in", "squares_added", "sums_in", "rms_in", "pre_act", "pre_pool", "fin_dve", "fin_pe", "stored")}
        per_layer = {}

        def S(name):
            if name not in per_layer:
                per_layer[name] = nc.alloc_semaphore(name)
            return per_layer[name]

        def par_(name, a=0, b=None):
            lo, hi = PCOLS[name]
            return par[:, lo + a:(lo + b if b is not None else hi)]

        def cst_(name, a=0, b=None):
            lo, hi = CCOLS[name]
            return cst[:, lo + a:(lo + b if b is not None else hi)]

        def halves(ap, n=2):
            return ap.rearrange("p (k t) -> p k t", k=n)

        def over(ap, n):
            return ap.unsqueeze(1).to_broadcast([P, n, ap.shape[-1]])

        ident, bo = cst_("ident"), cst_("bo")
        sm = {}
        for i, n in enumerate(["dt", "lrdt", "th", "mag", "n1", "r1", "r2", "sn", "cs", "ai", "nr", "den", "cre",
                               "cim", "ph", "phl", "t1", "t2"]):
            sm[n] = small[:, 8 * i:8 * i + 8]
        eps_col, scratch = small[:, 150:151], small[:, 149:150]
        rms_col, inv_rms = small[:, 172:174], small[:, 174:176]
        one_col = cst_("one")
        nega = small[:, 151:152]
        gnh = small[:, 152:153]
        rnh = small[:, 154:156]
        hba, hbi, hbg = small[:, 156:158], small[:, 158:160], small[:, 160:162]
        sp4, ly_, ls_, ls2, lq = (small[:, 162 + 2 * i:164 + 2 * i] for i in range(5))

        def piece_used(i):
            if PIECES[i][2]:
                return S("main"), main.ready(PIECES[i][2])
            return S("part"), sum(1 for _, _, unit in PIECES[:i + 1] if unit is None)

        def low_ready(i):
            name, mine = ("low_pool", BY_POOL) if i in BY_POOL else ("low_dve", BY_DVE)
            return S(name), mine.index(i) + 1

        def slot(ring, i):
            s0 = (i % (RAW_SLOTS if ring is raw else SLOTS)) * SLOT
            return ring[:, s0:s0 + P * PIECES[i][1]]

        def weight_piece(layer, i):
            name, n, _ = PIECES[i]
            at = PIECE_AT[name]
            return weights[bass.ds(layer, 1), at:at + P * P * n].rearrange("a (p n) -> (a p) n", p=P)

        def r32(ap):
            return ap.bitcast(F32)

        with nc.Block() as block:
            @block.sync
            def _(sp):
                ahead = params[DEPTH - 1:DEPTH, :, :].rearrange("a p n -> (a p) n")
                sp.dma_start(ropec.bitcast(mybir.dt.int32), positions).then_inc(once["small_loads"], 16)
                sp.dma_start(cst[:, 0:EARLY], consts[:, 0:EARLY]).then_inc(once["small_loads"], 16)
                sp.dma_start(x, x_in).then_inc(once["x_load"], 16)
                sp.dma_start(par[:, 0:NORMS], ahead[:, 0:NORMS]).then_inc(once["norms"], 16)
                for i in range(RAW_SLOTS):
                    sp.dma_start(slot(raw, i), weight_piece(DEPTH - 1, i)).then_inc(once[f"first{i}"], 16)
                sp.dma_start(par[:, NORMS:], ahead[:, NORMS:]).then_inc(once["par"], 16)
                sp.dma_start(cst[:, EARLY:], consts[:, EARLY:]).then_inc(once["tables_load"], 16)

            @block.gpsimd
            def _(pool):
                nc.gpsimd.memset(qkvp[:, :, 0:3], 0.0)
                nc.gpsimd.memset(lxp[:, :, 0:3], 0.0)
                nc.gpsimd.memset(rows, 0.0)
                nc.gpsimd.memset(eps_col, EPS).then_inc(once["pre_pool"], 1)

            @block.vector
            def _(dve):
                n = [0]

                def link(ins):
                    n[0] += 1
                    ins.then_inc(once["pre_dve"], 1)
                    dve.wait_ge(once["pre_dve"], n[0])

                ang, t, r = tmpA[:, 0, :], tmpB, tmpC
                dve.wait_ge(once["small_loads"], 32)
                link(nc.vector.tensor_copy(ang, ropec.bitcast(mybir.dt.int32)))
                link(nc.vector.tensor_scalar(ang, ang, cst_("freq"), None, ALU.mult))
                nc.vector.tensor_scalar(t[:, 0, :], ang, 1.0 / TWO_PI, None, ALU.mult)
                link(nc.vector.tensor_scalar(t[:, 1, :], ang, 1.0 / TWO_PI, 0.25, ALU.mult, ALU.add))
                link(nc.vector.tensor_scalar(t, t, ROUND, -ROUND, ALU.add, ALU.add))
                link(nc.vector.scalar_tensor_tensor(r, t, -PI_C[0], over(ang, 2), ALU.mult, ALU.add))
                link(nc.vector.scalar_tensor_tensor(r, t, -PI_C[1], r, ALU.mult, ALU.add))
                link(nc.vector.scalar_tensor_tensor(r, t, -PI_C[2], r, ALU.mult, ALU.add))
                link(nc.vector.tensor_scalar(r[:, 1, :], r[:, 1, :], TWO_PI / 4, None, ALU.add))
                nc.vector.tensor_scalar(r, r, PI_SAFE, -PI_SAFE, ALU.min, ALU.max).then_inc(once["remainders"], 1)
                dve.wait_ge(once["squares_in"], 2)
                nc.vector.tensor_tensor(squared[:, 0:4, :], squared[:, 0:4, :], squared[:, 4:8, :], ALU.add).then_inc(once["squares_added"], 1)
                dve.wait_ge(once["squares_added"], 1)
                nc.vector.tensor_tensor(squared[:, 0:2, :], squared[:, 0:2, :], squared[:, 2:4, :], ALU.add).then_inc(once["squares_added"], 1)
                dve.wait_ge(once["rms_in"], 1)
                nc.vector.reciprocal(inv_rms, rms_col)

            @block.scalar
            def _(act):
                act.wait_ge(once["x_load"], 16)
                for j in range(2):
                    nc.scalar.activation(squared[:, 4 * j:4 * j + 4, :], x[:, 4 * j:4 * j + 4, :], ACT.Square).then_inc(once["squares_in"], 1)
                act.wait_ge(once["remainders"], 1)
                nc.scalar.activation(ropes, tmpC[:, 0, :], ACT.Sin)
                nc.scalar.activation(ropec, tmpC[:, 1, :], ACT.Sin).then_inc(once["pre_act"], 1)
                act.wait_ge(once["pre_pool"], 1)
                nc.scalar.activation(scratch, eps_col, ACT.Sqrt)
                act.wait_ge(once["sums_in"], 1)
                for j in range(2):
                    last = nc.scalar.activation(rms_col[:, j:j + 1], psum[j][:, 0:1], ACT.Sqrt, bias=eps_col, scale=1.0 / DM)
                last.then_inc(once["rms_in"], 1)

            @block.tensor
            def _(pe):
                pe.wait_ge(once["small_loads"], 32)
                pe.wait_ge(once["squares_added"], 2)
                for j in range(2):
                    for k in range(2):
                        last = nc.tensor.matmul(psum[j][:, 0:1], squared[:, k, j * P:(j + 1) * P], one_col, start=(k == 0), stop=(k == 1))
                last.then_inc(once["sums_in"], 1)

        with nc.Fori(0, DEPTH) as layer:
            with nc.Block() as block:
                @block.sync
                def _(sp):
                    for i in range(RAW_SLOTS, len(PIECES)):
                        sp.wait_ge(*low_ready(i - RAW_SLOTS))
                        sp.dma_start(slot(raw, i), weight_piece(layer, i)).then_inc(S(f"raw{i % RAW_SLOTS}"), 16)
                    sp.wait_ge(S("normed_dve"), 3 * KD // 2)
                    sp.wait_ge(S("main_dve"), main.taken("inv2"))
                    sp.dma_start(par[:], params[bass.ds(layer, 1), :, :].rearrange("a p n -> (a p) n")).then_inc(S("next"), 16)
                    for i in range(RAW_SLOTS):
                        last = max(n for n in range(len(PIECES)) if n % RAW_SLOTS == i)
                        sp.wait_ge(*low_ready(last))
                        sp.dma_start(slot(raw, i), weight_piece(layer, i)).then_inc(S("next"), 16)
                    sp.wait_ge(S("next"), 16 * (1 + RAW_SLOTS))

                @block.tensor
                def _(pe):
                    mm = nc.tensor.matmul

                    def piece(name):
                        i = PIECE_INDEX[name]
                        pe.wait_ge(*low_ready(i))
                        return [slot(ring, i).rearrange("p (k m) -> p k m", m=P) for ring in (whi, wlo)]

                    def product(out, w, a, start, stop):
                        mm(out, w[0], a[0], start=start, stop=False)
                        mm(out, w[0], a[1], start=False, stop=False)
                        return mm(out, w[1], a[0], start=False, stop=stop)

                    def main_bank(name):
                        if main.previous(name):
                            who = main.previous(name)
                            pe.wait_ge(S(f"main_{who[1]}"), main.taken(who[0]))
                        return main.bank(name)

                    def side_bank(name):
                        if side.previous(name):
                            who = side.previous(name)
                            pe.wait_ge(S(f"side_{who[1]}"), side.taken(who[0]))
                        return side.bank(name)

                    def sums(which, ks):
                        for k in ks:
                            pe.wait_ge(S("squares"), which * 5 + (k // 2 + 1 if k < 6 else k - 2))
                            for j in range(2):
                                last = mm(sum_banks[j][:, 0:1], squared[:, k, j * P:(j + 1) * P], one_col, start=(k == 0), stop=(k == KD - 1))
                        if k == KD - 1:
                            last.then_inc(S("sums"), 1)

                    def inverse_norms(norm):
                        ps = main_bank(f"inv{norm}")
                        for j in range(2):
                            last = mm(ps[:, j * P:(j + 1) * P], inv_rms[:, j:j + 1].to_broadcast([P, P]), ident, start=True, stop=True)
                        last.then_inc(S("main"), 1)

                    def half(unit, o):
                        if f"{unit}{'ab'[o]}" in main.index:
                            ps = main_bank(f"{unit}{'ab'[o]}")[:, 0:SEQ]
                        else:
                            ps = (main_bank(unit) if o == 0 else main.bank(unit))[:, o * SEQ:(o + 1) * SEQ]
                        wh, wl = piece(f"{unit}.{o}")
                        for k in range(KD):
                            last = product(ps, (wh[:, k, :], wl[:, k, :]), (xh[:, k, :], xl[:, k, :]), k == 0, k == KD - 1)
                        last.then_inc(S("main" if PIECES[PIECE_INDEX[f"{unit}.{o}"]][2] else "part"), 1)

                    def pair(unit):
                        half(unit, 0)
                        half(unit, 1)

                    def norm_tile(which, k):
                        return S("normed_pool" if k % 2 else "normed_dve"), which * KD // 2 + k // 2 + 1

                    def first_two(units, arrived):
                        banks, tiles = [main_bank(u) for u in units], [piece(f"{u}.0") for u in units]
                        for k in range(KD):
                            pe.wait_ge(*arrived(k))
                            for u, ps, (wh, wl) in zip(units, banks, tiles):
                                last = product(ps[:, 0:SEQ], (wh[:, k, :], wl[:, k, :]), (xh[:, k, :], xl[:, k, :]), k == 0, k == KD - 1)
                                if k == KD - 1:
                                    last.then_inc(S("main" if PIECES[PIECE_INDEX[f"{u}.0"]][2] else "part"), 1)
                        for u in units:
                            if len(UNIT_PIECES[u]) > 1:
                                half(u, 1)

                    def ffn(f, which, which_after):
                        first_two([f"gu{f}_0", f"gu{f}_1"], lambda k: norm_tile(which, k))
                        for m in range(2, MF):
                            pair(f"gu{f}_{m}")
                        for j in range(4):
                            unit = f"dn{f}_{j}"
                            for o in range(2):
                                if j == 3:
                                    ps = main_bank(f"{unit}{'ab'[o]}")[:, 0:SEQ]
                                else:
                                    ps = (main_bank(unit) if o == 0 else main.bank(unit))[:, o * SEQ:(o + 1) * SEQ]
                                for n, (k0, k1) in enumerate(DOWN_K):
                                    if j and (o, n) in ((0, 1), (1, 0)):
                                        sums(which_after, [2 * (j - 1) + o])
                                    if (j, o, n) == (3, 1, 2):
                                        sums(which_after, [6])
                                    name = f"{unit}.{3 * o + n}"
                                    wh, wl = piece(name)
                                    for m in range(k0, k1):
                                        if j == 0 and o == 0:
                                            pe.wait_ge(S("hidden"), MF * (f - 1) + m + 1)
                                        last = product(ps, (wh[:, m - k0, :], wl[:, m - k0, :]), (hh[:, m, :], hl[:, m, :]),
                                                       m == 0, m == MF - 1)
                                    last.then_inc(S("main" if PIECES[PIECE_INDEX[name]][2] else "part"), 1)
                        sums(which_after, [7])

                    inverse_norms("1")
                    ffn(1, 0, 0)
                    pe.wait_ge(S("inv_rms"), 1)
                    inverse_norms("m")
                    first_two(["ba", "qkv0"], lambda k: norm_tile(1, k))
                    for unit in PROJ[2:8]:
                        pair(unit)
                    pe.wait_ge(once["par"], 16)
                    pe.wait_ge(once["tables_load"], 16)
                    pe.wait_ge(S("lru_conv"), 1)
                    xc = tmpA
                    for unit, wname in (("lr", "wa"), ("li", "wi")):
                        ps = side_bank(unit)
                        for t in range(2):
                            last = mm(ps[:, t * SEQ:(t + 1) * SEQ], par_(wname, t * P, (t + 1) * P), xc[:, t, :], start=True, stop=True)
                        last.then_inc(S("side"), 1)
                    pair("rq")
                    pair("rk")
                    for unit, q0, ev in (("l2q", 0, 1), ("l2k", 2, 2)):
                        pe.wait_ge(S("qk_sq"), ev)
                        ps = side_bank(unit)
                        for t in range(2):
                            last = mm(ps[:, t * SEQ:(t + 1) * SEQ], bo, mx_sq[:, q0 + t, :], start=True, stop=True)
                        last.then_inc(S("side"), 1)
                    pair("rg")
                    pe.wait_ge(S("rows"), 1)
                    ps = side_bank("rowt")
                    for j in range(2):
                        last = nc.tensor.transpose(ps[:, j * P:(j + 1) * P], rows[:, j * P:(j + 1) * P], ident)
                    last.then_inc(S("side"), 1)
                    ps, tiles = main_bank("rv"), [piece("rv.0"), piece("rv.1")]
                    for j in range(2):
                        c = slice(j * P, (j + 1) * P)
                        for k in range(KD):
                            wh, wl = (w.rearrange("p (k o) m -> p k (o m)", o=2)[:, k % 4, :] for w in tiles[k // 4])
                            last = product(ps[:, j * SEQ:(j + 1) * SEQ], (xh[:, k, c], xl[:, k, c]), (wh, wl), k == 0, k == KD - 1)
                            if (j, k) == (1, 3):
                                last.then_inc(S("part"), 1)
                    last.then_inc(S("main"), 1)

                    def gate(i):
                        pair(f"g{i}")

                    ps = side_bank("eb")
                    for t in range(2):
                        for hp in range(2):
                            h = 2 * t + hp
                            last = mm(ps[64 * hp:64 * hp + 64, t * SEQ:(t + 1) * SEQ], ident[:, h:h + 1].to_broadcast([P, 64]), rows, start=True, stop=True)
                    last.then_inc(S("side"), 1)
                    gate(0)
                    pe.wait_ge(S("k_normed"), 1)
                    for unit, q0 in (("ktr", 2), ("vtr", 4)):
                        ps = side_bank(unit)
                        for j in range(2):
                            for t in range(2):
                                last = nc.tensor.transpose(ps[:, j * 256 + t * P:j * 256 + (t + 1) * P], qkv[:, q0 + t, j * P:(j + 1) * P], ident)
                        last.then_inc(S("side"), 1)

                    def over_all(unit, row, hp):
                        ps = side_bank(unit)
                        for t in range(2):
                            h = 2 * t + hp
                            last = mm(ps[:, t * SEQ:(t + 1) * SEQ], ident[:, row + h:row + h + 1].to_broadcast([P, P]), rows, start=True, stop=True)
                        last.then_inc(S("side"), 1)

                    def against_k(unit, q0, hp):
                        ps = side_bank(unit)
                        r = slice(64 * hp, 64 * hp + 64)
                        for t in range(2):
                            for j in range(2):
                                c = slice(j * P, (j + 1) * P)
                                o = (t * 2 + j) * P
                                last = mm(ps[:, o:o + P], qkv[r, 2 + t, c], qkv[r, q0 + t, c], start=True, stop=True)
                        last.then_inc(S("side"), 1)

                    over_all("gb0", 0, 0)
                    over_all("gb1", 0, 1)
                    gate(1)
                    against_k("kk0", 2, 0)
                    over_all("bb0", 32, 0)
                    against_k("kk1", 2, 1)
                    over_all("bb1", 32, 1)
                    gate(2)
                    against_k("qk0", 0, 0)
                    against_k("qk1", 0, 1)
                    gate(3)

                    def s5_in(s):
                        ps = side_bank(f"pq{s}")
                        r, c = slice(32 * (s % 4), 32 * (s % 4) + 32), (s // 4) * P
                        mm(ps[:, 0:SEQ], par_("sbr", c, c + P)[r], su[r, s // 4, :], start=True, stop=True)
                        mm(ps[:, SEQ:512], par_("sbi", c, c + P)[r], su[r, s // 4, :], start=True, stop=True).then_inc(S("side"), 1)

                    def s5_out(s):
                        pe.wait_ge(S("s5x"), s + 1)
                        q = 32 * (s % 4)
                        o = ybank[q:q + 32, (s // 4) * SEQ:(s // 4 + 1) * SEQ]
                        xs = (tmpE, tmpF)[s % 2]
                        mm(o, par_("scr", s * 32, s * 32 + 32), xs[:, 0, :], start=True, stop=False, tile_position=(0, q))
                        mm(o, par_("sci", s * 32, s * 32 + 32), xs[:, 1, :], start=False, stop=True, tile_position=(0, q)).then_inc(S("s5y"), 1)

                    pe.wait_ge(S("main_act"), main.taken("su"))
                    for lv in range(LEVELS):
                        for hp in range(2):
                            if lv == 0:
                                pe.wait_ge(S("y_first"), hp + 1)
                            else:
                                pe.wait_ge(S("lowc"), 2 * lv + hp + 1)
                            if lv == 1:
                                pe.wait_ge(S("side_act"), side.taken(f"t{hp}_0"))
                            if lv > 1:
                                pe.wait_ge(S("side_dve"), side.taken(f"xt{hp}_{lv - 1}"))
                            ps = side_bank(f"t{hp}_{lv}")
                            for i in range(4):
                                t, j = i // 2, i % 2
                                if lv == 0:
                                    last = nc.tensor.transpose(ps[:, i * P:(i + 1) * P], my[:, hp, t, j, :], ident)
                                else:
                                    last = mm(ps[:, i * P:(i + 1) * P], lowc[:, hp, t, j, :], mx[:, hp, t, j, :], start=True, stop=True)
                            last.then_inc(S("side"), 1)
                        gate(4 + lv)
                        for hp in range(2):
                            if lv:
                                pe.wait_ge(S("side_act"), side.taken(f"t{hp}_{lv}"))
                            if lv > 1:
                                pe.wait_ge(S("side_dve"), side.taken(f"ty{hp}_{lv - 1}"))
                            for n in LEVEL_UNITS[lv]:
                                ps = side_bank(f"{n}{hp}_{lv}")
                                for i in range(4):
                                    t, j = i // 2, i % 2
                                    a, b = (my, mt) if n == "xt" else (mt, my)
                                    last = mm(ps[:, i * P:(i + 1) * P], a[:, hp, t, j, :], b[:, hp, t, j, :], start=True, stop=True)
                                last.then_inc(S("side"), 1)
                        if lv < 4:
                            s5_in(2 * lv)
                            s5_in(2 * lv + 1)
                        if 0 < lv < 5:
                            s5_out(2 * lv - 2)
                            s5_out(2 * lv - 1)
                        if lv == 4:
                            pe.wait_ge(S("main_act"), main.taken("rv"))
                            for unit, src in (("rotq", rq), ("rotk", rk)):
                                ps = side_bank(unit)
                                for t in range(2):
                                    last = mm(ps[:, t * SEQ:(t + 1) * SEQ], cst_("perm"), src[:, t, :], start=True, stop=True)
                                last.then_inc(S("side"), 1)
                    gate(10)
                    pe.wait_ge(S("side_dve"), side.taken(f"ty1_{LEVELS - 1}"))
                    ps = side_bank("u")
                    for h in range(NH):
                        t, hp = h // 2, h % 2
                        for j in range(2):
                            o = j * 256 + h * DH
                            last = mm(ps[:, o:o + DH], my[:, hp, t, j, :], vb[:, j, h * DH:(h + 1) * DH], start=True, stop=True)
                    last.then_inc(S("side"), 1)
                    ps = side_bank("w")
                    for h in range(NH):
                        t, hp = h // 2, h % 2
                        for j in range(2):
                            o = t * SEQ + j * P
                            last = mm(ps[64 * hp:64 * hp + 64, o:o + P], kbe[:, j, h * DH:(h + 1) * DH], my[:, hp, t, j, :], start=True, stop=True)
                    last.then_inc(S("side"), 1)

                    def state_up(n):
                        j, r = n // 2, slice(64 * (n % 2), 64 * (n % 2) + 64)
                        if n == 0:
                            pe.wait_ge(S("side_act"), side.taken("u"))
                        else:
                            pe.wait_ge(S("side_dve"), side.taken(f"ws{n}"))
                        ps = side_bank(f"su{n}")
                        for t in range(2):
                            last = mm(ps[:, t * P:(t + 1) * P], kdec[r, j, t * P:(t + 1) * P], uu[r, j, t * P:(t + 1) * P], start=True, stop=True)
                        last.then_inc(S("side"), 1)

                    def from_state(n):
                        r0 = 64 * (n % 2)
                        c = slice(64 * n, 64 * n + 64)
                        pe.wait_ge(S("side_dve"), side.taken(f"su{n - 1}"))
                        pe.wait_ge(S("side_act"), side.taken("w"))
                        ps = side_bank(f"ws{n}")
                        for t in range(2):
                            last = mm(ps[r0:r0 + 64, t * P:(t + 1) * P], wT[:, t, c], state[:, t, :], start=True, stop=True)
                        last.then_inc(S("side"), 1)
                        ps = side_bank(f"oi{n}")
                        for t in range(2):
                            last = mm(ps[:, t * 64:(t + 1) * 64], state[:, t, :], qdec[:, t, c], start=True, stop=True)
                        last.then_inc(S("side"), 1)

                    def scores(h):
                        t, r = h // 2, slice(64 * (h % 2), 64 * (h % 2) + 64)
                        ps = side_bank(f"sc{h}")
                        mm(ps[:, 0:SEQ], rk[r, t, 0:P], rq[r, t, :], start=True, stop=True)
                        mm(ps[:, SEQ:384], rk[r, t, P:SEQ], rq[r, t, P:SEQ], start=True, stop=True).then_inc(S("side"), 1)

                    def means(unit, src):
                        ps = side_bank(unit)
                        for t in range(2):
                            last = mm(ps[:, t * SEQ:(t + 1) * SEQ], bo, src[:, t, :], start=True, stop=True)
                        last.then_inc(S("side"), 1)

                    half("g11", 0)
                    state_up(0)
                    pe.wait_ge(S("rotated"), 2)
                    scores(0)
                    scores(1)
                    half("g11", 1)
                    from_state(1)
                    state_up(1)
                    scores(2)
                    scores(3)
                    half("g12", 0)
                    from_state(2)
                    state_up(2)
                    pe.wait_ge(S("side_dve"), side.taken("sc3"))
                    ps = side_bank("ro")
                    for h in range(NH):
                        t, q = h // 2, 64 * (h % 2)
                        v = slice(h * DH, (h + 1) * DH)
                        mm(ps[q:q + 64, t * SEQ:(t + 1) * SEQ], rv[:, 0, v], scm[:, h, 0:SEQ], start=True, stop=False)
                        last = mm(ps[q:q + 64, t * SEQ + P:(t + 1) * SEQ], rv[:, 1, v], scm[:, h, SEQ:384], start=False, stop=True)
                    last.then_inc(S("side"), 1)
                    half("g12", 1)
                    from_state(3)
                    pe.wait_ge(S("s5g"), 1)
                    ps = side_bank("glu")
                    for o in range(2):
                        for k in range(2):
                            c = k * 256 + o * P
                            last = mm(ps[:, o * SEQ:(o + 1) * SEQ], par_("wglu", c, c + P), tmpE[:, k, :], start=(k == 0), stop=(k == 1))
                    last.then_inc(S("side"), 1)
                    pe.wait_ge(S("side_act"), side.taken("ro"))
                    means("rm", tmpB)
                    pe.wait_ge(S("side_dve"), side.taken("ws3"))
                    for j in range(2):
                        ps = side_bank(f"oa{j}")
                        for h in range(NH):
                            t, q = h // 2, 64 * (h % 2)
                            last = mm(ps[q:q + 64, t * P:(t + 1) * P], uu[:, j, h * DH:(h + 1) * DH], attn[:, h % 2, t, j, :], start=True, stop=True)
                        last.then_inc(S("side"), 1)
                    half("g13", 0)
                    pe.wait_ge(S("go_sq"), 1)
                    means("gs", tmpD)
                    pe.wait_ge(S("ro_sq"), 1)
                    means("rv2", tmpC)
                    half("g13", 1)
                    gate(14)
                    gate(15)

                    for m in range(KD):
                        wh, wl = piece(f"mg{m}.0")
                        for ab in range(2):
                            ps = main_bank(f"mg{m}{'ab'[ab]}")
                            for n2 in range(2):
                                n = 2 * ab + n2
                                if m == 0:
                                    pe.wait_ge(S(f"branch{n}"), 1)
                                for k in range(2):
                                    last = product(ps[:, n2 * SEQ:(n2 + 1) * SEQ], (wh[:, 2 * n + k, :], wl[:, 2 * n + k, :]),
                                                   (brh[:, n, k, :], brl[n][:, k, :]), k == 0, k == 1)
                            last.then_inc(S("main"), 1)
                    first_two(["wo0", "wo1"], lambda k: (S("merged"), k + 1))
                    half("wo2", 0)
                    sums(1, [0])
                    half("wo2", 1)
                    sums(1, [1, 2])
                    half("wo3", 0)
                    sums(1, [3, 4, 5])
                    half("wo3", 1)
                    sums(1, [6, 7])
                    pe.wait_ge(S("inv_rms"), 2)
                    inverse_norms("2")
                    ffn(2, 2, 2)

                @block.scalar
                def _(act):
                    A = nc.scalar.activation
                    chain = [0]

                    def link(ins):
                        chain[0] += 1
                        ins.then_inc(S("act"), 1)
                        act.wait_ge(S("act"), chain[0])

                    split = [0]

                    def split_to(n):
                        for i in range(split[0], min(n, len(PIECES))):
                            if i < RAW_SLOTS:
                                act.wait_ge(once[f"first{i}"], 16)
                            else:
                                act.wait_ge(S(f"raw{i % RAW_SLOTS}"), 16 * (i // RAW_SLOTS))
                            if i >= SLOTS:
                                act.wait_ge(*piece_used(i - SLOTS))
                            A(slot(whi, i), slot(raw, i), ACT.Copy).then_inc(S("high"), 1)
                        split[0] = max(split[0], n)

                    def ahead(unit):
                        split_to(UNIT_PIECES[unit][-1] + 3)

                    def squares(which):
                        name = ("dn1_", "wo", "dn2_")[which]
                        for unit, tiles in ((f"{name}0", slice(0, 2)), (f"{name}1", slice(2, 4)), (f"{name}2", slice(4, 6)),
                                            (f"{name}3a", slice(6, 7)), (f"{name}3b", slice(7, 8))):
                            if tiles.start == 6:
                                split_to(UNIT_PIECES[f"{name}3"][-1])
                            else:
                                ahead(unit.rstrip("b"))
                            if tiles.start == 7:
                                A(scratch, eps_col, ACT.Sqrt)
                            act.wait_ge(S("main_dve"), main.taken(unit))
                            A(squared[:, tiles, :], x[:, tiles, :], ACT.Square).then_inc(S("squares"), 1)

                    def high_inputs(norm, which):
                        for k in range(KD):
                            if k < KD - 1:
                                act.wait_ge(S("xf"), which * (KD - 1) + k + 1)
                            else:
                                act.wait_ge(S("main_dve"), main.taken(f"inv{norm}"))
                            A(xh[:, k, :], flat8[:, k, :], ACT.Copy).then_inc(S("xh"), 1)
                            if k % 4 == 3:
                                split_to(split[0] + 1)

                    def high_merged():
                        for k in range(KD):
                            split_to(UNIT_PIECES[f"mg{k}"][-1] + 5)
                            act.wait_ge(S("summed"), k + 1)
                            A(xh[:, k, :], ret[:, k, :], ACT.Copy).then_inc(S("sum_high"), 1)

                    def rms(which):
                        act.wait_ge(S("sums"), which + 1)
                        for j in range(2):
                            last = A(rms_col[:, j:j + 1], sum_banks[j][:, 0:1], ACT.Sqrt, bias=eps_col, scale=1.0 / DM)
                        last.then_inc(S("rms"), 1)

                    def high_hidden(f, m):
                        act.wait_ge(S("main_dve"), main.taken(f"gu{f}_{m}"))
                        A(hh[:, m, :], tmpC[:, m % 2, :], ACT.Copy).then_inc(S("hh"), 1)

                    def silus(f, ms):
                        for m in ms:
                            ahead(f"gu{f}_{m}")
                            act.wait_ge(S("main"), main.ready(f"gu{f}_{m}"))
                            if m >= 2:
                                act.wait_ge(S("main_dve"), main.taken(f"gu{f}_{m - 2}"))
                            A(tmpB[:, m % 2, :], main.bank(f"gu{f}_{m}")[:, 0:SEQ], ACT.Silu).then_inc(S(f"silu{f}"), 1)
                            if m:
                                high_hidden(f, m - 1)
                        if m == MF - 1:
                            high_hidden(f, m)

                    split_to(2)
                    high_inputs("1", 0)
                    act.wait_ge(once["par"], 16)
                    A(sm["dt"], par_("ldt"), ACT.Exp)
                    A(nega, par_("alog"), ACT.Exp)
                    link(A(lq, par_("lam"), ACT.Abs))
                    A(ly_, lq, ACT.Exp, scale=-1.0).then_inc(S("pexp"), 1)
                    act.wait_ge(S("pmul"), 1)
                    A(sm["mag"], sm["lrdt"], ACT.Exp).then_inc(S("pexp"), 1)
                    silus(1, range(0, 4))
                    act.wait_ge(S("pang"), 1)
                    A(sm["sn"], sm["r1"], ACT.Sin)
                    A(sm["cs"], sm["r2"], ACT.Sin).then_inc(S("psin"), 1)
                    silus(1, range(4, 15))
                    act.wait_ge(S("turns"), 1)
                    A(sinE, turns_a, ACT.Sin, scale=SIN_SCALE).then_inc(S("tables"), 1)
                    silus(1, range(15, 20))
                    act.wait_ge(S("turns"), 2)
                    A(cosE, turns_b, ACT.Sin, scale=SIN_SCALE).then_inc(S("tables"), 1)
                    silus(1, range(20, MF))
                    squares(0)
                    rms(0)
                    high_inputs("m", 1)

                    split_to(PIECE_INDEX["qkv1.0"] + 1)
                    act.wait_ge(S("main"), main.ready("ba"))
                    A(tmpB[:, 0, :], main.bank("ba")[:, 0:SEQ], ACT.Identity, bias=par_("dtb")).then_inc(S("main_act"), 1)
                    act.wait_ge(S("main_act"), main.taken("ba"))
                    link(A(tmpF[:, 0, :], tmpB[:, 0, :], ACT.Abs))
                    split_to(PIECE_INDEX["qkv1.1"] + 1)
                    link(A(tmpF[:, 0, :], tmpF[:, 0, :], ACT.Exp, scale=-1.0))
                    split_to(PIECE_INDEX["qkv2.0"] + 1)
                    A(tmpF[:, 1, :], tmpF[:, 0, :], ACT.Ln, bias=1.0).then_inc(S("ln1p"), 1)
                    A(tmpB[:, 1, :], tmpB[:, 0, :], ACT.Tanh, scale=0.5).then_inc(S("ln1p"), 1)
                    for i in range(3):
                        ahead(f"qkv{i}")
                        act.wait_ge(S("main"), main.ready(f"qkv{i}"))
                        A(qkvp[:, 2 * i:2 * i + 2, 3:], halves(main.bank(f"qkv{i}")[:]), ACT.Identity).then_inc(S("main_act"), 1)
                    act.wait_ge(S("gc"), 1)
                    A(tmpF[:, 0, :], tmpC[:, 0, :], ACT.Exp)
                    for n in range(NCH):
                        c = slice(64 * n, 64 * n + 64)
                        last = A(tmpF[:, 1, c], tmpC[:, 0, c], ACT.Exp, scale=-1.0, bias=tmpC[:, 0, 64 * n + 63:64 * n + 64])
                    last.then_inc(S("egc"), 1)

                    def copied(unit, dst):
                        ahead(unit)
                        act.wait_ge(S("main"), main.ready(unit))
                        A(dst, halves(main.bank(unit)[:]), ACT.Identity).then_inc(S("main_act"), 1)

                    copied("lx", lxp[:, :, 3:])
                    copied("ly", ly)
                    copied("su", su)
                    ahead("z")
                    act.wait_ge(S("conv"), 1)
                    A(qkvp[:, :, 3:], qkv, ACT.Tanh, scale=0.5).then_inc(S("conv_t"), 1)
                    copied("z", zz)
                    act.wait_ge(S("main_act"), main.taken("z"))
                    A(tmpE, zz, ACT.Tanh, scale=0.5).then_inc(S("zt"), 1)
                    act.wait_ge(S("silu_q"), 1)
                    A(mx_sq[:, 0:2, :], qkv[:, 0:2, :], ACT.Square, scale=0.5).then_inc(S("qk_sq"), 1)
                    A(mx_sq[:, 2:4, :], qkv[:, 2:4, :], ACT.Square, scale=0.5).then_inc(S("qk_sq"), 1)
                    ahead("rq")
                    for unit, dst, hb in (("lr", tmpB, hba), ("li", tmpD, hbi)):
                        act.wait_ge(S("side"), side.ready(unit))
                        A(dst[:, 0, :], side.bank(unit)[:, 0:SEQ], ACT.Tanh, scale=0.5, bias=hb[:, 0:1])
                        A(dst[:, 1, :], side.bank(unit)[:, SEQ:512], ACT.Tanh, scale=0.5, bias=hb[:, 1:2]).then_inc(S("side_act"), 1)
                    act.wait_ge(S("log_a"), 1)
                    A(tmpF, tmpC, ACT.Exp, scale=2.0)
                    A(tmpE, tmpC, ACT.Tanh, scale=-1.0).then_inc(S("lru_t"), 1)
                    act.wait_ge(S("lru_t"), 1)
                    A(tmpC, tmpC, ACT.Exp).then_inc(S("lru_a"), 1)
                    copied("rq", rq)
                    copied("rk", rk)
                    ahead("rg")
                    for unit, dst in (("l2q", mx_sq[:, 0:2, :]), ("l2k", mx_sq[:, 2:4, :])):
                        act.wait_ge(S("side"), side.ready(unit))
                        A(dst, halves(side.bank(unit)[:]), ACT.Sqrt, scale=float(DH), bias=eps_col).then_inc(S("side_act"), 1)
                    act.wait_ge(S("lru_q"), 1)
                    A(tmpE, tmpE, ACT.Sqrt, scale=0.25).then_inc(S("lru_m"), 1)
                    copied("rg", rg)
                    ahead("rv")
                    act.wait_ge(S("gelu_in"), 1)
                    A(tmpD, tmpD, ACT.Tanh, scale=GELU_C).then_inc(S("gelu_t"), 1)
                    act.wait_ge(S("side"), side.ready("rowt"))
                    A(rowT, halves(side.bank("rowt")[:, 0:SEQ]), ACT.Identity).then_inc(S("side_act"), 1)
                    copied("rv", rv)

                    def gate(i):
                        ahead(f"g{i}")
                        act.wait_ge(S("main"), main.ready(f"g{i}"))
                        if i == 11:
                            act.wait_ge(S("s5x"), 8)
                        if i == 15:
                            act.wait_ge(S("branch2"), 1)
                        A(gates[:, 2 * i:2 * i + 2, :], halves(main.bank(f"g{i}")[:]), ACT.Tanh, scale=0.5).then_inc(S("main_act"), 1)

                    ahead("g0")
                    act.wait_ge(S("side"), side.ready("eb"))
                    A(egb, halves(side.bank("eb")[:]), ACT.Exp).then_inc(S("side_act"), 1)
                    gate(0)
                    act.wait_ge(S("griffin"), 1)
                    A(brh[:, 2], griffin, ACT.Copy).then_inc(S("branch_high"), 1)
                    ahead("g1")
                    for hp in range(2):
                        act.wait_ge(S("side_dve"), side.taken(f"gb{hp}"))
                        A(flat(dec)[:, hp, :], flat(dec)[:, hp, :], ACT.Exp).then_inc(S("dec"), 1)
                    gate(1)
                    gate(2)
                    gate(3)
                    for lv in range(LEVELS):
                        for hp in range(2):
                            act.wait_ge(S("side"), side.ready(f"t{hp}_{lv}"))
                            A(flat(mt if lv else mx)[:, hp, :], side.bank(f"t{hp}_{lv}")[:], ACT.Identity).then_inc(S("side_act"), 1)
                        gate(4 + lv)
                    gate(10)
                    act.wait_ge(S("s5gin"), 1)
                    A(tmpE, tmpE, ACT.Tanh, scale=GELU_C).then_inc(S("s5gt"), 1)
                    act.wait_ge(S("side"), side.ready("u"))
                    A(uu, halves(side.bank("u")[:]), ACT.Identity).then_inc(S("side_act"), 1)
                    act.wait_ge(S("side"), side.ready("w"))
                    A(wT, halves(side.bank("w")[:]), ACT.Identity).then_inc(S("side_act"), 1)
                    gate(11)

                    def inter(n):
                        act.wait_ge(S("side"), side.ready(f"oi{n}"))
                        A(go[:, :, 64 * n:64 * n + 64], halves(side.bank(f"oi{n}")[:, 0:P]), ACT.Identity).then_inc(S("side_act"), 1)

                    inter(1)
                    ahead("g12")
                    act.wait_ge(S("rotated"), 2)
                    A(tmpA, rg, ACT.Tanh, scale=0.5).then_inc(S("rgt"), 1)
                    inter(2)
                    act.wait_ge(S("side"), side.ready("ro"))
                    A(tmpB, halves(side.bank("ro")[:]), ACT.Identity).then_inc(S("side_act"), 1)
                    gate(12)
                    inter(3)
                    ahead("g13")
                    act.wait_ge(S("side"), side.ready("glu"))
                    A(tmpF[:, 0, :], side.bank("glu")[:, 0:SEQ], ACT.Tanh, scale=0.25, bias=hbg[:, 0:1])
                    A(tmpF[:, 1, :], side.bank("glu")[:, SEQ:512], ACT.Tanh, scale=0.25, bias=hbg[:, 1:2]).then_inc(S("side_act"), 1)
                    act.wait_ge(S("side_dve"), side.taken("rm"))
                    A(tmpC, tmpB, ACT.Square).then_inc(S("ro_sq"), 1)
                    act.wait_ge(S("side_dve"), side.taken("oa1"))
                    A(tmpD, go, ACT.Square).then_inc(S("go_sq"), 1)
                    act.wait_ge(S("side"), side.ready("gs"))
                    A(tmpD, halves(side.bank("gs")[:]), ACT.Sqrt, bias=eps_col).then_inc(S("side_act"), 1)
                    act.wait_ge(S("side"), side.ready("rv2"))
                    A(tmpC, halves(side.bank("rv2")[:]), ACT.Sqrt, bias=eps_col).then_inc(S("side_act"), 1)
                    act.wait_ge(S("s5_done"), 1)
                    A(brh[:, 1], tmpF, ACT.Copy).then_inc(S("branch_high"), 1)
                    gate(13)
                    ahead("g14")
                    gate(14)
                    gate(15)
                    high_merged()
                    squares(1)
                    rms(1)
                    high_inputs("2", 2)
                    silus(2, range(MF))
                    squares(2)
                    rms(2)

                @block.gpsimd
                def _(pool):
                    tt = nc.gpsimd.tensor_tensor

                    def low_parts(names):
                        for i in [i for i in BY_POOL if PIECES[i][0].split(".")[0] in names]:
                            pool.wait_ge(S("high"), i + 1)
                            tt(slot(wlo, i), slot(raw, i), r32(slot(whi, i)), ALU.subtract).then_inc(S("low_pool"), 1)

                    def low_inputs(which):
                        for k in range(1, KD, 2):
                            pool.wait_ge(S("xh"), which * KD + k + 1)
                            tt(xl[:, k, :], flat8[:, k, :], r32(xh[:, k, :]), ALU.subtract).then_inc(S("normed_pool"), 1)

                    def low_branch(n, src):
                        pool.wait_ge(S("branch_high"), {2: 1, 1: 2}[n])
                        tt(brl[n], src, r32(brh[:, n]), ALU.subtract).then_inc(S(f"branch{n}"), 1)

                    def level_blocks(lv):
                        for hp in range(2):
                            if lv == 0:
                                pool.wait_ge(S("side_dve"), side.taken(f"qk{hp}"))
                            elif lv == 1:
                                pool.wait_ge(S("y_first"), hp + 1)
                            else:
                                pool.wait_ge(S("side"), side.ready(f"t{hp}_{lv - 1}"))
                            tt(lowc[:, hp].rearrange("p t j c -> p (t j) c"), low[:, hp].rearrange("p t j c -> p (t j) c"),
                               over(cst_("lev", lv * P, (lv + 1) * P), 4), ALU.mult).then_inc(S("lowc"), 1)

                    def s5_back(s):
                        ss, xs = (tmpC, tmpD)[s % 2], (tmpE, tmpF)[s % 2]
                        pool.wait_ge(S("s5s"), s + 1)
                        if s >= 1:
                            pool.wait_ge(S("s5x"), s)
                        if s >= 2:
                            pool.wait_ge(S("s5y"), s - 1)
                        tt(xs, ss, over(cosE[:, s, :], 2), ALU.mult)
                        tt(s5n, ss, over(sinE[:, s, :], 2), ALU.mult).then_inc(S("pool"), 1)
                        pool.wait_ge(S("pool"), s + 1)
                        tt(xs[:, 0, :], xs[:, 0, :], s5n[:, 1, :], ALU.subtract)
                        tt(xs[:, 1, :], xs[:, 1, :], s5n[:, 0, :], ALU.add).then_inc(S("s5x"), 1)

                    ts = nc.gpsimd.tensor_scalar
                    ta, tb, tok = turns_a, turns_b, over(tmpF[:, 0, :], 8)
                    chain = [0]

                    def link(ins):
                        chain[0] += 1
                        ins.then_inc(S("turn_step"), 1)
                        pool.wait_ge(S("turn_step"), chain[0])

                    low_parts(["gu1_0"])
                    low_inputs(0)
                    pool.wait_ge(S("normed_dve"), KD // 2)
                    pool.wait_ge(S("normed_pool"), KD // 2)
                    pool.wait_ge(S("pang"), 1)
                    pool.wait_ge(S("tokens"), 1)
                    link(tt(ta, tok, sm["t1"].unsqueeze(2).to_broadcast([P, 8, SEQ]), ALU.mult))
                    link(ts(tb, ta, ROUND, -ROUND, ALU.add, ALU.add))
                    link(tt(ta, ta, tb, ALU.subtract))
                    link(tt(tb, tok, sm["phl"].unsqueeze(2).to_broadcast([P, 8, SEQ]), ALU.mult))
                    link(tt(tb, ta, tb, ALU.add))
                    link(ts(ta, tb, ROUND, -ROUND, ALU.add, ALU.add))
                    tt(ta, tb, ta, ALU.subtract).then_inc(S("turns"), 1)
                    pool.wait_ge(S("turns"), 1)
                    link(ts(tb, tb, 0.25, None, ALU.add))
                    pool.wait_ge(S("tables"), 1)
                    link(ts(ta, tb, ROUND, -ROUND, ALU.add, ALU.add))
                    tt(tb, tb, ta, ALU.subtract).then_inc(S("turns"), 1)

                    low_inputs(1)
                    low_parts(PROJ + [f"g{i}" for i in range(4)])
                    pool.wait_ge(once["tables_load"], 16)
                    level_blocks(0)
                    for hp in range(2):
                        pool.wait_ge(S("lowc"), hp + 1)
                        tt(my[:, hp].rearrange("p t j c -> p (t j) c"), over(ident, 4), lowc[:, hp].rearrange("p t j c -> p (t j) c"),
                           ALU.subtract).then_inc(S("y_first"), 1)
                    for lv in range(LEVELS):
                        if lv + 1 < LEVELS:
                            level_blocks(lv + 1)
                        if lv + 2 == LEVELS:
                            pool.wait_ge(S("lowc"), 2 * LEVELS)
                            nc.gpsimd.memset(state, 0.0).then_inc(S("state_zero"), 1)
                        if lv < 4:
                            s5_back(2 * lv)
                            s5_back(2 * lv + 1)
                    low_parts(["g11", "g12", "g13"])
                    pool.wait_ge(S("side_dve"), side.taken("su2"))
                    low_branch(2, griffin)
                    low_parts(["g14", "g15"])
                    low_branch(1, tmpF)
                    low_parts([f"mg{m}" for m in range(KD)] + ["wo0", "wo1"])
                    low_inputs(2)

                @block.vector
                def _(dve):
                    V = nc.vector
                    chain = [0]

                    def link(ins):
                        chain[0] += 1
                        ins.then_inc(S("dve"), 1)
                        dve.wait_ge(S("dve"), chain[0])

                    split = [0]

                    def split_to(n):
                        for i in [i for i in BY_DVE if split[0] <= i < n]:
                            dve.wait_ge(S("high"), i + 1)
                            V.tensor_tensor(slot(wlo, i), slot(raw, i), r32(slot(whi, i)), ALU.subtract).then_inc(S("low_dve"), 1)
                        split[0] = max(split[0], n)

                    def ahead(unit):
                        split_to(UNIT_PIECES[unit][-1] + 3)

                    def low_input(which, k):
                        if k % 2 == 0:
                            dve.wait_ge(S("xh"), which * KD + k + 1)
                            V.tensor_tensor(xl[:, k, :], flat8[:, k, :], r32(xh[:, k, :]), ALU.subtract).then_inc(S("normed_dve"), 1)

                    def inverted(which):
                        dve.wait_ge(S("rms"), which + 1)
                        V.reciprocal(inv_rms, rms_col).then_inc(S("inv_rms"), 1)

                    def normed(norm, which, wname):
                        dve.wait_ge(S("main"), main.ready(f"inv{norm}"))
                        ps = main.bank(f"inv{norm}")
                        for k in range(KD):
                            last = V.scalar_tensor_tensor(flat8[:, k, :], x[:, k, :], par_(wname, k, k + 1), ps[:, 0:SEQ], ALU.mult, ALU.mult)
                            last.then_inc(*((S("xf"), 1) if k < KD - 1 else (S("main_dve"), 1)))
                            if (which, k) == (0, 2):
                                split_to(2)
                            if k >= 2:
                                low_input(which, k - 2)
                        low_input(which, KD - 2)

                    def low_hidden(f, m):
                        dve.wait_ge(S("hh"), MF * (f - 1) + m + 1)
                        V.tensor_tensor(hl[:, m, :], tmpC[:, m % 2, :], r32(hh[:, m, :]), ALU.subtract).then_inc(S("hidden"), 1)

                    def up(f, ms):
                        for m in ms:
                            ahead(f"gu{f}_{m}")
                            dve.wait_ge(S(f"silu{f}"), m + 1)
                            if m >= 2:
                                dve.wait_ge(S("hidden"), MF * (f - 1) + m - 1)
                            ps = main.bank(f"gu{f}_{m}")
                            V.tensor_tensor(tmpC[:, m % 2, :], tmpB[:, m % 2, :], ps[:, SEQ:512], ALU.mult).then_inc(S("main_dve"), 1)
                            if m:
                                low_hidden(f, m - 1)
                        if m == MF - 1:
                            low_hidden(f, m)

                    def down(name, scale):
                        for j in range(4):
                            if j < 3:
                                ahead(f"{name}{j}")
                            else:
                                split_to(UNIT_PIECES[f"{name}3"][-1])
                            for unit, tiles in ((f"{name}{j}", slice(2 * j, 2 * j + 2)),) if j < 3 else ((f"{name}3a", slice(6, 7)), (f"{name}3b", slice(7, 8))):
                                if tiles.start == 7:
                                    ahead(f"{name}3")
                                n = tiles.stop - tiles.start
                                dve.wait_ge(S("main"), main.ready(unit))
                                V.scalar_tensor_tensor(x[:, tiles, :], halves(main.bank(unit)[:, 0:n * SEQ], n), scale, x[:, tiles, :],
                                                       ALU.mult, ALU.add).then_inc(S("main_dve"), 1)

                    dve.wait_ge(once["norms"], 16)
                    normed("1", 0, "n1")
                    split_to(3)
                    lre, lim = par_("lre"), par_("lim")
                    dve.wait_ge(once["par"], 16)
                    one = cst_("one").to_broadcast([P, SEQ])
                    V.tensor_tensor_scan(tmpF[:, 0, :], one, one, -1.0, ALU.mult, ALU.add).then_inc(S("tokens"), 1)
                    dve.wait_ge(S("pexp"), 1)
                    V.tensor_tensor(sm["lrdt"], lre, sm["dt"], ALU.mult).then_inc(S("pmul"), 1)
                    link(V.tensor_tensor(sm["th"], lim, sm["dt"], ALU.mult))
                    for r, quarter in ((sm["r1"], 0.0), (sm["r2"], 0.25)):
                        link(V.tensor_scalar(sm["n1"], sm["th"], 1.0 / TWO_PI, quarter, ALU.mult, ALU.add))
                        link(V.tensor_scalar(sm["n1"], sm["n1"], ROUND, -ROUND, ALU.add, ALU.add))
                        link(V.scalar_tensor_tensor(r, sm["n1"], -PI_C[0], sm["th"], ALU.mult, ALU.add))
                        link(V.scalar_tensor_tensor(r, sm["n1"], -PI_C[1], r, ALU.mult, ALU.add))
                        link(V.scalar_tensor_tensor(r, sm["n1"], -PI_C[2], r, ALU.mult, ALU.add))
                        link(V.tensor_scalar(r, r, quarter * TWO_PI, PI_SAFE, ALU.add, ALU.min))
                        link(V.tensor_scalar(r, r, -PI_SAFE, None, ALU.max))
                        up(1, [1 if quarter else 0])
                    link(V.tensor_scalar(sm["ph"], sm["r1"], 1.0 / TWO_PI, None, ALU.mult))
                    link(V.tensor_scalar(sm["t1"], sm["ph"], GRID, -GRID, ALU.add, ALU.add))
                    V.tensor_tensor(sm["phl"], sm["ph"], sm["t1"], ALU.subtract).then_inc(S("pang"), 1)
                    dve.wait_ge(S("pang"), 1)
                    up(1, [2])
                    dve.wait_ge(S("pmul"), 1)
                    V.tensor_scalar(nega, nega, -1.0, None, ALU.mult)
                    V.tensor_scalar(gnh, par_("gnorm"), 0.5, None, ALU.mult)
                    V.tensor_scalar(rnh, par_("rnorm"), 0.5, None, ALU.mult)
                    V.tensor_scalar(hba, par_("lba"), 0.5, None, ALU.mult)
                    V.tensor_scalar(hbi, par_("lbi"), 0.5, None, ALU.mult)
                    link(V.tensor_scalar(hbg, par_("bglu"), 0.5, None, ALU.mult))
                    link(V.tensor_scalar(ls_, ly_, 2.0, None, ALU.add))
                    link(V.reciprocal(ls_, ls_))
                    link(V.tensor_tensor(ls_, ls_, ly_, ALU.mult))
                    link(V.tensor_tensor(ls2, ls_, ls_, ALU.mult))
                    up(1, [3])
                    link(V.tensor_scalar(lq, ls2, 1.0 / 19, None, ALU.mult))
                    for k in range(17, 2, -2):
                        link(V.scalar_tensor_tensor(lq, lq, 1.0 / k, ls2, ALU.add, ALU.mult))
                    up(1, [4])
                    link(V.scalar_tensor_tensor(lq, lq, 1.0, ls_, ALU.add, ALU.mult))
                    link(V.tensor_scalar(sp4, par_("lam"), -1.0, 0.0, ALU.mult, ALU.max))
                    link(V.scalar_tensor_tensor(sp4, lq, 2.0, sp4, ALU.mult, ALU.add))
                    link(V.tensor_scalar(sp4, sp4, -4.0, None, ALU.mult))
                    up(1, [5])
                    dve.wait_ge(S("psin"), 1)
                    dve.wait_ge(S("pexp"), 2)
                    link(V.tensor_tensor(sm["ai"], sm["mag"], sm["sn"], ALU.mult))
                    link(V.tensor_tensor(sm["nr"], sm["mag"], sm["cs"], ALU.mult))
                    link(V.tensor_scalar(sm["nr"], sm["nr"], -1.0, None, ALU.add))
                    link(V.tensor_tensor(sm["den"], lre, lre, ALU.mult))
                    link(V.tensor_tensor(sm["t2"], lim, lim, ALU.mult))
                    link(V.tensor_tensor(sm["den"], sm["den"], sm["t2"], ALU.add))
                    link(V.reciprocal(sm["den"], sm["den"]))
                    up(1, [6])
                    link(V.tensor_tensor(sm["cre"], sm["nr"], lre, ALU.mult))
                    link(V.tensor_tensor(sm["t2"], sm["ai"], lim, ALU.mult))
                    link(V.tensor_tensor(sm["cre"], sm["cre"], sm["t2"], ALU.add))
                    link(V.tensor_tensor(sm["cre"], sm["cre"], sm["den"], ALU.mult))
                    link(V.tensor_tensor(sm["cim"], sm["ai"], lre, ALU.mult))
                    link(V.tensor_tensor(sm["t2"], sm["nr"], lim, ALU.mult))
                    link(V.tensor_tensor(sm["cim"], sm["cim"], sm["t2"], ALU.subtract))
                    link(V.tensor_tensor(sm["cim"], sm["cim"], sm["den"], ALU.mult))
                    up(1, [7])
                    cr, ci = halves(par_("scr"), 8), halves(par_("sci"), 8)
                    bre = sm["cre"].unsqueeze(2).to_broadcast([P, 8, 32])
                    bim = sm["cim"].unsqueeze(2).to_broadcast([P, 8, 32])
                    c1, c2 = halves(tmpD[:, 0, :], 8), halves(tmpD[:, 1, :], 8)
                    link(V.tensor_tensor(c1, ci, bim, ALU.mult))
                    link(V.tensor_tensor(c2, cr, bim, ALU.mult))
                    link(V.tensor_tensor(cr, cr, bre, ALU.mult))
                    up(1, [8])
                    link(V.tensor_tensor(cr, cr, c1, ALU.subtract))
                    link(V.tensor_tensor(ci, ci, bre, ALU.mult))
                    link(V.scalar_tensor_tensor(ci, ci, -1.0, c2, ALU.mult, ALU.subtract))
                    up(1, range(9, MF))
                    down("dn1_", 0.5)

                    inverted(0)
                    normed("m", 1, "nm")
                    split_to(PIECE_INDEX["qkv1.1"] + 1)
                    split_to(PIECE_INDEX["qkv2.0"] + 1)
                    dve.wait_ge(S("ln1p"), 1)
                    link(V.scalar_tensor_tensor(tmpC[:, 1, :], tmpB[:, 0, :], 0.0, tmpF[:, 1, :], ALU.max, ALU.add))
                    link(V.tensor_scalar(tmpC[:, 1, :], tmpC[:, 1, :], nega, None, ALU.mult))
                    for n in range(NCH):
                        c = slice(64 * n, 64 * n + 64)
                        last = V.tensor_tensor_scan(tmpC[:, 0, c], cst_("one").to_broadcast([P, 64]), tmpC[:, 1, c], 0.0, ALU.mult, ALU.add)
                    last.then_inc(S("gc"), 1)
                    split_to(PIECE_INDEX["lx.0"])
                    dve.wait_ge(S("ln1p"), 2)
                    dve.wait_ge(S("gc"), 1)
                    link(V.tensor_scalar(tmpC[:, 1, :], tmpB[:, 1, :], 1.0, 0.5, ALU.add, ALU.mult))
                    V.tensor_copy(rows[32:36, :], tmpC[32:36, 1, :])
                    link(V.tensor_copy(rows[64:68, :], tmpC[32:36, 1, :]))
                    V.tensor_copy(rows[0:4, :], tmpC[0:4, 0, :])
                    ahead("qkv2")
                    dve.wait_ge(S("egc"), 1)
                    V.tensor_tensor(rows[64:68, :], rows[64:68, :], tmpF[64:68, 0, :], ALU.mult)
                    V.tensor_copy(rows[96:100, :], tmpF[96:100, 1, :]).then_inc(S("rows"), 1)
                    ahead("lx")
                    gw = lambda k, t: par_("gconv", 6 * k + t, 6 * k + t + 1)
                    for k in range(4):
                        for t in range(6):
                            if k == 0:
                                if t % 2 == 0:
                                    dve.wait_ge(S("main_act"), main.taken(f"qkv{t // 2}"))
                                last = V.tensor_scalar(qkv[:, t, :], qkvp[:, t, 0:SEQ], gw(0, t), None, ALU.mult)
                            else:
                                last = V.scalar_tensor_tensor(qkv[:, t, :], qkvp[:, t, k:k + SEQ], gw(k, t), qkv[:, t, :], ALU.mult, ALU.add)
                        if k < 3:
                            link(last)
                        if k == 1:
                            ahead("ly")
                    last.then_inc(S("conv"), 1)
                    ahead("su")
                    xc = tmpA
                    dve.wait_ge(S("main_act"), main.taken("lx"))
                    lw = lambda k, t: par_("lconv", 2 * k + t, 2 * k + t + 1)
                    for k in range(4):
                        for t in range(2):
                            if k == 0:
                                last = V.tensor_scalar(xc[:, t, :], lxp[:, t, 0:SEQ], lw(0, t), par_("lcb", t, t + 1), ALU.mult, ALU.add)
                            else:
                                last = V.scalar_tensor_tensor(xc[:, t, :], lxp[:, t, k:k + SEQ], lw(k, t), xc[:, t, :], ALU.mult, ALU.add)
                        if k < 3:
                            link(last)
                    last.then_inc(S("lru_conv"), 1)
                    ahead("z")
                    dve.wait_ge(S("conv_t"), 1)
                    V.scalar_tensor_tensor(qkv, qkvp[:, :, 3:], 1.0, qkv, ALU.add, ALU.mult).then_inc(S("silu_q"), 1)
                    ahead("rq")
                    dve.wait_ge(S("zt"), 1)
                    V.scalar_tensor_tensor(zz, tmpE, 1.0, zz, ALU.add, ALU.mult)
                    dve.wait_ge(S("side_act"), side.taken("li"))
                    for t in range(2):
                        last = V.tensor_scalar(tmpC[:, t, :], tmpB[:, t, :], 1.0, sp4[:, t:t + 1], ALU.add, ALU.mult)
                    last.then_inc(S("log_a"), 1)
                    dve.wait_ge(S("log_a"), 1)
                    link(V.scalar_tensor_tensor(tmpB, tmpD, 1.0, xc, ALU.add, ALU.mult))
                    dve.wait_ge(S("lru_t"), 1)
                    V.scalar_tensor_tensor(tmpE, tmpF, 1.0, tmpE, ALU.add, ALU.mult).then_inc(S("lru_q"), 1)
                    ahead("rk")
                    dve.wait_ge(S("main_act"), main.taken("ly"))
                    dve.wait_ge(S("lru_q"), 1)
                    link(V.tensor_tensor(tmpD, ly, ly, ALU.mult))
                    link(V.tensor_scalar(tmpD, tmpD, 0.044715, 1.0, ALU.mult, ALU.add))
                    V.tensor_tensor(tmpD, tmpD, ly, ALU.mult).then_inc(S("gelu_in"), 1)
                    ahead("rg")
                    dve.wait_ge(S("lru_m"), 1)
                    dve.wait_ge(S("lru_a"), 1)
                    link(V.tensor_tensor(tmpB, tmpB, tmpE, ALU.mult))
                    for t in range(2):
                        last = V.tensor_tensor_scan(tmpF[:, t, :], tmpC[:, t, :], tmpB[:, t, :], 0.0, ALU.mult, ALU.add)
                    link(last)
                    dve.wait_ge(S("side_act"), side.taken("l2k"))
                    V.reciprocal(mx_sq[:, 0:2, :], mx_sq[:, 0:2, :])
                    ahead("rv")
                    link(V.reciprocal(mx_sq[:, 2:4, :], mx_sq[:, 2:4, :]))
                    V.scalar_tensor_tensor(qkv[:, 0:2, :], qkv[:, 0:2, :], 0.5 * DH ** -0.5, mx_sq[:, 0:2, :], ALU.mult, ALU.mult)
                    V.scalar_tensor_tensor(qkv[:, 2:4, :], qkv[:, 2:4, :], 0.5, mx_sq[:, 2:4, :], ALU.mult, ALU.mult).then_inc(S("k_normed"), 1)
                    dve.wait_ge(S("k_normed"), 1)
                    dve.wait_ge(S("gelu_t"), 1)
                    link(V.scalar_tensor_tensor(tmpD, tmpD, 1.0, ly, ALU.add, ALU.mult))
                    V.scalar_tensor_tensor(griffin, tmpF, 0.5, tmpD, ALU.mult, ALU.mult).then_inc(S("griffin"), 1)
                    ahead("g0")
                    dve.wait_ge(S("side_act"), side.taken("eb"))
                    V.tensor_tensor(qdec, qkv[:, 0:2, :], egb, ALU.mult).then_inc(S("dve_q"), 1)
                    dve.wait_ge(S("side"), side.ready("ktr"))
                    dve.wait_ge(S("side_act"), side.taken("rowt"))

                    def cols(r, j):
                        return rowT[:, j, 32 * r:32 * r + 4].unsqueeze(2).to_broadcast([P, 4, DH])

                    def heads(ap):
                        return ap.rearrange("p (h d) -> p h d", h=4)

                    for j in range(2):
                        ps = side.bank("ktr")[:, j * 256:(j + 1) * 256]
                        V.tensor_tensor(heads(kbe[:, j, :]), heads(ps), cols(2, j), ALU.mult)
                        last = V.tensor_tensor(heads(kdec[:, j, :]), heads(ps), cols(3, j), ALU.mult)
                    last.then_inc(S("side_dve"), 1)
                    dve.wait_ge(S("side"), side.ready("vtr"))
                    for j in range(2):
                        ps = side.bank("vtr")[:, j * 256:(j + 1) * 256]
                        last = V.scalar_tensor_tensor(heads(vb[:, j, :]), heads(ps), 0.5, cols(1, j), ALU.mult, ALU.mult)
                    last.then_inc(S("side_dve"), 1)
                    def branch(n, src):
                        link(V.tensor_copy(brh[:, n], src))
                        V.tensor_tensor(brl[n], src, r32(brh[:, n]), ALU.subtract).then_inc(S(f"branch{n}"), 1)

                    ahead("g1")
                    dve.wait_ge(once["tables_load"], 16)
                    for hp in range(2):
                        ps = side.bank(f"gb{hp}")
                        dve.wait_ge(S("side"), side.ready(f"gb{hp}"))
                        for t in range(2):
                            for j in range(2):
                                o = (t * 2 + j) * P
                                h = 2 * t + hp
                                last = V.tensor_scalar(dec[:, hp, t, j, :], ps[:, o:o + P], rowT[:, j, h:h + 1], 0.0, ALU.subtract, ALU.min)
                        last.then_inc(S("side_dve"), 1)
                    tj = lambda m, hp: m[:, hp].rearrange("p t j c -> p (t j) c")
                    for hp in range(2):
                        dve.wait_ge(S("dec"), hp + 1)
                        link(V.tensor_tensor(tj(dec, hp), tj(dec, hp), over(cst_("incl"), 4), ALU.mult))
                        dve.wait_ge(S("side"), side.ready(f"kk{hp}"))
                        V.tensor_tensor(flat(low)[:, hp, :], side.bank(f"kk{hp}")[:], flat(dec)[:, hp, :], ALU.mult).then_inc(S("side_dve"), 1)
                        dve.wait_ge(S("side_dve"), side.taken(f"kk{hp}"))
                        dve.wait_ge(S("side"), side.ready(f"bb{hp}"))
                        V.tensor_tensor(flat(low)[:, hp, :], side.bank(f"bb{hp}")[:], flat(low)[:, hp, :], ALU.mult).then_inc(S("side_dve"), 1)
                    ahead("g2")
                    for hp in range(2):
                        dve.wait_ge(S("side"), side.ready(f"qk{hp}"))
                        V.tensor_tensor(flat(attn)[:, hp, :], side.bank(f"qk{hp}")[:], flat(dec)[:, hp, :], ALU.mult).then_inc(S("side_dve"), 1)

                    def s5_state(s):
                        ps = halves(side.bank(f"pq{s}")[:])
                        dve.wait_ge(S("side"), side.ready(f"pq{s}"))
                        if s:
                            dve.wait_ge(S("s5s"), s)
                        V.tensor_tensor(tmpA, ps, over(cosE[:, s, :], 2), ALU.mult)
                        V.tensor_tensor(tmpB, ps, over(sinE[:, s, :], 2), ALU.mult).then_inc(S("side_dve"), 1)
                        dve.wait_ge(S("side_dve"), side.taken(f"pq{s}"))
                        V.tensor_tensor(tmpA[:, 0, :], tmpA[:, 0, :], tmpB[:, 1, :], ALU.add)
                        link(V.tensor_tensor(tmpA[:, 1, :], tmpA[:, 1, :], tmpB[:, 0, :], ALU.subtract))
                        ss = (tmpC, tmpD)[s % 2]
                        if s >= 2:
                            dve.wait_ge(S("s5x"), s - 1)
                        mag = sm["mag"][:, s:s + 1].to_broadcast([P, SEQ])
                        V.tensor_tensor_scan(ss[:, 0, :], mag, tmpA[:, 0, :], 0.0, ALU.mult, ALU.add)
                        V.tensor_tensor_scan(ss[:, 1, :], mag, tmpA[:, 1, :], 0.0, ALU.mult, ALU.add).then_inc(S("s5s"), 1)

                    dve.wait_ge(S("tables"), 2)
                    ahead("g3")
                    for lv in range(LEVELS):
                        ahead(f"g{4 + lv}")
                        for hp in range(2):
                            for n in LEVEL_UNITS[lv]:
                                m = mx if n == "xt" else my
                                unit = f"{n}{hp}_{lv}"
                                dve.wait_ge(S("side"), side.ready(unit))
                                V.tensor_tensor(flat(m)[:, hp, :], flat(m)[:, hp, :], side.bank(unit)[:], ALU.subtract).then_inc(S("side_dve"), 1)
                        if lv < 4:
                            s5_state(2 * lv)
                            s5_state(2 * lv + 1)
                        if lv == 4:
                            dve.wait_ge(S("s5s"), NST)
                            for i, (unit, src) in enumerate((("rotq", rq), ("rotk", rk))):
                                dve.wait_ge(S("side"), side.ready(unit))
                                if i:
                                    dve.wait_ge(S("rotated"), i)
                                V.tensor_tensor(tmpA, halves(side.bank(unit)[:]), over(ropes, 2), ALU.mult).then_inc(S("side_dve"), 1)
                                link(V.tensor_tensor(src, src, over(ropec, 2), ALU.mult))
                                dve.wait_ge(S("side_dve"), side.taken(unit))
                                V.tensor_tensor(src, src, tmpA, ALU.add).then_inc(S("rotated"), 1)
                    dve.wait_ge(S("s5y"), 8)
                    for t in range(2):
                        last = V.scalar_tensor_tensor(su[:, t, :], su[:, t, :], par_("s5d", t, t + 1), ybank[:, t * SEQ:(t + 1) * SEQ], ALU.mult, ALU.add)
                    link(last)
                    link(V.tensor_tensor(tmpE, su, su, ALU.mult))
                    link(V.tensor_scalar(tmpE, tmpE, 0.044715, 1.0, ALU.mult, ALU.add))
                    V.tensor_tensor(tmpE, tmpE, su, ALU.mult).then_inc(S("s5gin"), 1)

                    def state_up(n):
                        ps = side.bank(f"su{n}")
                        dve.wait_ge(S("side"), side.ready(f"su{n}"))
                        for t in range(2):
                            for hp in range(2):
                                r, c = slice(64 * hp, 64 * hp + 64), slice(64 * hp, 64 * hp + 64)
                                pc = slice(t * P + 64 * hp, t * P + 64 * hp + 64)
                                if n == 0:
                                    if t == 0 and hp == 0:
                                        dve.wait_ge(S("state_zero"), 1)
                                    last = V.tensor_copy(state[r, t, c], ps[r, pc])
                                else:
                                    last = V.scalar_tensor_tensor(state[r, t, c], state[r, t, c], egb[r, t, 64 * n + 63:64 * n + 64], ps[r, pc],
                                                                  ALU.mult, ALU.add)
                        last.then_inc(S("side_dve"), 1)

                    def values(n):
                        r, j = slice(64 * (n % 2), 64 * (n % 2) + 64), n // 2
                        dve.wait_ge(S("side"), side.ready(f"ws{n}"))
                        V.tensor_tensor(uu[r, j, :], uu[r, j, :], side.bank(f"ws{n}")[r, 0:256], ALU.subtract).then_inc(S("side_dve"), 1)

                    def masked(h):
                        dve.wait_ge(S("side"), side.ready(f"sc{h}"))
                        mask = cst_("rmask", SEQ * h, SEQ * (h + 1))
                        V.tensor_tensor(scm[:, h, 0:SEQ], side.bank(f"sc{h}")[:, 0:SEQ], mask, ALU.mult)
                        V.tensor_tensor(scm[:, h, SEQ:384], side.bank(f"sc{h}")[:, SEQ:384], mask[:, 0:P], ALU.mult).then_inc(S("side_dve"), 1)

                    ahead("g10")
                    ahead("g11")
                    state_up(0)
                    masked(0)
                    masked(1)
                    values(1)
                    state_up(1)
                    masked(2)
                    masked(3)
                    dve.wait_ge(S("s5gt"), 1)
                    V.scalar_tensor_tensor(tmpE, tmpE, 1.0, su, ALU.add, ALU.mult).then_inc(S("s5g"), 1)
                    ahead("g12")
                    values(2)
                    state_up(2)
                    dve.wait_ge(S("rgt"), 1)
                    link(V.scalar_tensor_tensor(rg, tmpA, 1.0, rg, ALU.add, ALU.mult))
                    values(3)
                    dve.wait_ge(S("side_act"), side.taken("ro"))
                    dve.wait_ge(S("side"), side.ready("rm"))
                    V.tensor_tensor(tmpB, tmpB, halves(side.bank("rm")[:]), ALU.subtract).then_inc(S("side_dve"), 1)
                    dve.wait_ge(S("side_act"), side.taken("oi3"))
                    for j in range(2):
                        dve.wait_ge(S("side"), side.ready(f"oa{j}"))
                        ps = halves(side.bank(f"oa{j}")[:, 0:256])
                        if j == 0:
                            V.tensor_copy(go[:, :, 0:64], ps[:, :, 0:64])
                            V.tensor_tensor(go[:, :, 64:P], go[:, :, 64:P], ps[:, :, 64:P], ALU.add).then_inc(S("side_dve"), 1)
                        else:
                            V.tensor_tensor(go[:, :, P:SEQ], go[:, :, P:SEQ], ps, ALU.add).then_inc(S("side_dve"), 1)
                    ahead("g13")
                    dve.wait_ge(S("side_act"), side.taken("glu"))
                    dve.wait_ge(S("s5g"), 1)
                    link(V.scalar_tensor_tensor(tmpF, tmpF, 1.0, tmpE, ALU.add, ALU.mult))
                    V.tensor_scalar(tmpF, tmpF, 0.25, None, ALU.mult).then_inc(S("s5_done"), 1)
                    dve.wait_ge(S("side_act"), side.taken("gs"))
                    link(V.reciprocal(tmpD, tmpD))
                    link(V.tensor_tensor(go, go, tmpD, ALU.mult))
                    link(V.scalar_tensor_tensor(go, go, gnh, zz, ALU.mult, ALU.mult))
                    branch(0, go)
                    ahead("g14")
                    dve.wait_ge(S("side_act"), side.taken("rv2"))
                    link(V.reciprocal(tmpC, tmpC))
                    link(V.tensor_tensor(tmpB, tmpB, tmpC, ALU.mult))
                    for t in range(2):
                        last = V.scalar_tensor_tensor(tmpB[:, t, :], tmpB[:, t, :], rnh[:, t:t + 1], rg[:, t, :], ALU.mult, ALU.mult)
                    link(last)
                    branch(3, tmpB)
                    ahead("g15")
                    gbr = gates.rearrange("p (n m) t -> p n m t", n=NB)
                    dve.wait_ge(S("main_act"), main.taken("g15"))

                    def merge_sum(m):
                        a, b = ((tmpA, tmpB), (tmpC, tmpD))[m % 2]
                        dve.wait_ge(S("main_dve"), main.taken(f"mg{m}b"))
                        link(V.tensor_tensor(a, a, b, ALU.add))
                        V.tensor_tensor(ret[:, m, :], a[:, 0, :], a[:, 1, :], ALU.add).then_inc(S("summed"), 1)

                    def low_merged(m):
                        dve.wait_ge(S("sum_high"), m + 1)
                        V.tensor_tensor(xl[:, m, :], ret[:, m, :], r32(xh[:, m, :]), ALU.subtract).then_inc(S("merged"), 1)

                    for m in range(KD):
                        ahead(f"mg{m}")
                        pair_ab = ((tmpA, tmpB), (tmpC, tmpD))[m % 2]
                        if m >= 2:
                            dve.wait_ge(S("summed"), m - 1)
                        for ab, t in enumerate(pair_ab):
                            unit = f"mg{m}{'ab'[ab]}"
                            dve.wait_ge(S("main"), main.ready(unit))
                            V.scalar_tensor_tensor(t, gbr[:, 2 * ab:2 * ab + 2, m, :], 1.0, halves(main.bank(unit)[:]), ALU.add, ALU.mult).then_inc(S("main_dve"), 1)
                        if m >= 2:
                            low_merged(m - 2)
                        if m:
                            merge_sum(m - 1)
                    low_merged(KD - 2)
                    merge_sum(KD - 1)
                    low_merged(KD - 1)
                    down("wo", 0.5)
                    inverted(1)
                    normed("2", 2, "n2")
                    up(2, range(MF))
                    down("dn2_", 0.5)
                    inverted(2)

            handles = [per_layer[n].num for n in per_layer]
            assert sorted(handles) == list(range(min(handles), max(handles) + 1))
            nc.all_engine_barrier(sems_to_clear=range(min(handles), max(handles) + 1))

        with nc.Block() as block:
            @block.tensor
            def _(pe):
                for j in range(2):
                    last = nc.tensor.matmul(psum[2][:, j * P:(j + 1) * P], inv_rms[:, j:j + 1].to_broadcast([P, P]), ident, start=True, stop=True)
                last.then_inc(once["fin_pe"], 1)

            @block.vector
            def _(dve):
                dve.wait_ge(once["fin_pe"], 1)
                for k in range(KD):
                    nc.vector.scalar_tensor_tensor(ret[:, k, :], x[:, k, :], cst_("fnorm", k, k + 1), psum[2][:, 0:SEQ], ALU.mult, ALU.mult).then_inc(once["fin_dve"], 1)

            @block.sync
            def _(sp):
                for j in range(4):
                    sp.wait_ge(once["fin_dve"], 2 * (j + 1))
                    sp.dma_start(y_out[:, 2 * j:2 * j + 2, :], ret[:, 2 * j:2 * j + 2, :]).then_inc(once["stored"], 16)
                sp.wait_ge(once["stored"], 64)


def _weight_pieces(a, l):
    def tiles(w):
        k, m = w.shape
        return w.reshape(k // P, P, m // P, P).transpose(1, 2, 0, 3)

    out = {}

    def pair(name, w):
        for o in range(w.shape[1]):
            out[f"{name}.{o}"] = w[:, o]

    for f in (1, 2):
        g, u, d = (tiles(a[f"ffn{f}_{n}"][l]) for n in ("w_gate", "w_up", "w_down"))
        for m in range(MF):
            pair(f"gu{f}_{m}", np.stack([g[:, m], u[:, m]], axis=1))
        for j in range(4):
            for o in range(2):
                for n, (k0, k1) in enumerate(DOWN_K):
                    out[f"dn{f}_{j}.{3 * o + n}"] = d[:, 2 * j + o, k0:k1]
    w = a["w_in"][l]
    offs = np.cumsum([0, 768, 256, 4, 4, 256, 256, 256, 256, 256, 256, 256, 4096])
    col = {n: w[:, offs[i]:offs[i + 1]] for i, n in enumerate(["qkv", "z", "b", "a", "su", "lx", "ly", "rq", "rk", "rv", "rg", "g"])}
    ba = np.zeros((DM, P), np.float32)
    for r in (0, 64, 96):
        ba[:, r:r + 4] = col["a"]
    ba[:, 32:36] = col["b"]
    pair("ba", tiles(ba))
    for i in range(3):
        pair(f"qkv{i}", tiles(col["qkv"][:, 256 * i:256 * i + 256]))
    for n in ("z", "su", "lx", "ly", "rq", "rk", "rg"):
        pair(n, tiles(col[n]))
    rv = tiles(col["rv"]).transpose(0, 2, 1, 3)
    for o in range(2):
        out[f"rv.{o}"] = rv[:, 4 * o:4 * o + 4]
    for i in range(16):
        pair(f"g{i}", tiles(col["g"][:, 256 * i:256 * i + 256]))
    wb = a["w_branch"][l].reshape(NB, 2, P, KD, P).transpose(2, 3, 0, 1, 4).reshape(P, KD, NB * 2, P)
    wo = tiles(a["w_out"][l])
    for m in range(KD):
        out[f"mg{m}.0"] = wb[:, m]
    for i in range(4):
        pair(f"wo{i}", wo[:, 2 * i:2 * i + 2])
    return out


def _weight_stream(a, l):
    this, after = _weight_pieces(a, l), _weight_pieces(a, (l + 1) % DEPTH)
    out = [(this if i < len(PIECES) - RAW_SLOTS else after)[n] for i, (n, _, _) in enumerate(STREAM)]
    return np.concatenate([np.ascontiguousarray(w).reshape(-1) for w in out])


def _params(a, l):
    p = np.zeros((P, NPAR), np.float32)

    def put(name, v):
        lo, hi = PCOLS[name]
        p[:, lo:hi] = v.reshape(P, hi - lo)

    feat = lambda v: v.reshape(-1, P).T
    put("n1", feat(a["ffn1_norm"][l]))
    put("nm", feat(a["mix_norm"][l]))
    put("n2", feat(a["ffn2_norm"][l]))
    put("gconv", feat(a["gdn_conv_w"][l]))
    for name, v in (("dtb", a["gdn_dt_bias"][l]), ("alog", a["gdn_a_log"][l])):
        for r in (0, 64, 96):
            p[r:r + 4, PCOLS[name][0]] = v
    put("gnorm", np.concatenate([a["gdn_norm_w"][l]] * 2))
    put("lre", feat(a["s5_lambda_re"][l]))
    put("lim", feat(a["s5_lambda_im"][l]))
    put("ldt", feat(np.repeat(a["s5_log_dt"][l], 64)))
    put("s5d", feat(a["s5_d"][l]))
    put("bglu", feat(a["s5_b_glu"][l]))
    put("lconv", feat(a["lru_conv_w"][l]))
    put("lcb", feat(a["lru_conv_b"][l]))
    put("lba", feat(a["lru_b_a"][l]))
    put("lbi", feat(a["lru_b_i"][l]))
    put("lam", feat(a["lru_lambda"][l]))
    put("rnorm", feat(a["ret_norm_w"][l]))
    for name, b in (("sbr", a["s5_b_re"][l]), ("sbi", a["s5_b_im"][l])):
        w = np.zeros((P, 2, P), np.float32)
        for g in range(16):
            w[16 * (g % 8):16 * (g % 8) + 16, g // 8, 64 * (g % 2):64 * (g % 2) + 64] = b[g].T
        put(name, w)
    for name, c in (("scr", a["s5_c_re"][l]), ("sci", a["s5_c_im"][l])):
        w = np.zeros((P, NST, 32), np.float32)
        for g in range(16):
            w[64 * (g % 2):64 * (g % 2) + 64, g // 2, 16 * (g % 2):16 * (g % 2) + 16] = c[g].T
        put(name, w)
    put("wglu", a["s5_w_glu"][l].reshape(2, P, 256).transpose(1, 0, 2))
    for name, b in (("wa", a["lru_w_a"][l]), ("wi", a["lru_w_i"][l])):
        w = np.zeros((P, 2, P), np.float32)
        for n in range(4):
            r = 64 * (n % 2)
            w[r:r + 64, n // 2, r:r + 64] = b[n]
        put(name, w)
    return p


def _constants(fnorm):
    c = np.zeros((P, NCST), np.float32)

    def put(name, v):
        lo, hi = CCOLS[name]
        c[:, lo:hi] = np.asarray(v, np.float64).reshape(P, hi - lo)

    i = np.arange(P)
    put("ident", np.eye(P))
    put("one", np.ones(P))
    put("bo", (i[:, None] // 64 == i[None] // 64) / 64.0)
    put("incl", (i[:, None] // 64 == i[None] // 64) & (i[:, None] <= i[None]))
    lev = []
    for s in (1, 2, 4, 8, 16, 32):
        m, cc = i[:, None], i[None]
        lev.append((m // (2 * s) == cc // (2 * s)) & (m % (2 * s) < s) & (cc % (2 * s) >= s))
    put("lev", np.stack(lev, axis=1))
    perm = np.zeros((P, P))
    for r in range(P):
        if r % 64 < 32:
            perm[r + 32, r] = -1.0
        else:
            perm[r - 32, r] = 1.0
    put("perm", perm)
    rmask = np.zeros((P, 4, SEQ))
    for h in range(4):
        lg = np.log1p(-np.exp2(-5.0 - h))
        m, q = i[:, None], np.arange(SEQ)[None]
        rmask[:, h] = np.where(q >= m, np.exp(np.maximum(q - m, 0) * lg), 0.0) * DH ** -0.5
    put("rmask", rmask)
    put("freq", (10000.0 ** (-(i % 32) / 32.0)))
    lo, hi = CCOLS["fnorm"]
    c[:, lo:hi] = fnorm.reshape(KD, P).T
    return c


def kernel(**inputs):
    import concourse.bacc as _bacc
    from concourse import mybir as _mybir
    from concourse.bass_utils import run_bass_kernel_spmd as _run

    a = {k: np.asarray(v) for k, v in inputs.items()}
    arrays = {
        "weights": np.stack([_weight_stream(a, l) for l in range(DEPTH)]),
        "params": np.stack([_params(a, (l + 1) % DEPTH) for l in range(DEPTH)]),
        "consts": _constants(a["final_norm"]),
        "positions": np.ascontiguousarray(np.broadcast_to(a["positions"].reshape(1, SEQ), (P, SEQ))),
        "x_in": np.ascontiguousarray(a["x"].reshape(SEQ, KD, P).transpose(2, 1, 0)),
    }
    nc = _bacc.Bacc("TRN2", target_bir_lowering=False, num_devices=1)
    args = [nc.dram_tensor(n, v.shape, _mybir.dt.from_np(v.dtype), kind="ExternalInput").ap() for n, v in arrays.items()]
    args.append(nc.dram_tensor("y_out", (P, KD, SEQ), F32, kind="ExternalOutput").ap())
    trunk(nc, *args)
    r = _run(nc, [arrays], core_ids=[0])
    return r.results[0]["y_out"].transpose(2, 1, 0).reshape(1, SEQ, DM)
```
